# Optimizing a Trainium2 kernel written in Bass

```python
import math
import jax, jax.numpy as jnp
from jax import lax
import numpy as np

D_MODEL = 1024
BATCH = 1
SEQ = 512
DEPTH = 1
DEC_BATCH = 1
DEC_SEQ = 64
PAST_LEN = 256

CHUNK = 64
EPS = 1e-6
DA_HEADS = 8
DA_HEAD_DIM = 64
DA_V_DIM = 2 * DA_HEAD_DIM
ROPE_THETA = 10000.0
Q_BLOCK = 128
GLA_HEADS = 4
GLA_DK = D_MODEL // 2 // GLA_HEADS
GLA_DV = D_MODEL // GLA_HEADS
GLA_GATE_RANK = 16
GLA_GATE_TAU = 16.0
PEER_HEADS = 8
PEER_N_KEYS = 128
PEER_N_EXPERTS = PEER_N_KEYS * PEER_N_KEYS
PEER_QDIM = 256
PEER_TOPK = 16
PEER_TOKEN_BLOCK = 128

DA_QK_W = DA_HEADS * 2 * DA_HEAD_DIM
DA_V_W = DA_HEADS * DA_V_DIM
GLA_QK_W = GLA_HEADS * GLA_DK
GLA_V_W = GLA_HEADS * GLA_DV
IN_SPLITS = (DA_QK_W, DA_QK_W, DA_V_W, GLA_QK_W, GLA_QK_W, GLA_V_W, GLA_GATE_RANK, GLA_V_W, D_MODEL, D_MODEL)
IN_WIDTH = 2 * DA_QK_W + DA_V_W + 2 * GLA_QK_W + 2 * GLA_V_W + GLA_GATE_RANK + 2 * D_MODEL

kernel_name = "diffattn_gla_peer_streaming_step"

def _rms(x, gain):
    xf = x.astype(jnp.float32)
    y = xf * lax.rsqrt(jnp.mean(xf * xf, axis=-1, keepdims=True) + EPS)
    return (y * gain.astype(jnp.float32)).astype(x.dtype)

def _split_cols(t):
    outs, start = [], 0
    for w in IN_SPLITS:
        outs.append(t[..., start:start + w])
        start += w
    return outs

def _rope(x, pos):
    half = DA_HEAD_DIM // 2
    inv_freq = ROPE_THETA ** (-jnp.arange(half, dtype=jnp.float32) / half)
    ang = pos.astype(jnp.float32)[:, None] * inv_freq[None, :]
    cos = jnp.cos(ang)[:, None, None, :]
    sin = jnp.sin(ang)[:, None, None, :]
    xf = x.astype(jnp.float32)
    x1, x2 = xf[..., :half], xf[..., half:]
    return jnp.concatenate([x1 * cos - x2 * sin, x2 * cos + x1 * sin], axis=-1).astype(x.dtype)

def _diff_attn(q, k, v, q_pos, k_pos, lam):
    s = jnp.einsum('bqhmd,bkhmd->bhmqk', q, k).astype(jnp.float32) * (DA_HEAD_DIM ** -0.5)
    allowed = (k_pos[None, :] // CHUNK) <= (q_pos[:, None] // CHUNK)
    s = jnp.where(allowed, s, -jnp.inf)
    p = jax.nn.softmax(s, axis=-1)
    w = p[:, :, 0] - lam * p[:, :, 1]
    return jnp.einsum('bhqk,bkhd->bqhd', w.astype(v.dtype), v)

def _diff_attn_prompt(q, k, v, lam):
    B, L = q.shape[0], q.shape[1]
    nb = L // Q_BLOCK
    qb = q.reshape(B, nb, Q_BLOCK, DA_HEADS, 2, DA_HEAD_DIM).swapaxes(0, 1)
    pos = jnp.arange(L)
    qpos = pos.reshape(nb, Q_BLOCK)
    out = lax.map(lambda a: _diff_attn(a[0], k, v, a[1], pos, lam), (qb, qpos))
    return out.swapaxes(0, 1).reshape(B, L, DA_HEADS, DA_V_DIM)

def _gla(q, k, v, log_a, s0):
    B, L = q.shape[0], q.shape[1]
    c = CHUNK if L % CHUNK == 0 else L
    n = L // c

    def to_chunks(t):
        t = t.astype(jnp.float32)
        return t.reshape(B, n, c, t.shape[2], t.shape[3]).transpose(1, 0, 3, 2, 4)

    qc = to_chunks(q * (GLA_DK ** -0.5))
    kc, vc, ac = to_chunks(k), to_chunks(v), to_chunks(log_a)
    causal = jnp.tril(jnp.ones((c, c), dtype=bool))[:, :, None]

    def step(S, inp):
        qi, ki, vi, ai = inp
        b = jnp.cumsum(ai, axis=2)
        diff = b[:, :, :, None, :] - b[:, :, None, :, :]
        decay = jnp.exp(jnp.where(causal, diff, -jnp.inf))
        A = jnp.einsum('bhid,bhjd,bhijd->bhij', qi, ki, decay)
        o = jnp.einsum('bhid,bhdv->bhiv', qi * jnp.exp(b), S) + jnp.einsum('bhij,bhjv->bhiv', A, vi)
        b_last = b[:, :, -1:, :]
        S = S * jnp.exp(b_last)[:, :, 0, :, None] + jnp.einsum('bhjd,bhjv->bhdv', ki * jnp.exp(b_last - b), vi)
        return S, o

    S, o = lax.scan(step, s0.astype(jnp.float32), (qc, kc, vc, ac))
    o = o.transpose(1, 0, 3, 2, 4).reshape(B, L, GLA_HEADS, GLA_DV)
    return o.astype(q.dtype), S.astype(q.dtype)

def _peer(x, w_q, sub_keys, expert_u, expert_v):
    B, L, D = x.shape
    T = B * L
    nb = -(-T // PEER_TOKEN_BLOCK)
    xt = jnp.pad(x.reshape(T, D), ((0, nb * PEER_TOKEN_BLOCK - T), (0, 0))).reshape(nb, PEER_TOKEN_BLOCK, D)

    def block(xb):
        q = (xb @ w_q).reshape(PEER_TOKEN_BLOCK, PEER_HEADS, 2, PEER_QDIM // 2)
        s = jnp.einsum('thpd,hpnd->thpn', q, sub_keys).astype(jnp.float32)
        sv, si = lax.top_k(s, PEER_TOPK)
        cand = sv[..., 0, :, None] + sv[..., 1, None, :]
        cidx = si[..., 0, :, None] * PEER_N_KEYS + si[..., 1, None, :]
        top_s, top_pos = lax.top_k(cand.reshape(PEER_TOKEN_BLOCK, PEER_HEADS, PEER_TOPK * PEER_TOPK), PEER_TOPK)
        idx = jnp.take_along_axis(cidx.reshape(PEER_TOKEN_BLOCK, PEER_HEADS, PEER_TOPK * PEER_TOPK), top_pos, axis=-1)
        g = jax.nn.softmax(top_s, axis=-1)
        act = jax.nn.gelu(jnp.einsum('thkd,td->thk', expert_u[idx], xb).astype(jnp.float32), approximate=False)
        return jnp.einsum('thk,thkd->td', (g * act).astype(xb.dtype), expert_v[idx])

    y = lax.map(block, xt).reshape(nb * PEER_TOKEN_BLOCK, D)[:T]
    return y.reshape(B, L, D)

def _layer(x, cache_k, cache_v, s0, p, lam_init):
    B, L, _ = x.shape
    past = 0 if cache_k is None else cache_k.shape[1]
    xn = _rms(x, p['norm1_g'])
    dq, dk, dv, gq, gk, gv, glr, gr, ga, gb = _split_cols(xn @ p['w_in'])
    pos = past + jnp.arange(L)

    lq = p['da_lambda'].astype(jnp.float32)
    lam = jnp.exp(jnp.sum(lq[0] * lq[1])) - jnp.exp(jnp.sum(lq[2] * lq[3])) + lam_init
    q = _rope(_rms(dq.reshape(B, L, DA_HEADS, 2, DA_HEAD_DIM), p['qk_norm_g'][0]), pos)
    k = _rope(_rms(dk.reshape(B, L, DA_HEADS, 2, DA_HEAD_DIM), p['qk_norm_g'][1]), pos)
    v = dv.reshape(B, L, DA_HEADS, DA_V_DIM)
    if cache_k is None:
        o_a = _diff_attn_prompt(q, k, v, lam)
    else:
        kk = jnp.concatenate([cache_k.astype(k.dtype), k], axis=1)
        vv = jnp.concatenate([cache_v.astype(v.dtype), v], axis=1)
        o_a = _diff_attn(q, kk, vv, pos, jnp.arange(past + L), lam)
    o_a = (_rms(o_a, p['da_subln_g']) * (1.0 - lam_init)).reshape(B, L, DA_V_W)

    log_a = jax.nn.log_sigmoid((glr @ p['gla_w_gate2'] + p['gla_b_gate']).astype(jnp.float32)) / GLA_GATE_TAU
    if s0 is None:
        s0 = jnp.zeros((B, GLA_HEADS, GLA_DK, GLA_DV), jnp.float32)
    o_b, s_new = _gla(gq.reshape(B, L, GLA_HEADS, GLA_DK), gk.reshape(B, L, GLA_HEADS, GLA_DK),
                      gv.reshape(B, L, GLA_HEADS, GLA_DV), log_a.reshape(B, L, GLA_HEADS, GLA_DK), s0)
    o_b = _rms(o_b, p['gla_norm_g']).reshape(B, L, GLA_V_W) * jax.nn.silu(gr)

    mix = jax.nn.sigmoid(ga) * (o_a @ p['w_branch_a']) + jax.nn.sigmoid(gb) * (o_b @ p['w_branch_b'])
    h = x + mix @ p['w_out']
    y = h + _peer(_rms(h, p['norm2_g']), p['peer_w_q'], p['peer_sub_keys'], p['peer_u'], p['peer_v'])
    return y, k, v, s_new

def setup_inputs(seed: int = 0) -> dict:
    key = jax.random.key(seed)
    ks = jax.random.split(key, 24)
    f32 = jnp.float32

    def nrm(k, shape, scale):
        return jax.random.normal(k, shape, f32) * scale

    return {
        'x_prompt': nrm(ks[0], (BATCH, SEQ, D_MODEL), 1.0),
        'x_sample': nrm(ks[1], (DEC_BATCH, DEC_SEQ, D_MODEL), 1.0),
        'cache_k': nrm(ks[2], (DEPTH, DEC_BATCH, PAST_LEN, DA_HEADS, 2, DA_HEAD_DIM), 1.0),
        'cache_v': nrm(ks[3], (DEPTH, DEC_BATCH, PAST_LEN, DA_HEADS, DA_V_DIM), 1.0),
        'state_gla': nrm(ks[4], (DEPTH, DEC_BATCH, GLA_HEADS, GLA_DK, GLA_DV), 0.5),
        'norm1_g': 1.0 + nrm(ks[5], (DEPTH, D_MODEL), 0.02),
        'w_in': nrm(ks[6], (DEPTH, D_MODEL, IN_WIDTH), D_MODEL ** -0.5),
        'qk_norm_g': 1.0 + nrm(ks[7], (DEPTH, 2, DA_HEAD_DIM), 0.02),
        'da_lambda': nrm(ks[8], (DEPTH, 4, DA_HEAD_DIM), 0.1),
        'da_subln_g': 1.0 + nrm(ks[9], (DEPTH, DA_V_DIM), 0.02),
        'gla_w_gate2': nrm(ks[10], (DEPTH, GLA_GATE_RANK, GLA_QK_W), GLA_GATE_RANK ** -0.5),
        'gla_b_gate': nrm(ks[11], (DEPTH, GLA_QK_W), 0.1),
        'gla_norm_g': 1.0 + nrm(ks[12], (DEPTH, GLA_DV), 0.02),
        'w_branch_a': nrm(ks[13], (DEPTH, DA_V_W, D_MODEL), DA_V_W ** -0.5),
        'w_branch_b': nrm(ks[14], (DEPTH, GLA_V_W, D_MODEL), GLA_V_W ** -0.5),
        'w_out': nrm(ks[15], (DEPTH, D_MODEL, D_MODEL), D_MODEL ** -0.5),
        'norm2_g': 1.0 + nrm(ks[16], (DEPTH, D_MODEL), 0.02),
        'peer_w_q': nrm(ks[17], (DEPTH, D_MODEL, PEER_HEADS * PEER_QDIM), D_MODEL ** -0.5),
        'peer_sub_keys': nrm(ks[18], (DEPTH, PEER_HEADS, 2, PEER_N_KEYS, PEER_QDIM // 2), (PEER_QDIM // 2) ** -0.5),
        'peer_u': nrm(ks[19], (DEPTH, PEER_N_EXPERTS, D_MODEL), D_MODEL ** -0.5),
        'peer_v': nrm(ks[20], (DEPTH, PEER_N_EXPERTS, D_MODEL), PEER_HEADS ** -0.5),
    }

def reference(x_prompt, x_sample, cache_k, cache_v, state_gla, norm1_g, w_in, qk_norm_g, da_lambda,
              da_subln_g, gla_w_gate2, gla_b_gate, gla_norm_g, w_branch_a, w_branch_b, w_out, norm2_g,
              peer_w_q, peer_sub_keys, peer_u, peer_v):
    yp, ys = x_prompt, x_sample
    kp_l, vp_l, sp_l, ks_l, vs_l, ss_l = [], [], [], [], [], []
    for l in range(DEPTH):
        p = {
            'norm1_g': norm1_g[l], 'w_in': w_in[l], 'qk_norm_g': qk_norm_g[l], 'da_lambda': da_lambda[l],
            'da_subln_g': da_subln_g[l], 'gla_w_gate2': gla_w_gate2[l], 'gla_b_gate': gla_b_gate[l],
            'gla_norm_g': gla_norm_g[l], 'w_branch_a': w_branch_a[l], 'w_branch_b': w_branch_b[l],
            'w_out': w_out[l], 'norm2_g': norm2_g[l], 'peer_w_q': peer_w_q[l],
            'peer_sub_keys': peer_sub_keys[l], 'peer_u': peer_u[l], 'peer_v': peer_v[l],
        }
        lam_init = 0.8 - 0.6 * math.exp(-0.3 * l)
        yp, kp, vp, sp = _layer(yp, None, None, None, p, lam_init)
        ys, kn, vn, sn = _layer(ys, cache_k[l], cache_v[l], state_gla[l], p, lam_init)
        kp_l.append(kp); vp_l.append(vp); sp_l.append(sp)
        ks_l.append(kn); vs_l.append(vn); ss_l.append(sn)
    return (yp, ys, jnp.stack(kp_l), jnp.stack(vp_l), jnp.stack(sp_l), jnp.stack(ks_l), jnp.stack(vs_l), jnp.stack(ss_l))


_drawn_inputs = setup_inputs


def setup_inputs(seed=0):
    import zlib

    import numpy as np

    out = dict(_drawn_inputs(seed))
    spreads = {}
    factors = {'da_subln_g': 27.721, 'gla_norm_g': 44.689, 'norm2_g': 15.639}
    for name, (base, spread) in spreads.items():
        noise = np.random.default_rng([zlib.crc32(name.encode()), seed]).standard_normal(out[name].shape)
        drawn = base * np.exp(spread * noise) if base else spread * noise
        out[name] = __import__('jax').numpy.asarray(drawn.astype(out[name].dtype))
    for name, factor in factors.items():
        out[name] = (out[name] * factor).astype(out[name].dtype)
    return out
```

```python
from contextlib import ExitStack

import numpy as np

import concourse.bass as bass
from concourse import mybir

F32 = mybir.dt.float32
F32R = mybir.dt.float32r
U32 = mybir.dt.uint32
ALU = mybir.AluOpType
ACT = mybir.ActivationFunctionType
AX = mybir.AxisListType

P = 128
D = 1024
KT = D // P
SEQ = 512
DEC = 64
PAST = 256
TOK = SEQ + DEC
HALF = TOK // 2
NC_T = 5
NH = 8
HD = 64
GH = 4
EPS = 1e-6
NEG = -1e30
RANK = 16
LEVELS = [64, 32, 16, 8, 4, 2, 1]
CHUNK_TOK = 64
N_KEYS = 128
TOPK = 16
PH = 8
LAM_INIT = 0.2

T_Q, T_K, T_V, T_GQ, T_GK, T_GV, T_GR = 0, 8, 16, 24, 28, 32, 40
T_GA, T_GB, T_WA, T_WB, T_WO, T_PQ, T_END = 48, 56, 64, 72, 80, 88, 104

C_ID, C_BLK, C_ROT, C_IOTA, C_COS, C_SIN, C_RST, C_MSK = 0, 128, 256, 384, 512, 1088, 1664, 2240
N_MASK = len(LEVELS) + 1
C_END = C_MSK + N_MASK * P
G_N1, G_N2, G_QK, G_SUB, G_GLA, G_BG, G_LAM, G_END = 0, 8, 16, 32, 33, 35, 39, 43


def token_cols(c):
    return c * P, (P if c < 4 else DEC)


def bcast(ap, axis, n):
    ap = ap.unsqueeze(axis)
    shape = list(ap.shape)
    shape[axis] = n
    return ap.to_broadcast(shape)


def apart(eng, S):
    eng.sem_inc(S["passed"], 1)


def load_w(sp, S, i, c):
    t = 2 * i + c
    if not (isinstance(t, int) and t < 2):
        sp.wait_ge(S["w_split"], t - 1)
    sp.dma_start(S["w_raw"][:, c % 2, :], S["w_all"][:, bass.ds(t, 1), :]).then_inc(S["w_loaded"][c % 2], 16)


def split_hi(nc, act, S, i, c):
    u, t = c % 2, 2 * i + c
    act.wait_ge(S["w_loaded"][u], 16 * (i + c // 2 + 1))
    if not (isinstance(t, int) and t < 2):
        act.wait_ge(S["tile_done"], t - 1)
    nc.scalar.activation(S["w_hi"][:, u, :], S["w_raw"][:, u, :], ACT.Copy).then_inc(S["w_hi_done"], 1)


def split_lo(nc, dve, S, i, c):
    u, t = c % 2, 2 * i + c
    dve.wait_ge(S["w_hi_done"], t + 1)
    nc.vector.tensor_tensor(S["w_lo"][:, u, :], S["w_raw"][:, u, :], S["w_hi"][:, u, :].bitcast(F32),
                            ALU.subtract).then_inc(S["w_split"], 1)


def product3(nc, out, wh, wl, xh, xl, first, last):
    nc.tensor.matmul(out, wh, xh, start=first, stop=False)
    nc.tensor.matmul(out, wh, xl, start=False, stop=False)
    return nc.tensor.matmul(out, wl, xh, start=False, stop=last)


def dense_tile(nc, pe, S, i, c):
    u, t = c % 2, 2 * i + c
    pe.wait_ge(S["w_split"], t + 1)
    if not (isinstance(t, int) and t < 2):
        pe.wait_ge(S["evacuated"], t - 1)
    for f in range(2):
        cols = slice(f * HALF, (f + 1) * HALF)
        for k in range(KT):
            w = slice(k * P, (k + 1) * P)
            ins = product3(nc, S["mm"][u][:, f, 0:HALF], S["w_hi"][:, u, w], S["w_lo"][:, u, w],
                           S["x_hi"][:, k, cols], S["x_lo"][:, k, cols], k == 0, k == KT - 1)
    ins.then_inc(S["tile_done"], 1)


def halves(ap):
    return ap.rearrange("p (f n) -> p f n", f=2)


def feat(S, j):
    return S["big"][:, bass.ds(j * TOK, TOK)]


def split_activation_hi(nc, act, S, src, ready, count):
    act.wait_ge(ready, count)
    nc.scalar.activation(S["x_hi"][:, :, :], src, ACT.Copy).then_inc(S["x_hi_done"], 1)


def split_activation_lo(nc, dve, S, src, count):
    dve.wait_ge(S["x_hi_done"], count)
    nc.vector.tensor_tensor(S["x_lo"][:, :, :], src, S["x_hi"][:, :, :].bitcast(F32),
                            ALU.subtract).then_inc(S["x_split"], 1)


def matmul_tok(nc, out, lhsT, rhs, first, last):
    nc.tensor.matmul(out[:, 0, 0:HALF], lhsT, rhs[:, 0:HALF], start=first, stop=last)
    return nc.tensor.matmul(out[:, 1, 0:HALF], lhsT, rhs[:, HALF:TOK], start=first, stop=last)


def as3(ap):
    return ap.rearrange("p (k n) -> p k n", n=TOK)


def rms_squares(nc, act, S, ready, count):
    act.wait_ge(ready, count)
    nc.scalar.activation(S["big"][:, 0:KT * TOK], S["res"][:, :], ACT.Square).then_inc(S["n_sq"], 1)


def rms_sum(nc, pe, S, r):
    pe.wait_ge(S["n_sq"], r + 1)
    for k in range(KT):
        ins = matmul_tok(nc, S["aux"], S["ones"][:, :], S["big"][:, k * TOK:(k + 1) * TOK], k == 0, k == KT - 1)
    ins.then_inc(S["n_sum"], 1)


def rms_root(nc, act, S, r):
    act.wait_ge(S["n_sum"], r + 1)
    nc.scalar.activation(halves(S["root"][:, :]), S["aux"][:, :, 0:HALF], ACT.Sqrt, bias=S["eps"][:, 0:1],
                         scale=1.0 / D).then_inc(S["n_root"], 1)


def rms_apply(nc, dve, S, r, gain):
    dve.wait_ge(S["n_root"], r + 1)
    nc.vector.reciprocal(S["rinv"][:, :], S["root"][:, :]).then_inc(S["n_rinv"], 1)
    dve.wait_ge(S["n_rinv"], r + 1)
    for k in range(KT):
        ins = nc.vector.scalar_tensor_tensor(
            out=S["big"][:, (8 + k) * TOK:(9 + k) * TOK], in0=S["res"][:, k * TOK:(k + 1) * TOK],
            scalar=S["gains"][:, gain + k:gain + k + 1], in1=S["rinv"][:, :], op0=ALU.mult, op1=ALU.mult)
    ins.then_inc(S["n_done"], 1)


FROM_ONE = {
    "tensor": "a_turned a_pv g_at g_kT g_o g_osum t_turned",
    "scalar": "a_exp a_wT g_root o_root t_tab",
    "vector": "a_w g_fin g_gated g_oc o_done o_evac q_roped q_rsin r_top t_ij y_add",
    "gpsimd": "r_kept",
    "sync": "g_out",
}


def start_at_one(eng, S, engine):
    for name in FROM_ONE[engine].split():
        eng.sem_inc(S[name], 1)


def stage_norm1(nc, S, A):
    with nc.Block() as block:
        @block.sync
        def _(sp):
            sp.dma_start(S["res"][:, :], A["xT"]).then_inc(S["x_in"], 16)
            start_at_one(sp, S, "sync")
            for store in S["e_store"]:
                sp.sem_inc(store, 1)
            for dst, src in ((S["gains"][:, :], A["gains"]), (S["const"][:, :], A["const"]),
                             (S["w_glr"][:, :], A["w_glr"]), (S["w_gate"][0:RANK, :], A["w_gate"])):
                sp.dma_start(dst, src).then_inc(S["c_in"], 16)
            load_w(sp, S, 0, 0)
            load_w(sp, S, 0, 1)
            load_w(sp, S, 0, 2)

        @block.scalar
        def _(act):
            start_at_one(act, S, "scalar")
            rms_squares(nc, act, S, S["x_in"], 16)
            rms_root(nc, act, S, 0)
            split_hi(nc, act, S, 0, 0)
            split_activation_hi(nc, act, S, as3(S["big"][:, 8 * TOK:16 * TOK]), S["n_done"], 1)
            act.wait_ge(S["lam_sum"], 1)
            nc.scalar.activation(S["lam"][:, 2:4], S["aux2"][:, 0, 0:2], ACT.Exp).then_inc(S["lam_exp"], 1)
            act.wait_ge(S["glr_mm"], 1)
            nc.scalar.activation(halves(S["glr"][0:RANK, :]), S["mm"][0][0:RANK, :, 0:HALF],
                                 ACT.Copy).then_inc(S["glr_done"], 1)

        @block.vector
        def _(dve):
            start_at_one(dve, S, "vector")
            nc.vector.memset(S["ones"][:, :], 1.0).then_inc(S["d_init"], 1)
            nc.vector.memset(S["eps"][:, :], EPS).then_inc(S["d_init"], 1)
            dve.wait_ge(S["c_in"], 64)
            nc.vector.tensor_tensor(S["lam"][0:HD, 0:1], S["gains"][0:HD, G_LAM:G_LAM + 1],
                                    S["gains"][0:HD, G_LAM + 1:G_LAM + 2], ALU.mult).then_inc(S["d_init"], 1)
            nc.vector.tensor_tensor(S["lam"][0:HD, 1:2], S["gains"][0:HD, G_LAM + 2:G_LAM + 3],
                                    S["gains"][0:HD, G_LAM + 3:G_LAM + 4], ALU.mult).then_inc(S["d_init"], 1)
            nc.vector.tensor_scalar(S["gqk"][:, 0:8], S["gains"][:, G_QK:G_QK + 8], HD ** -0.5, None,
                                    ALU.mult).then_inc(S["d_init"], 1)
            nc.vector.tensor_copy(S["gqk"][:, 8:16], S["gains"][:, G_QK + 8:G_QK + 16]).then_inc(S["d_init"], 1)
            nc.vector.tensor_scalar(S["gsub"][:, :], S["gains"][:, G_SUB:G_SUB + 1], 1.0 - LAM_INIT, None,
                                    ALU.mult).then_inc(S["d_init"], 1)
            split_lo(nc, dve, S, 0, 0)
            rms_apply(nc, dve, S, 0, G_N1)
            split_activation_lo(nc, dve, S, as3(S["big"][:, 8 * TOK:16 * TOK]), 1)
            dve.wait_ge(S["lam_exp"], 1)
            nc.vector.tensor_tensor(S["lam"][:, 4:5], S["lam"][:, 3:4], S["lam"][:, 2:3],
                                    ALU.subtract).then_inc(S["lam_d"], 1)
            dve.wait_ge(S["lam_d"], 1)
            nc.vector.tensor_scalar(S["neglam"][:, :], S["lam"][:, 4:5], LAM_INIT, None,
                                    ALU.subtract).then_inc(S["lam_d"], 1)

        @block.gpsimd
        def _(pool):
            start_at_one(pool, S, "gpsimd")

        @block.tensor
        def _(pe):
            start_at_one(pe, S, "tensor")
            pe.wait_ge(S["d_init"], 7)
            rms_sum(nc, pe, S, 0)
            nc.tensor.matmul(S["aux2"][:, 0, 0:2], S["ones"][0:HD, :], S["lam"][0:HD, 0:2], start=True,
                             stop=True).then_inc(S["lam_sum"], 1)
            pe.wait_ge(S["n_done"], 1)
            for k in range(KT):
                ins = matmul_tok(nc, S["mm"][0][0:RANK], S["w_glr"][:, k * RANK:(k + 1) * RANK],
                                 S["big"][:, (8 + k) * TOK:(9 + k) * TOK], k == 0, k == KT - 1)
            ins.then_inc(S["glr_mm"], 1)


def stage_qkv(nc, S, A):
    with nc.Block() as block:
        @block.sync
        def _(sp):
            with sp.Fori(0, 12) as i:
                load_w(sp, S, i, 3)
                load_w(sp, S, i, 4)

        def hi_square_root(act, i, u, square=True, root=True):
            t = 2 * i + u
            split_hi(nc, act, S, i, u + 1)
            if square:
                act.wait_ge(S["evacuated"], t + 1)
                if not isinstance(t, int):
                    act.wait_ge(S["q_sum"], t - 1)
                nc.scalar.activation(S["sq"][:, u, :], feat(S, t), ACT.Square).then_inc(S["q_sq"], 1)
            if root:
                act.wait_ge(S["q_sum"], t)
                if not (isinstance(t, int) and t < 2):
                    act.wait_ge(S["q_norm"], t - 1)
                nc.scalar.activation(halves(S["root"][:, :]), S["aux"][:, :, 0:HALF], ACT.Sqrt,
                                     bias=S["eps"][:, 0:1], scale=1.0 / HD).then_inc(S["q_root"], 1)

        @block.scalar
        def _(act):
            hi_square_root(act, 0, 0, root=False)
            hi_square_root(act, 0, 1)
            with act.Fori(1, 8) as i:
                hi_square_root(act, i, 0)
                hi_square_root(act, i, 1)
            hi_square_root(act, 8, 0, square=False)
            hi_square_root(act, 8, 1, square=False, root=False)
            with act.Fori(9, 12) as i:
                split_hi(nc, act, S, i, 1)
                split_hi(nc, act, S, i, 2)

        def evacuate(dve, i, u):
            t = 2 * i + u
            split_lo(nc, dve, S, i, u + 1)
            dve.wait_ge(S["tile_done"], t + 1)
            nc.vector.tensor_copy(halves(feat(S, t)), S["mm"][u][:, :, 0:HALF]).then_inc(S["evacuated"], 1)

        def norm(dve, i, u):
            n = 2 * i + u
            dve.wait_ge(S["q_root"], n + 1)
            dve.wait_ge(S["q_norm"], n)
            nc.vector.reciprocal(S["rinv"][:, :], S["root"][:, :]).then_inc(S["q_rinv"], 1)
            dve.wait_ge(S["q_rinv"], n + 1)
            nc.vector.scalar_tensor_tensor(out=S["nq"][:, u, :], in0=feat(S, n), scalar=S["gqk"][:, bass.ds(n, 1)],
                                           in1=S["rinv"][:, :], op0=ALU.mult,
                                           op1=ALU.mult).then_inc(S["q_norm"], 1)

        def rotate(dve, i, u):
            n = 2 * i + u
            dve.wait_ge(S["q_swap"], n + 1)
            dve.wait_ge(S["q_roped"], 1 + n)
            nc.vector.tensor_tensor(halves(S["rsin"][:, :]), S["aux2"][:, :, 0:HALF],
                                    halves(S["const"][:, C_SIN:C_SIN + TOK]), ALU.mult).then_inc(S["q_rsin"], 1)
            dve.wait_ge(S["q_rsin"], 1 + n + 1)
            dve.wait_ge(S["q_cos"], n + 1)
            nc.vector.tensor_tensor(feat(S, n), S["rsin"][:, :], S["ncos"][:, u, :],
                                    ALU.add).then_inc(S["q_roped"], 1)

        @block.vector
        def _(dve):
            evacuate(dve, 0, 0)
            evacuate(dve, 0, 1)
            norm(dve, 0, 0)
            with dve.Fori(1, 8) as i:
                evacuate(dve, i, 0)
                norm(dve, i - 1, 1)
                rotate(dve, i - 1, 0)
                evacuate(dve, i, 1)
                norm(dve, i, 0)
                rotate(dve, i - 1, 1)
            evacuate(dve, 8, 0)
            norm(dve, 7, 1)
            rotate(dve, 7, 0)
            evacuate(dve, 8, 1)
            rotate(dve, 7, 1)
            with dve.Fori(9, 12) as i:
                evacuate(dve, i, 0)
                evacuate(dve, i, 1)

        @block.gpsimd
        def _(pool):
            def ncos(i, u):
                n = 2 * i + u
                pool.wait_ge(S["q_norm"], n + 1)
                if not isinstance(n, int):
                    pool.wait_ge(S["q_roped"], 1 + n - 1)
                    apart(pool, S)
                nc.gpsimd.tensor_tensor(S["ncos"][:, u, :], S["nq"][:, u, :], S["const"][:, C_COS:C_COS + TOK],
                                        ALU.mult).then_inc(S["q_cos"], 1)
            ncos(0, 0)
            ncos(0, 1)
            with pool.Fori(1, 8) as i:
                ncos(i, 0)
                ncos(i, 1)

        def head_sum(pe, i, u):
            n = 2 * i + u
            pe.wait_ge(S["q_sq"], n + 1)
            if not (isinstance(n, int) and n < 1):
                pe.wait_ge(S["q_root"], n)
            matmul_tok(nc, S["aux"], S["const"][:, C_BLK:C_BLK + P], S["sq"][:, u, :], True, True).then_inc(S["q_sum"], 1)

        def swap(pe, i, u):
            n = 2 * i + u
            pe.wait_ge(S["q_norm"], n + 1)
            if not (isinstance(n, int) and n < 1):
                pe.wait_ge(S["q_rsin"], 1 + n)
            matmul_tok(nc, S["aux2"], S["const"][:, C_ROT:C_ROT + P], S["nq"][:, u, :], True, True).then_inc(S["q_swap"], 1)

        @block.tensor
        def _(pe):
            pe.wait_ge(S["x_split"], 1)
            dense_tile(nc, pe, S, 0, 0)
            dense_tile(nc, pe, S, 0, 1)
            head_sum(pe, 0, 0)
            with pe.Fori(1, 8) as i:
                dense_tile(nc, pe, S, i, 0)
                head_sum(pe, i - 1, 1)
                swap(pe, i - 1, 0)
                dense_tile(nc, pe, S, i, 1)
                head_sum(pe, i, 0)
                swap(pe, i - 1, 1)
            dense_tile(nc, pe, S, 8, 0)
            head_sum(pe, 7, 1)
            swap(pe, 7, 0)
            dense_tile(nc, pe, S, 8, 1)
            swap(pe, 7, 1)
            with pe.Fori(9, 12) as i:
                dense_tile(nc, pe, S, i, 0)
                dense_tile(nc, pe, S, i, 1)


def stage_attention(nc, S, A, B):
    keys = [P * (j + 1) for j in range(4)] + [PAST + DEC]

    with nc.Block() as block:
        @block.sync
        def _(sp):
            sp.dma_start(A["kT_out"], as3(S["big"][:, 8 * TOK:16 * TOK])).then_inc(S["out_kv"], 16)
            sp.dma_start(A["vT_out"], as3(S["big"][:, 16 * TOK:24 * TOK])).then_inc(S["out_kv"], 16)
            def cache(i, u):
                h = 2 * i + u
                if not isinstance(h, int):
                    sp.wait_ge(S["a_pv"], 1 + 5 * (h - 1))
                sp.dma_start(B["ck"][:, u, :], A["ckT"][:, bass.ds(h, 1), :]).then_inc(S["a_cache"][u], 16)
                sp.dma_start(B["cv"][:, u, :], A["cv"][:, bass.ds(h, 1), :]).then_inc(S["a_cache"][u], 16)
            cache(0, 0)
            cache(0, 1)
            with sp.Fori(1, 4) as i:
                cache(i, 0)
                cache(i, 1)

        @block.gpsimd
        def _(pool):
            def stage(i, u):
                h = 2 * i + u
                if not isinstance(h, int):
                    pool.wait_ge(S["a_pv"], 1 + 5 * (h - 1))
                    apart(pool, S)
                for dst, j in ((B["qs"], 0), (B["ks"], 8), (B["vs"], 16)):
                    nc.gpsimd.tensor_copy(dst[:, u, :], feat(S, h + j)).then_inc(S["a_staged"], 1)
            stage(0, 0)
            stage(0, 1)
            with pool.Fori(1, 4) as i:
                stage(i, 0)
                stage(i, 1)

        @block.tensor
        def _(pe):
            def scores(i, u, j):
                h = 2 * i + u
                if j == 0:
                    pe.wait_ge(S["a_staged"], 3 * (h + 1))
                    pe.wait_ge(S["a_exp"], 1 + 5 * h)
                elif j == 1:
                    pe.wait_ge(S["o_root"], 1 + h)
                else:
                    pe.wait_ge(S["a_exp"], 1 + 5 * h + j - 1)
                apart(pe, S)
                q0, nq = token_cols(j)
                for m in range(2):
                    rows = slice(HD * m, HD * (m + 1))
                    q = B["qs"][rows, u, q0:q0 + nq]
                    out = B["s"][j % 2][0:nq, m]
                    if j < 4:
                        ins = nc.tensor.matmul(out[:, 0:keys[j]], q, B["ks"][rows, u, 0:keys[j]],
                                               start=True, stop=True)
                    else:
                        pe.wait_ge(S["a_cache"][u], 32 * (i + 1))
                        apart(pe, S)
                        nc.tensor.matmul(out[:, 0:PAST], q, B["ck"][rows, u, :], start=True, stop=True)
                        ins = nc.tensor.matmul(out[:, PAST:PAST + DEC], q, B["ks"][rows, u, SEQ:TOK],
                                               start=True, stop=True)
                ins.then_inc(S["a_scores"], 1)

            def turn_v(i, u):
                h = 2 * i + u
                pe.wait_ge(S["a_wT"], 1 + 5 * h)
                for c in range(NC_T):
                    t0, n = token_cols(c)
                    out = B["tr"][0][:, t0:t0 + P] if c < 4 else B["tr"][1][0:DEC, 0:P]
                    ins = nc.tensor.transpose(out, B["vs"][:, u, t0:t0 + n], S["ident"])
                ins.then_inc(S["a_vT"], 1)

            def turn_w(i, u, j):
                h = 2 * i + u
                pe.wait_ge(S["a_w"], 1 + 5 * h + j + 1)
                if j < 2:
                    pe.wait_ge(S["a_vtok"], 2 * (h + 1))
                else:
                    pe.wait_ge(S["a_wT"], 1 + 5 * h + j - 1)
                apart(pe, S)
                nq = token_cols(j)[1]
                for k in range((keys[j] + P - 1) // P):
                    nk = min(P, keys[j] - k * P)
                    ins = nc.tensor.transpose(B["tr"][j % 2][0:nk, k * nq:(k + 1) * nq],
                                              B["w"][0:nq, j % 2, k * P:k * P + nk], S["ident"][0:nq, 0:nq])
                ins.then_inc(S["a_turned"], 1)

            def times_v(i, u, j):
                h = 2 * i + u
                pe.wait_ge(S["a_wT"], 1 + 5 * h + j + 1)
                if j == 0:
                    pe.wait_ge(S["a_vtok"], 2 * (h + 1))
                    pe.wait_ge(S["o_evac"], 1 + h)
                nq = token_cols(j)[1]
                n_k = (keys[j] + P - 1) // P
                for k in range(n_k):
                    w = B["wT"][:, j % 2, k * nq:(k + 1) * nq]
                    if j < 4:
                        out, v = B["o"][:, 0, j * P:(j + 1) * P], B["vtok"][:, u, k * P:(k + 1) * P]
                    else:
                        out = B["o"][:, 1, 0:DEC]
                        v = B["cv"][:, u, k * P:(k + 1) * P] if k < 2 else B["vtok"][0:DEC, u, SEQ:SEQ + P]
                        w = w if k < 2 else w[0:DEC]
                    ins = nc.tensor.matmul(out, v, w, start=k == 0, stop=k == n_k - 1)
                ins.then_inc(S["a_pv"], 1)

            with pe.Fori(0, 4) as i:
                for u in range(2):
                    scores(i, u, 0)
                    turn_v(i, u)
                    for j in range(5):
                        if j < 4:
                            scores(i, u, j + 1)
                        turn_w(i, u, j)
                        times_v(i, u, j)
                    pe.wait_ge(S["o_sq"], 2 * i + u + 1)
                    nc.tensor.matmul(B["s"][1][:, 0, :], S["ones"][:, :], B["osq"][:, 0:SEQ], start=True, stop=True)
                    nc.tensor.matmul(B["s"][1][:, 1, 0:DEC], S["ones"][:, :], B["osq"][:, SEQ:TOK], start=True,
                                     stop=True).then_inc(S["o_sum"], 1)

        @block.scalar
        def _(act):
            def exps(i, u, j):
                n = 5 * (2 * i + u) + j
                act.wait_ge(S["a_max"], n + 1)
                nq = token_cols(j)[1]
                act.wait_ge(S["a_w"], 1 + (n - j if j < 2 else n - 1))
                for m in range(2):
                    ins = nc.scalar.activation(B["p"][0:nq, j % 2, m, 0:keys[j]], B["s"][j % 2][0:nq, m, 0:keys[j]],
                                               ACT.Exp, bias=B["nmax"][0:nq, j % 2, m:m + 1],
                                               accum_out=B["z"][0:nq, j % 2, m:m + 1])
                ins.then_inc(S["a_exp"], 1)

            def evac_wT(i, u, j):
                n = 5 * (2 * i + u) + j
                act.wait_ge(S["a_turned"], 1 + n + 1)
                act.wait_ge(S["a_pv"], 1 + (n - j if j < 2 else n - 1))
                if j < 4:
                    nc.scalar.activation(B["wT"][:, j % 2, 0:keys[j]], B["tr"][j % 2][:, 0:keys[j]],
                                         ACT.Copy).then_inc(S["a_wT"], 1)
                else:
                    nc.scalar.activation(B["wT"][:, 0, 0:2 * DEC], B["tr"][0][:, 0:2 * DEC], ACT.Copy)
                    nc.scalar.activation(B["wT"][0:DEC, 0, 2 * DEC:3 * DEC], B["tr"][0][0:DEC, 2 * DEC:3 * DEC],
                                         ACT.Copy).then_inc(S["a_wT"], 1)

            with act.Fori(0, 4) as i:
                for u in range(2):
                    h = 2 * i + u
                    exps(i, u, 0)
                    act.wait_ge(S["a_vT"], h + 1)
                    nc.scalar.activation(B["vtok"][:, u, 0:SEQ], B["tr"][0][:, :], ACT.Copy).then_inc(S["a_vtok"], 1)
                    nc.scalar.activation(B["vtok"][0:DEC, u, SEQ:SEQ + P], B["tr"][1][0:DEC, 0:P],
                                         ACT.Copy).then_inc(S["a_vtok"], 1)
                    for j in range(5):
                        if j < 4:
                            exps(i, u, j + 1)
                        evac_wT(i, u, j)
                    act.wait_ge(S["o_evac"], 1 + h + 1)
                    nc.scalar.activation(B["osq"][:, :], B["osb"][:, :], ACT.Square).then_inc(S["o_sq"], 1)
                    act.wait_ge(S["o_sum"], h + 1)
                    nc.scalar.activation(S["root"][:, 0:SEQ], B["s"][1][:, 0, :], ACT.Sqrt, bias=S["eps"][:, 0:1],
                                         scale=1.0 / P)
                    nc.scalar.activation(S["root"][:, SEQ:TOK], B["s"][1][:, 1, 0:DEC], ACT.Sqrt,
                                         bias=S["eps"][:, 0:1], scale=1.0 / P).then_inc(S["o_root"], 1)

        @block.vector
        def _(dve):
            def neg_max(i, u, j):
                n = 5 * (2 * i + u) + j
                dve.wait_ge(S["a_scores"], n + 1)
                nq = token_cols(j)[1]
                if j < 4:
                    nc.vector.memset(B["s"][j % 2][0:HD, :, P * j + HD:P * (j + 1)], NEG).then_inc(S["a_mask"], 1)
                    dve.wait_ge(S["a_mask"], 4 * (2 * i + u) + j + 1)
                nc.vector.tensor_reduce(B["nmax"][0:nq, j % 2, :], B["s"][j % 2][0:nq, :, 0:keys[j]], AX.X, ALU.max,
                                        negate=True).then_inc(S["a_max"], 1)

            def weights(i, u, j):
                n = 5 * (2 * i + u) + j
                nq = token_cols(j)[1]
                dve.wait_ge(S["a_exp"], 1 + n + 1)
                dve.wait_ge(S["a_w"], 1 + (n - j if j < 2 else n - 1))
                nc.vector.reciprocal(B["rz"][0:nq, j % 2, :], B["z"][0:nq, j % 2, :]).then_inc(S["a_rz"], 1)
                dve.wait_ge(S["a_rz"], 2 * n + 1)
                nc.vector.tensor_scalar(B["rz2"][0:nq, j % 2, 0:1], B["rz"][0:nq, j % 2, 1:2], S["neglam"][0:nq, 0:1], None,
                                        ALU.mult).then_inc(S["a_rz"], 1)
                dve.wait_ge(S["a_turned"], 1 + (n - j if j < 2 else n - 1))
                k = slice(0, keys[j])
                nc.vector.tensor_scalar(B["w"][0:nq, j % 2, k], B["p"][0:nq, j % 2, 0, k], B["rz"][0:nq, j % 2, 0:1], None,
                                        ALU.mult).then_inc(S["a_w1"], 1)
                dve.wait_ge(S["a_rz"], 2 * n + 2)
                dve.wait_ge(S["a_w1"], n + 1)
                nc.vector.scalar_tensor_tensor(out=B["w"][0:nq, j % 2, k], in0=B["p"][0:nq, j % 2, 1, k],
                                               scalar=B["rz2"][0:nq, j % 2, 0:1], in1=B["w"][0:nq, j % 2, k],
                                               op0=ALU.mult, op1=ALU.add).then_inc(S["a_w"], 1)

            with dve.Fori(0, 4) as i:
                for u in range(2):
                    h = 2 * i + u
                    neg_max(i, u, 0)
                    for j in range(5):
                        if j < 4:
                            neg_max(i, u, j + 1)
                        weights(i, u, j)
                    dve.wait_ge(S["a_pv"], 1 + 5 * (h + 1))
                    dve.wait_ge(S["o_done"], 1 + h)
                    nc.vector.tensor_copy(B["osb"][:, 0:SEQ], B["o"][:, 0, :])
                    nc.vector.tensor_copy(B["osb"][:, SEQ:TOK], B["o"][:, 1, 0:DEC]).then_inc(S["o_evac"], 1)
                    dve.wait_ge(S["o_root"], 1 + h + 1)
                    nc.vector.reciprocal(S["rinv"][:, :], S["root"][:, :]).then_inc(S["o_rinv"], 1)
                    dve.wait_ge(S["o_rinv"], h + 1)
                    nc.vector.scalar_tensor_tensor(out=S["res"][:, bass.ds(h * TOK, TOK)], in0=B["osb"][:, :],
                                                   scalar=S["gsub"][:, 0:1], in1=S["rinv"][:, :],
                                                   op0=ALU.mult, op1=ALU.mult).then_inc(S["o_done"], 1)


def stage_gla_inputs(nc, S, A):
    with nc.Block() as block:
        @block.sync
        def _(sp):
            with sp.Fori(T_GQ // 2, T_GA // 2) as i:
                load_w(sp, S, i, 3)
                load_w(sp, S, i, 4)

        @block.scalar
        def _(act):
            with act.Fori(T_GQ // 2, T_GR // 2) as i:
                split_hi(nc, act, S, i, 1)
                split_hi(nc, act, S, i, 2)
            with act.Fori(T_GR // 2, T_GA // 2) as i:
                for u in range(2):
                    split_hi(nc, act, S, i, u + 1)
                    act.wait_ge(S["tile_done"], 2 * i + u + 1)
                    nc.scalar.activation(halves(feat(S, 2 * i + u - T_GQ)), S["mm"][u][:, :, 0:HALF],
                                         ACT.Silu).then_inc(S["evacuated"], 1)

        @block.vector
        def _(dve):
            with dve.Fori(T_GQ // 2, T_GR // 2) as i:
                for u in range(2):
                    split_lo(nc, dve, S, i, u + 1)
                    dve.wait_ge(S["tile_done"], 2 * i + u + 1)
                    nc.vector.tensor_copy(halves(feat(S, 2 * i + u - T_GQ)),
                                          S["mm"][u][:, :, 0:HALF]).then_inc(S["evacuated"], 1)
            with dve.Fori(T_GR // 2, T_GA // 2) as i:
                split_lo(nc, dve, S, i, 1)
                split_lo(nc, dve, S, i, 2)

        @block.tensor
        def _(pe):
            for a, b in ((T_GQ, T_GR), (T_GR, T_GA)):
                pe.wait_ge(S["evacuated"], a)
                with pe.Fori(a // 2, b // 2) as i:
                    dense_tile(nc, pe, S, i, 0)
                    dense_tile(nc, pe, S, i, 1)


def stage_gla(nc, S, A, G):
    dk_scale = float(P) ** -0.5
    tau = 1.0 / 16.0
    n_lv = len(LEVELS)

    with nc.Block() as block:
        @block.sync
        def _(sp):
            with sp.Fori(0, GH) as h:
                sp.wait_ge(S["g_o"], 1 + 2 * h)
                apart(sp, S)
                sp.wait_ge(S["g_fin"], 1 + h)
                apart(sp, S)
                sp.dma_start(G["st"][:, 4, :], A["state_in"][:, bass.ds(h, 1), :]).then_inc(S["g_state"], 16)
                sp.wait_ge(S["g_chain"], 4 * h + 4)
                apart(sp, S)
                sp.dma_start(A["s_out"][:, bass.ds(h, 1), :], G["st"][:, 0, :]).then_inc(S["g_out"], 16)
                sp.wait_ge(S["g_fin"], 1 + h + 1)
                apart(sp, S)
                sp.dma_start(A["s_out"][:, bass.ds(h + GH, 1), :], G["s_fin"][:, :]).then_inc(S["g_out"], 16)

        @block.gpsimd
        def _(pool):
            with pool.Fori(0, GH) as h:
                pool.wait_ge(S["g_osum"], 1 + h)
                apart(pool, S)
                for v in range(2):
                    nc.gpsimd.tensor_copy(G["vs"][:, v, :], feat(S, 8 + 2 * h + v)).then_inc(S["g_vs"], 1)
                for n in range(n_lv + 2):
                    s = n % 2
                    w = SEQ if n == 0 else TOK
                    if n != n_lv:
                        pool.wait_ge(S["g_e"], (n_lv + 1) * h + min(n, n_lv) + 1 if n < n_lv else (n_lv + 1) * (h + 1))
                    if n >= 2:
                        pool.wait_ge(S["g_at"], 1 + n_lv * h + h + n - 1)
                    else:
                        pool.wait_ge(S["g_kT"], 1 + h)
                    apart(pool, S)
                    k = S["big"][:, bass.ds((GH + h) * TOK, w)]
                    if n == n_lv:
                        nc.gpsimd.tensor_copy(G["kl"][:, s, 0:w], k).then_inc(S["g_kl"], 1)
                    else:
                        nc.gpsimd.tensor_tensor(G["kl"][:, s, 0:w], k, G["e"][:, s, 0:w], ALU.mult).then_inc(S["g_kl"], 1)

        @block.scalar
        def _(act):
            act.wait_ge(S["g_z"], GH)
            for h in range(GH):
                pb = [S["mm"][0], S["mm"][1], S["aux"], S["aux2"]][h]
                ins = nc.scalar.activation(halves(G["b"][:, h * TOK:(h + 1) * TOK]), pb[:, :, 0:HALF], ACT.Identity,
                                           bias=S["gains"][:, G_BG + h:G_BG + h + 1])
            ins.then_inc(S["g_zb"], 1)
            act.wait_ge(S["g_zb"], 1)
            nc.scalar.activation(G["la"][:, :], G["b"][:, :], ACT.Abs).then_inc(S["g_la"], 1)
            act.wait_ge(S["g_la"], 1)
            nc.scalar.activation(G["la"][:, :], G["la"][:, :], ACT.Exp, scale=-1.0).then_inc(S["g_la"], 1)
            act.wait_ge(S["g_la"], 2)
            nc.scalar.activation(G["la"][:, :], G["la"][:, :], ACT.Ln, bias=1.0).then_inc(S["g_la"], 1)
            with act.Fori(0, GH) as h:
                bh = G["b"][:, bass.ds(h * TOK, TOK)]
                act.wait_ge(S["g_cum"], GH)
                act.wait_ge(S["g_at"], 1 + (n_lv + 1) * h)
                act.wait_ge(S["g_gated"], 1 + 2 * h)
                nc.scalar.activation(G["qb"][:, :], bh, ACT.Exp, scale=tau).then_inc(S["g_eb"], 1)
                bl = G["b"][:, bass.ds(h * TOK, SEQ)].rearrange("p (c n) -> p c n", n=P)[:, :, P - 1]
                nc.scalar.activation(G["el"][:, 0:4], bl, ACT.Exp, scale=tau).then_inc(S["g_eb"], 1)
                nc.scalar.activation(G["el"][:, 4:5], G["b"][:, bass.ds(h * TOK + TOK - 1, 1)], ACT.Exp,
                                     scale=tau).then_inc(S["g_eb"], 1)
                for v in range(2):
                    act.wait_ge(S["g_vT"], 2 * h + v + 1)
                    tr = [S["aux"], S["aux2"]][v]
                    cols = slice(v * P, (v + 1) * P)
                    nc.scalar.activation(G["vt"][:, 0:4, cols], tr[:, 0, :].rearrange("p (c n) -> p c n", n=P),
                                         ACT.Copy).then_inc(S["g_vt"], 1)
                    nc.scalar.activation(G["vt"][0:DEC, 4, cols], tr[0:DEC, 1, 0:P], ACT.Copy).then_inc(S["g_vt"], 1)
                for n in range(n_lv + 1):
                    s = n % 2 if n < n_lv else (n + 1) % 2
                    w = SEQ if n == 0 else TOK
                    act.wait_ge(S["g_d"], (n_lv + 1) * h + n + 1)
                    if n >= 2:
                        act.wait_ge(S["g_kl"], (n_lv + 2) * h + (n - 1 if n < n_lv else n_lv))
                        act.wait_ge(S["g_ql"], (n_lv + 1) * h + (n - 1 if n < n_lv else n_lv))
                    if n < n_lv:
                        nc.scalar.activation(G["e"][:, s, 0:w], G["dd"][:, n % 2, 0:w], ACT.Abs).then_inc(S["g_abs"], 1)
                        act.wait_ge(S["g_abs"], n_lv * h + n + 1)
                        nc.scalar.activation(G["e"][:, s, 0:w], G["e"][:, s, 0:w], ACT.Exp,
                                             scale=-tau).then_inc(S["g_e"], 1)
                    else:
                        nc.scalar.activation(G["e"][:, s, 0:w], G["dd"][:, n % 2, 0:w], ACT.Exp,
                                             scale=tau).then_inc(S["g_e"], 1)
                act.wait_ge(S["g_kT"], 1 + h + 1)
                nc.scalar.activation(G["kt"][:, 0:4, :], S["aux"][:, 0, :].rearrange("p (c n) -> p c n", n=P),
                                     ACT.Copy).then_inc(S["g_kt"], 1)
                nc.scalar.activation(G["kt"][0:DEC, 4, :], S["aux"][0:DEC, 1, 0:P], ACT.Copy).then_inc(S["g_kt"], 1)
                for v in range(2):
                    act.wait_ge(S["g_oc"], 1 + 2 * h + v + 1)
                    nc.scalar.activation(G["osq"][:, v, :], G["oc"][:, v, :], ACT.Square).then_inc(S["g_osq"], 1)
                act.wait_ge(S["g_osum"], 1 + h + 1)
                nc.scalar.activation(halves(S["root"][:, :]), S["aux"][:, :, 0:HALF], ACT.Sqrt, bias=S["eps"][:, 0:1],
                                     scale=1.0 / (2 * P)).then_inc(S["g_root"], 1)

        @block.vector
        def _(dve):
            dve.wait_ge(S["g_la"], 3)
            nc.vector.scalar_tensor_tensor(out=G["la"][:, :], in0=G["b"][:, :], scalar=0.0, in1=G["la"][:, :],
                                           op0=ALU.min, op1=ALU.subtract).then_inc(S["g_ls"], 1)
            dve.wait_ge(S["g_ls"], 1)
            for h in range(GH):
                nc.vector.tensor_tensor_scan(G["b"][:, h * TOK:(h + 1) * TOK], S["const"][:, C_RST:C_RST + TOK],
                                             G["la"][:, h * TOK:(h + 1) * TOK], 0.0, ALU.mult,
                                             ALU.add).then_inc(S["g_cum"], 1)
            with dve.Fori(0, GH) as h:
                q = S["big"][:, bass.ds(h * TOK, TOK)]
                dve.wait_ge(S["g_cum"], GH)
                dve.wait_ge(S["g_osum"], 1 + h)
                dve.wait_ge(S["g_gated"], 1 + 2 * h)
                nc.vector.memset(G["at"][:, :], 0.0).then_inc(S["g_at0"], 1)

                def delta(n):
                    s = n % 2
                    if n == n_lv:
                        dve.wait_ge(S["g_e"], (n_lv + 1) * h + n - 1)
                        bv = G["b"][:, bass.ds(h * TOK, SEQ)].rearrange("p (c n) -> p c n", n=P)
                        nc.vector.tensor_tensor(G["dd"][:, s, 0:SEQ].rearrange("p (c n) -> p c n", n=P),
                                                bcast(bv[:, :, P - 1], 2, P), bv, ALU.subtract)
                        bl = G["b"][:, bass.ds(h * TOK + TOK - 1, 1)]
                        nc.vector.tensor_tensor(G["dd"][:, s, SEQ:TOK], bl.to_broadcast([P, DEC]),
                                                G["b"][:, bass.ds(h * TOK + SEQ, DEC)],
                                                ALU.subtract).then_inc(S["g_d"], 1)
                        return
                    m = LEVELS[n]
                    w = SEQ if n == 0 else TOK
                    if n >= 2:
                        dve.wait_ge(S["g_e"], (n_lv + 1) * h + n - 1)
                    bv = G["b"][:, bass.ds(h * TOK, w)].rearrange("p (c n) -> p c n", n=2 * m)
                    nc.vector.tensor_tensor(G["dd"][:, s, 0:w].rearrange("p (c n) -> p c n", n=2 * m), bv,
                                            bcast(bv[:, :, m - 1], 2, 2 * m), ALU.subtract).then_inc(S["g_d"], 1)

                def merge(n):
                    s = n % 2
                    dve.wait_ge(S["g_at"], 1 + (n_lv + 1) * h + n + 1)
                    if n == 0:
                        dve.wait_ge(S["g_at0"], h + 1)
                    else:
                        dve.wait_ge(S["g_merge"], (n_lv + 1) * h + n)
                    apart(dve, S)
                    mask = S["const"][:, C_MSK + n * P:C_MSK + (n + 1) * P].bitcast(U32)
                    ins = nc.vector.copy_predicated(G["at"][:, 0:SEQ].rearrange("p (c n) -> p c n", n=P),
                                                    bcast(mask, 1, 4),
                                                    S["mm"][s][:, 0, :].rearrange("p (c n) -> p c n", n=P))
                    if n:
                        ins = nc.vector.copy_predicated(G["at"][0:DEC, SEQ:TOK], mask[0:DEC, 0:DEC],
                                                        S["mm"][s][0:DEC, 1, 0:DEC])
                    ins.then_inc(S["g_merge"], 1)

                delta(0)
                for n in range(n_lv + 1):
                    delta(n + 1) if n + 1 <= n_lv else None
                    s = n % 2
                    w = SEQ if n == 0 else TOK
                    if n >= 2:
                        dve.wait_ge(S["g_at"], 1 + (n_lv + 1) * h + n - 1)
                    qw = S["big"][:, bass.ds(h * TOK, w)]
                    if n < n_lv:
                        dve.wait_ge(S["g_e"], (n_lv + 1) * h + n + 1)
                        nc.vector.scalar_tensor_tensor(out=G["ql"][:, s, 0:w], in0=qw, scalar=dk_scale,
                                                       in1=G["e"][:, s, 0:w], op0=ALU.mult,
                                                       op1=ALU.mult).then_inc(S["g_ql"], 1)
                    else:
                        nc.vector.tensor_scalar(G["ql"][:, s, 0:w], qw, dk_scale, None, ALU.mult).then_inc(S["g_ql"], 1)
                    if n:
                        merge(n - 1)
                merge(n_lv)
                dve.wait_ge(S["g_eb"], 3 * h + 3)
                nc.vector.scalar_tensor_tensor(out=G["qb"][:, :], in0=q, scalar=dk_scale, in1=G["qb"][:, :],
                                               op0=ALU.mult, op1=ALU.mult).then_inc(S["g_qb"], 1)
                dve.wait_ge(S["g_ds"], h + 1)
                dve.wait_ge(S["g_out"], 1 + 32 * h)
                nc.vector.tensor_copy(G["st"][:, 1, :], S["aux2"][:, 0, 0:256]).then_inc(S["g_chain"], 1)
                for c in range(1, 4):
                    dve.wait_ge(S["g_chain"], 4 * h + c)
                    nc.vector.scalar_tensor_tensor(out=G["st"][:, (c + 1) % 4, :], in0=G["st"][:, c, :],
                                                   scalar=G["el"][:, c:c + 1],
                                                   in1=S["aux2"][:, c // 2, (c % 2) * 256:(c % 2) * 256 + 256],
                                                   op0=ALU.mult, op1=ALU.add).then_inc(S["g_chain"], 1)
                dve.wait_ge(S["g_state"], 16 * (h + 1))
                nc.vector.scalar_tensor_tensor(out=G["s_fin"][:, :], in0=G["st"][:, 4, :], scalar=G["el"][:, 4:5],
                                               in1=S["aux"][:, 0, 0:256], op0=ALU.mult,
                                               op1=ALU.add).then_inc(S["g_fin"], 1)
                for v in range(2):
                    dve.wait_ge(S["g_o"], 1 + 2 * h + v + 1)
                    nc.vector.tensor_copy(G["oc"][:, v, 0:SEQ], S["mm"][v][:, 0, :])
                    nc.vector.tensor_copy(G["oc"][:, v, SEQ:TOK], S["mm"][v][:, 1, 0:DEC]).then_inc(S["g_oc"], 1)
                dve.wait_ge(S["g_root"], 1 + h + 1)
                nc.vector.reciprocal(S["rinv"][:, :], S["root"][:, :]).then_inc(S["g_rinv"], 1)
                dve.wait_ge(S["g_rinv"], h + 1)
                for v in range(2):
                    nc.vector.scalar_tensor_tensor(out=G["oc"][:, v, :], in0=G["oc"][:, v, :],
                                                   scalar=S["gains"][:, G_GLA + v:G_GLA + v + 1], in1=S["rinv"][:, :],
                                                   op0=ALU.mult, op1=ALU.mult).then_inc(S["g_on"], 1)
                for v in range(2):
                    gate = feat(S, 16 + 2 * h + v)
                    dve.wait_ge(S["g_on"], 2 * h + v + 1)
                    nc.vector.tensor_tensor(gate, gate, G["oc"][:, v, :], ALU.mult).then_inc(S["g_gated"], 1)

        @block.tensor
        def _(pe):
            for h in range(GH):
                pb = [S["mm"][0], S["mm"][1], S["aux"], S["aux2"]][h]
                matmul_tok(nc, pb, S["w_gate"][0:RANK, h * P:(h + 1) * P], S["glr"][0:RANK, :], True,
                           True).then_inc(S["g_z"], 1)
            with pe.Fori(0, GH) as h:
                pe.wait_ge(S["g_vs"], 2 * h + 2)
                pe.wait_ge(S["g_zb"], 1)
                pe.wait_ge(S["g_root"], 1 + h)
                pe.wait_ge(S["g_fin"], 1 + h)
                for v in range(2):
                    tr = [S["aux"], S["aux2"]][v]
                    for c in range(NC_T):
                        t0, n = token_cols(c)
                        out = tr[:, 0, t0:t0 + P] if c < 4 else tr[0:DEC, 1, 0:P]
                        ins = nc.tensor.transpose(out, G["vs"][:, v, t0:t0 + n], S["ident"])
                    ins.then_inc(S["g_vT"], 1)
                for n in range(n_lv + 1):
                    s = n % 2
                    pe.wait_ge(S["g_ql"], (n_lv + 1) * h + n + 1)
                    pe.wait_ge(S["g_kl"], (n_lv + 2) * h + n + 1)
                    if n >= 2:
                        pe.wait_ge(S["g_merge"], (n_lv + 1) * h + n - 1)
                    else:
                        pe.wait_ge(S["g_oc"], 1 + 2 * h)
                    for c in range(4 if n == 0 else 5):
                        t0, w = token_cols(c)
                        out = S["mm"][s][:, 0, t0:t0 + P] if c < 4 else S["mm"][s][0:DEC, 1, 0:DEC]
                        ins = nc.tensor.matmul(out, G["kl"][:, s, t0:t0 + w], G["ql"][:, s, t0:t0 + w], start=True,
                                               stop=True)
                    ins.then_inc(S["g_at"], 1)
                s = (n_lv + 1) % 2
                pe.wait_ge(S["g_kl"], (n_lv + 2) * (h + 1))
                pe.wait_ge(S["g_vt"], 4 * (h + 1))
                for c in range(NC_T):
                    t0, n = token_cols(c)
                    out = S["aux"][:, 0, t0:t0 + P] if c < 4 else S["aux"][0:DEC, 1, 0:P]
                    ins = nc.tensor.transpose(out, G["kl"][:, s, t0:t0 + n], S["ident"])
                ins.then_inc(S["g_kT"], 1)
                pe.wait_ge(S["g_kt"], 2 * (h + 1))
                for c in range(4):
                    nc.tensor.matmul(S["aux2"][:, c // 2, (c % 2) * 256:(c % 2) * 256 + 256], G["kt"][:, c, :],
                                     G["vt"][:, c, :], start=True, stop=True)
                nc.tensor.matmul(S["aux"][:, 0, 0:256], G["kt"][0:DEC, 4, :], G["vt"][0:DEC, 4, :], start=True,
                                 stop=True).then_inc(S["g_ds"], 1)
                pe.wait_ge(S["g_merge"], (n_lv + 1) * (h + 1))
                pe.wait_ge(S["g_qb"], h + 1)
                pe.wait_ge(S["g_fin"], 1 + h + 1)
                for v in range(2):
                    vc = slice(v * P, (v + 1) * P)
                    for c in range(NC_T):
                        t0, n = token_cols(c)
                        out = S["mm"][v][:, 0, t0:t0 + P] if c < 4 else S["mm"][v][:, 1, 0:DEC]
                        ins = nc.tensor.matmul(out, G["vt"][0:n, c, vc], G["at"][0:n, t0:t0 + n], start=True,
                                               stop=c == 0)
                        if c:
                            ins = nc.tensor.matmul(out, G["st"][:, c, vc], G["qb"][:, t0:t0 + n], start=False,
                                                   stop=True)
                    ins.then_inc(S["g_o"], 1)
                for v in range(2):
                    pe.wait_ge(S["g_osq"], 2 * h + v + 1)
                    ins = matmul_tok(nc, S["aux"], S["ones"][:, :], G["osq"][:, v, :], v == 0, v == 1)
                ins.then_inc(S["g_osum"], 1)


def stage_mix(nc, S, A):
    res3 = as3(S["res"][:, :])
    ob3 = as3(S["big"][:, 16 * TOK:24 * TOK])
    mix3 = as3(S["big"][:, 0:8 * TOK])

    with nc.Block() as block:
        @block.sync
        def _(sp):
            with sp.Fori(T_GA // 2, T_PQ // 2) as i:
                load_w(sp, S, i, 3)
                load_w(sp, S, i, 4)

        @block.gpsimd
        def _(pool):
            pool.wait_ge(S["x_split"], 2)
            pool.dma_start(S["res"][:, :], A["xT"]).then_inc(S["x_again"], 16)

        @block.scalar
        def _(act):
            with act.Fori(T_GA // 2, T_WA // 2) as i:
                for u in range(2):
                    split_hi(nc, act, S, i, u + 1)
                    act.wait_ge(S["tile_done"], 2 * i + u + 1)
                    nc.scalar.activation(halves(feat(S, 2 * i + u - T_GA)), S["mm"][u][:, :, 0:HALF],
                                         ACT.Sigmoid).then_inc(S["evacuated"], 1)
            split_activation_hi(nc, act, S, res3, S["tile_done"], T_WA)
            with act.Fori(T_WA // 2, T_WB // 2) as i:
                split_hi(nc, act, S, i, 1)
                split_hi(nc, act, S, i, 2)
            split_activation_hi(nc, act, S, ob3, S["tile_done"], T_WB)
            with act.Fori(T_WB // 2, T_WO // 2) as i:
                split_hi(nc, act, S, i, 1)
                split_hi(nc, act, S, i, 2)
            split_activation_hi(nc, act, S, mix3, S["evacuated"], T_WO)
            with act.Fori(T_WO // 2, T_PQ // 2) as i:
                split_hi(nc, act, S, i, 1)
                split_hi(nc, act, S, i, 2)
            rms_squares(nc, act, S, S["evacuated"], T_PQ)
            rms_root(nc, act, S, 1)
            split_activation_hi(nc, act, S, as3(S["big"][:, 8 * TOK:16 * TOK]), S["n_done"], 2)

        @block.vector
        def _(dve):
            with dve.Fori(T_GA // 2, T_WA // 2) as i:
                split_lo(nc, dve, S, i, 1)
                split_lo(nc, dve, S, i, 2)
            split_activation_lo(nc, dve, S, res3, 2)
            with dve.Fori(T_WA // 2, T_WB // 2) as i:
                for u in range(2):
                    gate = halves(feat(S, 2 * i + u - T_WA))
                    split_lo(nc, dve, S, i, u + 1)
                    dve.wait_ge(S["tile_done"], 2 * i + u + 1)
                    nc.vector.tensor_tensor(gate, gate, S["mm"][u][:, :, 0:HALF], ALU.mult).then_inc(S["evacuated"], 1)
            split_activation_lo(nc, dve, S, ob3, 3)
            with dve.Fori(T_WB // 2, T_WO // 2) as i:
                for u in range(2):
                    n = 2 * i + u - T_WB
                    split_lo(nc, dve, S, i, u + 1)
                    dve.wait_ge(S["evacuated"], 2 * i + u)
                    dve.wait_ge(S["tile_done"], 2 * i + u + 1)
                    nc.vector.tensor_tensor(halves(S["rsin"][:, :]), halves(feat(S, n + 8)), S["mm"][u][:, :, 0:HALF],
                                            ALU.mult).then_inc(S["m_tmp"], 1)
                    dve.wait_ge(S["m_tmp"], n + 1)
                    nc.vector.tensor_tensor(feat(S, n), feat(S, n), S["rsin"][:, :],
                                            ALU.add).then_inc(S["evacuated"], 1)
            split_activation_lo(nc, dve, S, mix3, 4)
            dve.wait_ge(S["x_again"], 16)
            with dve.Fori(T_WO // 2, T_PQ // 2) as i:
                for u in range(2):
                    h = halves(S["res"][:, bass.ds((2 * i + u - T_WO) * TOK, TOK)])
                    split_lo(nc, dve, S, i, u + 1)
                    dve.wait_ge(S["tile_done"], 2 * i + u + 1)
                    nc.vector.tensor_tensor(h, h, S["mm"][u][:, :, 0:HALF], ALU.add).then_inc(S["evacuated"], 1)
            rms_apply(nc, dve, S, 1, G_N2)
            split_activation_lo(nc, dve, S, as3(S["big"][:, 8 * TOK:16 * TOK]), 5)

        @block.tensor
        def _(pe):
            for n, (a, b) in enumerate(((T_GA, T_WA), (T_WA, T_WB), (T_WB, T_WO), (T_WO, T_PQ))):
                pe.wait_ge(S["x_split"], n + 1)
                pe.wait_ge(S["evacuated"], a)
                with pe.Fori(a // 2, b // 2) as i:
                    dense_tile(nc, pe, S, i, 0)
                    dense_tile(nc, pe, S, i, 1)
            rms_sum(nc, pe, S, 1)


def stage_keys(nc, S, A, R):
    with nc.Block() as block:
        @block.sync
        def _(sp):
            sp.dma_start(R["sk"][:, :], A["skT"]).then_inc(S["r_sk"], 16)
            with sp.Fori(T_PQ // 2, T_END // 2 - 2) as i:
                load_w(sp, S, i, 3)
                load_w(sp, S, i, 4)
            load_w(sp, S, T_END // 2 - 2, 3)

        @block.scalar
        def _(act):
            def query(i, u, last=False):
                t = 2 * i + u
                if not last:
                    split_hi(nc, act, S, i, u + 1)
                act.wait_ge(S["tile_done"], t + 1)
                act.wait_ge(S["r_mm"], t - T_PQ - 1) if not (isinstance(t, int) and t < T_PQ + 2) else None
                nc.scalar.activation(halves(R["qp"][:, u, :]), S["mm"][u][:, :, 0:HALF], ACT.Copy).then_inc(S["evacuated"], 1)

            def scores(i, u):
                n = 2 * i + u - T_PQ
                act.wait_ge(S["r_mm"], n + 1)
                if not (isinstance(n, int) and n < 2):
                    act.wait_ge(S["r_top"], 1 + n - 1)
                nc.scalar.activation(R["s"][:, u, 0:SEQ], S["aux"][:, 0, :], ACT.Copy)
                nc.scalar.activation(R["s"][0:DEC, u, SEQ:SEQ + P], S["aux"][0:DEC, 1, 0:P],
                                     ACT.Copy).then_inc(S["r_s"], 1)
            b = T_PQ // 2
            query(b, 0)
            query(b, 1)
            scores(b, 0)
            with act.Fori(b + 1, T_END // 2 - 1) as i:
                query(i, 0)
                scores(i - 1, 1)
                query(i, 1)
                scores(i, 0)
            e = T_END // 2 - 1
            query(e, 0)
            scores(e - 1, 1)
            query(e, 1, last=True)
            scores(e, 0)
            scores(e, 1)

        @block.tensor
        def _(pe):
            def scores(i, u):
                n = 2 * i + u - T_PQ
                pe.wait_ge(S["evacuated"], 2 * i + u + 1)
                if not (isinstance(n, int) and n < 1):
                    pe.wait_ge(S["r_s"], n)
                for c in range(NC_T):
                    t0, w = token_cols(c)
                    out = S["aux"][:, 0, t0:t0 + P] if c < 4 else S["aux"][0:DEC, 1, 0:P]
                    ins = nc.tensor.matmul(out, R["qp"][:, u, t0:t0 + w], R["sk"][:, bass.ds(n * P, P)], start=True,
                                           stop=True)
                ins.then_inc(S["r_mm"], 1)
            pe.wait_ge(S["x_split"], 5)
            pe.wait_ge(S["evacuated"], T_PQ)
            pe.wait_ge(S["r_sk"], 16)
            b = T_PQ // 2
            dense_tile(nc, pe, S, b, 0)
            dense_tile(nc, pe, S, b, 1)
            scores(b, 0)
            with pe.Fori(b + 1, T_END // 2) as i:
                dense_tile(nc, pe, S, i, 0)
                scores(i - 1, 1)
                dense_tile(nc, pe, S, i, 1)
                scores(i, 0)
            scores(T_END // 2 - 1, 1)

        @block.vector
        def _(dve):
            def top16(i, u):
                n = 2 * i + u - T_PQ
                dve.wait_ge(S["r_s"], n + 1)
                if not (isinstance(n, int) and n < 2):
                    dve.wait_ge(S["r_kept"], 1 + 2 * n - 2)
                if not (isinstance(n, int) and n < 1):
                    dve.wait_ge(S["r_top"], 1 + n)
                apart(dve, S)
                rows = [P] * 4 + [DEC]

                def sc(c):
                    return R["s"][0:rows[c], u, c * P:(c + 1) * P]
                for c in range(NC_T):
                    ins = nc.vector.max(R["tv"][0:rows[c], u, c * 16:c * 16 + 8], sc(c))
                ins.then_inc(S["r_c"], 1)
                dve.wait_ge(S["r_c"], 3 * n + 1)
                apart(dve, S)
                for c in range(NC_T):
                    ins = nc.vector.match_replace(R["s2"][0:rows[c], c * P:(c + 1) * P],
                                                  R["tv"][0:rows[c], u, c * 16:c * 16 + 8], sc(c), NEG)
                ins.then_inc(S["r_c"], 1)
                for c in range(NC_T):
                    nc.vector.max_index(R["ti"][0:rows[c], u, c * 16:c * 16 + 8],
                                        R["tv"][0:rows[c], u, c * 16:c * 16 + 8], sc(c))
                dve.wait_ge(S["r_c"], 3 * n + 2)
                apart(dve, S)
                for c in range(NC_T):
                    ins = nc.vector.max(R["tv"][0:rows[c], u, c * 16 + 8:c * 16 + 16],
                                        R["s2"][0:rows[c], c * P:(c + 1) * P])
                ins.then_inc(S["r_c"], 1)
                dve.wait_ge(S["r_c"], 3 * n + 3)
                apart(dve, S)
                for c in range(NC_T):
                    ins = nc.vector.max_index(R["ti"][0:rows[c], u, c * 16 + 8:c * 16 + 16],
                                              R["tv"][0:rows[c], u, c * 16 + 8:c * 16 + 16],
                                              R["s2"][0:rows[c], c * P:(c + 1) * P])
                ins.then_inc(S["r_top"], 1)
            nc.vector.memset(R["tv"][:, :, :], 0.0).then_inc(S["r_init"], 1)
            nc.vector.memset(R["ti"][:, :, :], 0).then_inc(S["r_init"], 1)
            dve.wait_ge(S["r_init"], 2)
            b = T_PQ // 2
            split_lo(nc, dve, S, b, 1)
            split_lo(nc, dve, S, b, 2)
            top16(b, 0)
            with dve.Fori(b + 1, T_END // 2 - 1) as i:
                split_lo(nc, dve, S, i, 1)
                top16(i - 1, 1)
                split_lo(nc, dve, S, i, 2)
                top16(i, 0)
            e = T_END // 2 - 1
            split_lo(nc, dve, S, e, 1)
            top16(e - 1, 1)
            top16(e, 0)
            top16(e, 1)

        @block.gpsimd
        def _(pool):
            with pool.Fori(0, 2 * PH // 2) as i:
                for u in range(2):
                    n = 2 * i + u
                    pool.wait_ge(S["r_top"], 1 + n + 1)
                    apart(pool, S)
                    nc.gpsimd.tensor_copy(R["sv"][:, :, bass.ds(n * 16, 16)],
                                          R["tv"][:, u, :].rearrange("p (c k) -> p c k", k=16)).then_inc(S["r_kept"], 1)
                    nc.gpsimd.tensor_copy(R["si"][:, :, bass.ds(n * 16, 16)],
                                          R["ti"][:, u, :].rearrange("p (c k) -> p c k", k=16)).then_inc(S["r_kept"], 1)


def stage_route(nc, S, A, R):
    hk = PH * TOPK
    with nc.Block() as block:
        @block.vector
        def _(dve):
            with dve.Fori(0, NC_T) as c:
                def picks(table, half):
                    v = table[:, bass.ds(c, 1), :].rearrange("p o (h q k) -> p (o h) q k", h=PH, q=2)
                    return v[:, :, half, :]
                dve.wait_ge(S["t_ij"], 1 + 2 * c)
                cand4 = R["cand"][:, :].rearrange("p (h a b) -> p h a b", h=PH, a=TOPK)
                nc.vector.tensor_tensor(cand4, bcast(picks(R["sv"], 0), 3, TOPK), bcast(picks(R["sv"], 1), 2, TOPK),
                                        ALU.add).then_inc(S["t_cand"], 1)
                dve.wait_ge(S["t_cand"], c + 1)
                apart(dve, S)

                def cols(h):
                    return slice(h * 256, (h + 1) * 256)
                for h in range(PH):
                    ins = nc.vector.max(R["v2"][:, h * 16:h * 16 + 8], R["cand"][:, cols(h)])
                ins.then_inc(S["t_c"], 1)
                dve.wait_ge(S["t_c"], 3 * c + 1)
                apart(dve, S)
                for h in range(PH):
                    ins = nc.vector.match_replace(R["cand2"][:, cols(h)], R["v2"][:, h * 16:h * 16 + 8],
                                                  R["cand"][:, cols(h)], NEG)
                ins.then_inc(S["t_c"], 1)
                for h in range(PH):
                    nc.vector.max_index(R["i2"][:, h * 16:h * 16 + 8], R["v2"][:, h * 16:h * 16 + 8], R["cand"][:, cols(h)])
                dve.wait_ge(S["t_c"], 3 * c + 2)
                apart(dve, S)
                for h in range(PH):
                    ins = nc.vector.max(R["v2"][:, h * 16 + 8:h * 16 + 16], R["cand2"][:, cols(h)])
                ins.then_inc(S["t_c"], 1)
                dve.wait_ge(S["t_c"], 3 * c + 3)
                apart(dve, S)
                for h in range(PH):
                    ins = nc.vector.max_index(R["i2"][:, h * 16 + 8:h * 16 + 16], R["v2"][:, h * 16 + 8:h * 16 + 16],
                                              R["cand2"][:, cols(h)])
                ins.then_inc(S["t_idx"], 1)
                v3 = R["v2"][:, :].rearrange("p (h k) -> p h k", h=PH)
                g3 = R["gij"][:, 0, :].rearrange("p (h k) -> p h k", h=PH)
                nc.vector.tensor_tensor(R["e2"][:, :].rearrange("p (h k) -> p h k", h=PH), v3,
                                        bcast(v3[:, :, 0], 2, TOPK), ALU.subtract).then_inc(S["t_sub"], 1)
                dve.wait_ge(S["t_exp"], c + 1)
                nc.vector.tensor_reduce(R["z2"][:, 0:PH], R["e2"][:, :].rearrange("p (h k) -> p h k", h=PH), AX.X,
                                        ALU.add).then_inc(S["t_z"], 1)
                dve.wait_ge(S["t_z"], 2 * c + 1)
                nc.vector.reciprocal(R["z2"][:, PH:2 * PH], R["z2"][:, 0:PH]).then_inc(S["t_z"], 1)
                dve.wait_ge(S["t_z"], 2 * c + 2)
                dve.wait_ge(S["t_turned"], 1 + c)
                nc.vector.tensor_tensor(g3, R["e2"][:, :].rearrange("p (h k) -> p h k", h=PH),
                                        bcast(R["z2"][:, PH:2 * PH], 2, TOPK), ALU.mult).then_inc(S["t_g"], 1)
                dve.wait_ge(S["t_idx"], c + 1)
                nc.vector.tensor_scalar(R["ab"][:, 0, :], R["i2"][:, :], 4, None, ALU.logical_shift_right).then_inc(S["t_ab"], 1)
                nc.vector.tensor_scalar(R["ab"][:, 1, :], R["i2"][:, :], 15, None, ALU.bitwise_and).then_inc(S["t_ab"], 1)
                dve.wait_ge(S["t_ab"], 4 * c + 2)
                nc.vector.tensor_copy(R["abf"][:, 0, :], R["ab"][:, 0, :]).then_inc(S["t_ab"], 1)
                nc.vector.tensor_copy(R["abf"][:, 1, :], R["ab"][:, 1, :]).then_inc(S["t_ab"], 1)
                dve.wait_ge(S["t_ab"], 4 * c + 4)
                iota16 = S["const"][:, C_IOTA:C_IOTA + TOPK]
                for q in range(2):
                    eq = R["cand2"] if q else R["cand"]
                    nc.vector.tensor_tensor(eq[:, :].rearrange("p (n a) -> p n a", a=TOPK),
                                            bcast(R["abf"][:, q, :], 2, TOPK), bcast(iota16, 1, hk),
                                            ALU.is_equal).then_inc(S["t_eq"], 1)
                for q in range(2):
                    eq = R["cand2"] if q else R["cand"]
                    e4 = eq[:, :].rearrange("p (h k a) -> p h k a", h=PH, k=TOPK)
                    dve.wait_ge(S["t_eq"], 4 * c + q + 1)
                    nc.vector.tensor_tensor(e4, e4, bcast(picks(R["si"], q), 2, TOPK), ALU.mult).then_inc(S["t_eq"], 1)
                for q in range(2):
                    eq = R["cand2"] if q else R["cand"]
                    dve.wait_ge(S["t_eq"], 4 * c + q + 3)
                    nc.vector.tensor_reduce(R["gij"][:, 1 + q, :], eq[:, :].rearrange("p (n a) -> p n a", a=TOPK),
                                            AX.X, ALU.add).then_inc(S["t_ij"], 1)

        @block.scalar
        def _(act):
            with act.Fori(0, NC_T) as c:
                act.wait_ge(S["t_sub"], c + 1)
                nc.scalar.activation(R["e2"][:, :], R["e2"][:, :], ACT.Exp).then_inc(S["t_exp"], 1)
                act.wait_ge(S["t_turned"], 1 + c + 1)
                nc.scalar.activation(R["tab"][:, :, bass.ds(c * P, P)],
                                     S["aux"][:, 0, 0:3 * P].rearrange("p (q n) -> p q n", q=3),
                                     ACT.Copy).then_inc(S["t_tab"], 1)

        @block.tensor
        def _(pe):
            with pe.Fori(0, NC_T) as c:
                pe.wait_ge(S["t_ij"], 1 + 2 * c + 2)
                pe.wait_ge(S["t_g"], c + 1)
                pe.wait_ge(S["t_tab"], 1 + c)
                for q in range(3):
                    ins = nc.tensor.transpose(S["aux"][:, 0, q * P:(q + 1) * P], R["gij"][:, q, :], S["ident"])
                ins.then_inc(S["t_turned"], 1)


def stage_gates(nc, S, A, R, Q):
    GRP = 8
    n_grp = CHUNK_TOK // GRP
    n_chunk = TOK // CHUNK_TOK
    pairs = n_chunk * n_grp // 2
    iota = S["const"][:, C_IOTA:C_IOTA + P]
    banks = [S["mm"][0], S["mm"][1]]

    with nc.Block() as block:
        @block.vector
        def _(dve):
            def weighted(i, u):
                g = 2 * i + u
                if not isinstance(g, int):
                    dve.wait_ge(S["e_mm"], g - 1)
                for j in range(GRP):
                    ins = nc.vector.tensor_scalar(Q["a"][:, u, j * P:(j + 1) * P], iota,
                                                  R["tab"][:, 1, bass.ds(g * GRP + j, 1)],
                                                  R["tab"][:, 0, bass.ds(g * GRP + j, 1)], ALU.is_equal, ALU.mult)
                ins.then_inc(S["e_a"], 1)
            weighted(0, 0)
            weighted(0, 1)
            with dve.Fori(1, pairs) as i:
                weighted(i, 0)
                weighted(i, 1)

        @block.gpsimd
        def _(pool):
            def one_hot(i, u):
                g = 2 * i + u
                if not isinstance(g, int):
                    pool.wait_ge(S["e_mm"], g - 1)
                    apart(pool, S)
                nc.gpsimd.tensor_copy(Q["i2"][:, u, :], R["tab"][:, 2, bass.ds(g * GRP, GRP)]).then_inc(S["e_i2"], 1)
                pool.wait_ge(S["e_i2"], g + 1)
                apart(pool, S)
                for j in range(GRP):
                    ins = nc.gpsimd.tensor_scalar(Q["b"][:, u, j * P:(j + 1) * P], iota, Q["i2"][:, u, j:j + 1], None,
                                                  ALU.is_equal)
                ins.then_inc(S["e_b"], 1)
            one_hot(0, 0)
            one_hot(0, 1)
            with pool.Fori(1, pairs) as i:
                one_hot(i, 0)
                one_hot(i, 1)

        @block.tensor
        def _(pe):
            def products(i, u):
                g = 2 * i + u
                pe.wait_ge(S["e_a"], g + 1)
                pe.wait_ge(S["e_b"], g + 1)
                if not isinstance(g, int):
                    pe.wait_ge(S["e_out"], g - 1)
                for j in range(GRP):
                    ins = nc.tensor.matmul(banks[u][:, j // 4, (j % 4) * P:(j % 4 + 1) * P],
                                           Q["b"][:, u, j * P:(j + 1) * P], Q["a"][:, u, j * P:(j + 1) * P],
                                           start=True, stop=True)
                ins.then_inc(S["e_mm"], 1)
            products(0, 0)
            products(0, 1)
            with pe.Fori(1, pairs) as i:
                products(i, 0)
                products(i, 1)

        @block.scalar
        def _(act):
            def chunk(k2, half):
                act.wait_ge(S["e_store"][half], 1 + 16 * k2)
                with act.Fori(0, n_grp // 2) as i:
                    for u in range(2):
                        g = k2 * (2 * n_grp) + half * n_grp + 2 * i + u
                        act.wait_ge(S["e_mm"], g + 1)
                        src = banks[u][:, :, :].rearrange("p q (j n) -> p n (q j)", n=P)
                        dst = Q["ring"][:, :, bass.ds((2 * i + u) * GRP + half * CHUNK_TOK, GRP)]
                        nc.scalar.activation(dst, src, ACT.Copy).then_inc(S["e_out"], 1)
            with act.Fori(0, n_chunk // 2) as k2:
                chunk(k2, 0)
                chunk(k2, 1)
            chunk(n_chunk // 2, 0)

        @block.sync
        def _(sp):
            def store(k2, half):
                sp.wait_ge(S["e_out"], n_grp * (2 * k2 + half + 1))
                sp.dma_start(A["gate"][:, :, bass.ds((2 * k2 + half) * CHUNK_TOK, CHUNK_TOK)],
                             Q["ring"][:, :, half * CHUNK_TOK:(half + 1) * CHUNK_TOK]).then_inc(S["e_store"][half], 16)
            with sp.Fori(0, n_chunk // 2) as k2:
                store(k2, 0)
                store(k2, 1)
            store(n_chunk // 2, 0)
            sp.wait_ge(S["e_store"][0], 1 + 16 * (n_chunk // 2 + 1))
            sp.wait_ge(S["e_store"][1], 1 + 16 * (n_chunk // 2))


def stage_experts(nc, S, A, E):
    groups = N_KEYS // 4

    def load_u(sp, g, c):
        e = 4 * g + c
        if not (isinstance(e, int) and e < 2):
            sp.wait_ge(S["u_lo"], e - 1)
        sp.dma_start(S["w_raw"][:, c % 2, :], A["u"][:, bass.ds(e, 1), :]).then_inc(S["u_in"][c % 2], 16)

    def load_gv(sp, g, c):
        e = 4 * g + c
        if not (isinstance(e, int) and e < 2):
            sp.wait_ge(S["u_p"], e - 1)
        sp.dma_start(E["gate"][:, c % 2, :], A["gate"][:, bass.ds(e, 1), :]).then_inc(S["g_in"][c % 2], 16)
        if not (isinstance(e, int) and e < 2):
            sp.wait_ge(S["v_lo"], e - 1)
        sp.dma_start(E["v_raw"][:, c % 2, :], A["v"][:, bass.ds(e, 1), :]).then_inc(S["v_in"][c % 2], 16)

    def u_hi(act, g, c):
        e = 4 * g + c
        act.wait_ge(S["u_in"][c % 2], 16 * (2 * g + c // 2 + 1))
        if not (isinstance(e, int) and e < 2):
            act.wait_ge(S["u_mm"], e - 1)
        nc.scalar.activation(S["w_hi"][:, c % 2, :], S["w_raw"][:, c % 2, :], ACT.Copy).then_inc(S["u_hi"], 1)

    def u_lo(dve, g, c):
        dve.wait_ge(S["u_hi"], 4 * g + c + 1)
        nc.vector.tensor_tensor(S["w_lo"][:, c % 2, :], S["w_raw"][:, c % 2, :], S["w_hi"][:, c % 2, :].bitcast(F32),
                                ALU.subtract).then_inc(S["u_lo"], 1)

    def last(g, c, ahead):
        e = 4 * g + c
        return isinstance(e, int) and e + ahead >= N_KEYS

    with nc.Block() as block:
        @block.sync
        def _(sp):
            def step(g, c):
                if not last(g, c, 4):
                    load_u(sp, g, c + 4)
                if not last(g, c, 2):
                    load_gv(sp, g, c + 2)
            load_u(sp, 0, 0)
            load_u(sp, 0, 1)
            load_gv(sp, 0, 0)
            load_gv(sp, 0, 1)
            load_u(sp, 0, 2)
            load_u(sp, 0, 3)
            step(0, 0)
            with sp.Fori(0, groups - 2) as g:
                for c in range(1, 5):
                    step(g, c)
            for c in range(1, 5):
                step(groups - 2, c)
            step(groups - 1, 1)
            sp.wait_ge(S["y_add"], 1 + KT * groups)
            sp.dma_start(A["yT_out"], as3(S["res"][:, :])).then_inc(S["out_y"], 16)
            sp.wait_ge(S["out_y"], 16)
            sp.wait_ge(S["out_kv"], 32)
            sp.wait_ge(S["g_out"], 1 + 32 * GH)

        @block.scalar
        def _(act):
            def step(g, c):
                e = 4 * g + c
                act.wait_ge(S["u_mm"], e + 1)
                nc.scalar.activation(halves(E["gel"][:, :]), S["mm"][c % 2][:, :, 0:HALF], ACT.Gelu).then_inc(S["u_gel"], 1)
                if not last(g, c, 2):
                    u_hi(act, g, c + 2)
                act.wait_ge(S["u_p"], e + 1)
                if c == 4:
                    act.wait_ge(S["y_mm"], KT * (g + 1))
                nc.scalar.activation(E["p_hi"][:, c % 4, :], E["p"][:, :], ACT.Copy).then_inc(S["u_phi"], 1)
                act.wait_ge(S["v_in"][c % 2], 16 * (2 * g + c // 2 + 1))
                nc.scalar.activation(E["v_hi"][:, c % 4, :], E["v_raw"][:, c % 2, :], ACT.Copy).then_inc(S["v_hi"], 1)
            u_hi(act, 0, 0)
            u_hi(act, 0, 1)
            step(0, 0)
            with act.Fori(0, groups - 1) as g:
                for c in range(1, 5):
                    step(g, c)
            for c in range(1, 4):
                step(groups - 1, c)

        @block.vector
        def _(dve):
            def add_y(g):
                for d in range(KT):
                    r = halves(S["res"][:, d * TOK:(d + 1) * TOK])
                    dve.wait_ge(S["y_mm"], KT * g + d + 1)
                    nc.vector.tensor_tensor(r, r, [S["aux"], S["aux2"]][d % 2][:, :, 0:HALF], ALU.add).then_inc(S["y_add"], 1)

            def step(g, c):
                e = 4 * g + c
                if not last(g, c, 2):
                    u_lo(dve, g, c + 2)
                if c == 4:
                    add_y(g)
                dve.wait_ge(S["u_gel"], e + 1)
                if not (isinstance(e, int) and e < 1):
                    dve.wait_ge(S["u_plo"], e)
                dve.wait_ge(S["g_in"][c % 2], 16 * (2 * g + c // 2 + 1))
                nc.vector.tensor_tensor(E["p"][:, :], E["gel"][:, :], E["gate"][:, c % 2, :], ALU.mult).then_inc(S["u_p"], 1)
                dve.wait_ge(S["u_phi"], e + 1)
                nc.vector.tensor_tensor(E["p_lo"][:, c % 4, :], E["p"][:, :], E["p_hi"][:, c % 4, :].bitcast(F32),
                                        ALU.subtract).then_inc(S["u_plo"], 1)
                dve.wait_ge(S["v_hi"], e + 1)
                nc.vector.tensor_tensor(E["v_lo"][:, c % 4, :], E["v_raw"][:, c % 2, :], E["v_hi"][:, c % 4, :].bitcast(F32),
                                        ALU.subtract).then_inc(S["v_lo"], 1)
            u_lo(dve, 0, 0)
            u_lo(dve, 0, 1)
            step(0, 0)
            with dve.Fori(0, groups - 1) as g:
                for c in range(1, 5):
                    step(g, c)
            for c in range(1, 4):
                step(groups - 1, c)
            add_y(groups - 1)

        @block.tensor
        def _(pe):
            def run_u(g, c):
                e = 4 * g + c
                pe.wait_ge(S["u_lo"], e + 1)
                if not (isinstance(e, int) and e < 2):
                    pe.wait_ge(S["u_gel"], e - 1) if c > 1 else pe.wait_ge(S["u_gel"], e)
                for f in range(2):
                    cols = slice(f * HALF, (f + 1) * HALF)
                    for k in range(KT):
                        w = slice(k * P, (k + 1) * P)
                        ins = product3(nc, S["mm"][c % 2][:, f, 0:HALF], S["w_hi"][:, c % 2, w], S["w_lo"][:, c % 2, w],
                                       S["x_hi"][:, k, cols], S["x_lo"][:, k, cols], k == 0, k == KT - 1)
                ins.then_inc(S["u_mm"], 1)

            def run_y(g):
                pe.wait_ge(S["u_plo"], 4 * (g + 1))
                pe.wait_ge(S["v_lo"], 4 * (g + 1))
                for d in range(KT):
                    pe.wait_ge(S["y_add"], 1 + (KT * g if d < 2 else KT * g + d - 1))
                    w = slice(d * P, (d + 1) * P)
                    for f in range(2):
                        cols = slice(f * HALF, (f + 1) * HALF)
                        for j in range(4):
                            ins = product3(nc, [S["aux"], S["aux2"]][d % 2][:, f, 0:HALF], E["v_hi"][:, j, w],
                                           E["v_lo"][:, j, w], E["p_hi"][:, j, cols], E["p_lo"][:, j, cols], j == 0, j == 3)
                    ins.then_inc(S["y_mm"], 1)
            run_u(0, 0)
            with pe.Fori(0, groups - 1) as g:
                for c in range(1, 5):
                    run_u(g, c)
                run_y(g)
            for c in range(1, 4):
                run_u(groups - 1, c)
            run_y(groups - 1)


SEMS = """passed x_in x_again c_in w_split w_hi_done tile_done evacuated x_hi_done x_split n_sq n_sum n_root n_rinv
n_done d_init lam_sum lam_exp lam_d glr_mm glr_done q_sq q_sum q_root q_rinv q_norm q_swap q_cos q_rsin
q_roped out_kv a_staged a_scores a_mask a_max a_exp a_rz a_w1 a_w a_vT a_vtok a_turned a_wT a_pv o_evac
o_sq o_sum o_root o_rinv o_done g_z g_zb g_la g_ls g_cum g_state g_out g_vs g_vT g_vt g_eb g_at0 g_d
g_abs g_e g_kl g_ql g_at g_merge g_kT g_kt g_ds g_chain g_fin g_qb g_o g_oc g_osq g_osum g_root
g_rinv g_on g_gated m_tmp r_sk r_mm r_s r_c r_top r_kept r_init t_cand t_c t_idx t_sub t_exp t_z t_g
t_ab t_eq t_ij t_turned t_tab e_mm e_a e_i2 e_b e_out u_lo u_hi u_mm u_gel u_p u_phi u_plo v_hi v_lo
y_mm y_add out_y""".split()
PAIR_SEMS = "w_loaded a_cache e_store u_in g_in v_in".split()


def build(nc, A):
    with ExitStack() as ctx:
        S = {}
        for name in SEMS:
            S[name] = ctx.enter_context(nc.semaphore(name))
        for name in PAIR_SEMS:
            S[name] = [ctx.enter_context(nc.semaphore(f"{name}{i}")) for i in range(2)]

        def make(stack, ns, stage, **shapes):
            for name, (shape, dt) in shapes.items():
                ns[name] = stack.enter_context(nc.sbuf_tensor(f"{stage}_{name}", [P] + shape, dt))

        psum = [ctx.enter_context(nc.psum_tensor(f"bank{i}", [P, 2, 512], F32)) for i in range(4)]
        S["mm"], S["aux"], S["aux2"] = psum[0:2], psum[2], psum[3]
        S["w_all"] = A["w_all"]
        make(ctx, S, "all",
             res=([KT * TOK], F32),
             x_hi=([KT, TOK], F32R), x_lo=([KT, TOK], F32R),
             w_raw=([2, D], F32), w_hi=([2, D], F32R), w_lo=([2, D], F32R),
             const=([C_END], F32), gains=([G_END], F32), gqk=([16], F32), gsub=([1], F32),
             lam=([5], F32), neglam=([1], F32), eps=([1], F32), ones=([P], F32),
             root=([TOK], F32), rinv=([TOK], F32), rsin=([TOK], F32))
        S["ident"] = S["const"][:, C_ID:C_ID + P]
        with ExitStack() as mixers:
            make(mixers, S, "mix", w_glr=([KT * RANK], F32), w_gate=([D // 2], F32), glr=([TOK], F32),
                 big=([24 * TOK], F32))
            stage_norm1(nc, S, A)
            with ExitStack() as here:
                make(here, S, "qkv", sq=([2, TOK], F32), nq=([2, TOK], F32), ncos=([2, TOK], F32))
                stage_qkv(nc, S, A)
            with ExitStack() as here:
                B = {}
                make(here, B, "att", qs=([2, TOK], F32), ks=([2, TOK], F32), vs=([2, TOK], F32), ck=([2, PAST], F32),
                     cv=([2, PAST], F32), vtok=([2, NC_T * P], F32), p=([2, 2, 512], F32), w=([2, 512], F32),
                     wT=([2, 512], F32), nmax=([2, 2], F32), z=([2, 2], F32), rz=([2, 2], F32),
                     rz2=([2, 1], F32), osb=([TOK], F32), osq=([TOK], F32))
                B["s"], B["o"] = S["mm"], S["aux2"]
                B["tr"] = [S["aux"][:, 0, :], S["aux"][:, 1, :]]
                stage_attention(nc, S, A, B)
            stage_gla_inputs(nc, S, A)
            with ExitStack() as here:
                G = {}
                make(here, G, "gla", b=([GH * TOK], F32), la=([GH * TOK], F32), e=([2, TOK], F32), dd=([2, TOK], F32),
                     qb=([TOK], F32), at=([TOK], F32), vt=([NC_T, 256], F32), kt=([NC_T, P], F32),
                     st=([5, 256], F32), s_fin=([256], F32), el=([5], F32))
                G["kl"] = G["la"][:, 0:2 * TOK].rearrange("p (s n) -> p s n", s=2)
                G["ql"] = G["la"][:, 2 * TOK:4 * TOK].rearrange("p (s n) -> p s n", s=2)
                G["vs"] = G["osq"] = G["e"]
                G["oc"] = G["dd"]
                stage_gla(nc, S, A, G)
            stage_mix(nc, S, A)
        R = {}
        with ExitStack() as routing:
            make(routing, R, "route", tab=([3, NC_T * P], F32))
            with ExitStack() as here:
                make(here, R, "keys", sk=([2 * PH * P], F32), qp=([2, TOK], F32), s=([2, NC_T * P], F32),
                     s2=([NC_T * P], F32), tv=([2, NC_T * 16], F32), ti=([2, NC_T * 16], U32),
                     sv=([NC_T, 2 * PH * 16], F32), si=([NC_T, 2 * PH * 16], F32), cand=([PH * 256], F32),
                     cand2=([PH * 256], F32), v2=([P], F32), i2=([P], U32), e2=([P], F32), z2=([2 * PH], F32),
                     ab=([2, P], U32), abf=([2, P], F32), gij=([3, P], F32))
                stage_keys(nc, S, A, R)
                stage_route(nc, S, A, R)
            with ExitStack() as here:
                Q = {}
                make(here, Q, "gates", a=([2, 8 * P], F32), b=([2, 8 * P], F32), i2=([2, 8], F32), ring=([P, 2 * CHUNK_TOK], F32))
                stage_gates(nc, S, A, R, Q)
        with ExitStack() as here:
            E = {}
            make(here, E, "exp", v_raw=([2, D], F32), v_hi=([4, D], F32R), v_lo=([4, D], F32R), gate=([2, TOK], F32),
                 gel=([TOK], F32), p=([TOK], F32), p_hi=([4, TOK], F32R), p_lo=([4, TOK], F32R))
            stage_experts(nc, S, A, E)


def const_table():
    t = np.zeros((P, C_END), np.float32)
    idx = np.arange(P)
    t[:, C_ID:C_ID + P] = np.eye(P)
    t[:, C_BLK:C_BLK + P] = idx[:, None] // HD == idx[None, :] // HD
    d = idx % HD
    for m in range(P):
        if d[m] < HD // 2:
            t[m + HD // 2, C_ROT + m] = -1.0
        else:
            t[m - HD // 2, C_ROT + m] = 1.0
    t[:, C_IOTA:C_IOTA + P] = idx[None, :]
    half = HD // 2
    inv = np.float32(10000.0) ** (-np.arange(half, dtype=np.float32) / np.float32(half))
    pos = np.concatenate([np.arange(SEQ), PAST + np.arange(DEC)]).astype(np.float32)
    ang = pos[None, :] * inv[idx % half][:, None]
    t[:, C_COS:C_COS + TOK] = np.cos(ang)
    t[:, C_SIN:C_SIN + TOK] = np.sin(ang)
    t[:, C_RST:C_RST + TOK] = (np.arange(TOK) % P != 0)[None, :]
    j, i = idx[:, None], idx[None, :]
    for n, m in enumerate(LEVELS):
        t[:, C_MSK + n * P:C_MSK + (n + 1) * P] = (
            (j // (2 * m) == i // (2 * m)) & (j % (2 * m) < m) & (i % (2 * m) >= m))
    n = len(LEVELS)
    t[:, C_MSK + n * P:C_MSK + (n + 1) * P] = np.eye(P)
    return t


def kernel(**inputs):
    import numpy as _np
    import concourse.bacc as _bacc
    from concourse import mybir as _mybir
    from concourse.bass_utils import run_bass_kernel_spmd as _run

    x = {k: _np.asarray(v) for k, v in inputs.items()}

    def tiles(w):
        n = w.shape[1] // P
        return w.reshape(KT, P, n, P).transpose(2, 1, 0, 3).reshape(n, P, D)

    def columns(v):
        return v.reshape(-1, P).T

    w_in = x["w_in"][0]
    starts = _np.cumsum([0, D, D, D, D // 2, D // 2, D, RANK, D, D, D])
    dq, dk, dv, gq, gk, gv, glr, gr, ga, gb = [w_in[:, a:b] for a, b in zip(starts[:-1], starts[1:])]
    w_all = _np.concatenate([tiles(w) for w in (dq, dk, dv, gq, gk, gv, gr, ga, gb, x["w_branch_a"][0],
                                                x["w_branch_b"][0], x["w_out"][0], x["peer_w_q"][0])])
    frames = _np.concatenate([x["x_prompt"][0], x["x_sample"][0]])
    qk = x["qk_norm_g"][0]
    lam = _np.zeros((P, 4), _np.float32)
    lam[:HD] = x["da_lambda"][0].T
    gains = _np.concatenate([
        columns(x["norm1_g"][0]), columns(x["norm2_g"][0]),
        _np.tile(_np.concatenate([qk[0], qk[0]])[:, None], (1, 8)),
        _np.tile(_np.concatenate([qk[1], qk[1]])[:, None], (1, 8)),
        columns(x["da_subln_g"][0]), columns(x["gla_norm_g"][0]), columns(x["gla_b_gate"][0]), lam], axis=1)
    arrays = {
        "xT": frames.T.reshape(KT, P, TOK).transpose(1, 0, 2).reshape(P, KT * TOK),
        "w_all": w_all,
        "gains": gains,
        "const": const_table(),
        "w_glr": glr.reshape(KT, P, RANK).transpose(1, 0, 2).reshape(P, KT * RANK),
        "w_gate": x["gla_w_gate2"][0],
        "ckT": x["cache_k"][0, 0].reshape(PAST, NH, P).transpose(2, 1, 0),
        "cv": x["cache_v"][0, 0].reshape(2, P, NH, P).transpose(1, 2, 0, 3).reshape(P, NH, PAST),
        "state_in": x["state_gla"][0, 0].transpose(1, 0, 2),
        "skT": x["peer_sub_keys"][0].reshape(2 * PH, N_KEYS, P).transpose(2, 0, 1).reshape(P, 2 * PH * N_KEYS),
        "u": x["peer_u"][0].reshape(N_KEYS, N_KEYS, KT, P).transpose(0, 3, 2, 1).reshape(N_KEYS, P, D),
        "v": x["peer_v"][0].reshape(N_KEYS, N_KEYS, D),
    }
    arrays = {k: _np.ascontiguousarray(v) for k, v in arrays.items()}

    nc = _bacc.Bacc("TRN2", target_bir_lowering=False, num_devices=1)
    A = {}
    for name, a in arrays.items():
        A[name] = nc.dram_tensor("in_" + name, a.shape, _mybir.dt.from_np(a.dtype), kind="ExternalInput").ap()
    for name in ("w_all", "u", "v"):
        A[name] = A[name].rearrange("t p n -> p t n")
    outs = {"kT_out": (D, TOK), "vT_out": (D, TOK), "yT_out": (D, TOK), "s_out": (2 * GH, P, 256)}
    for name, shape in outs.items():
        ap = nc.dram_tensor("out_" + name, shape, _mybir.dt.float32, kind="ExternalOutput").ap()
        A[name] = (ap.rearrange("h p n -> p h n") if name == "s_out"
                            else ap.rearrange("(k p) n -> p k n", p=P))
    gate = nc.dram_tensor("gate_by_expert", (N_KEYS, N_KEYS, TOK), _mybir.dt.float32, kind="Internal").ap()
    A["gate"] = gate.rearrange("i j t -> j i t")
    build(nc, A)
    r = _run(nc, [{"in_" + k: v for k, v in arrays.items()}], core_ids=[0]).results[0]

    def by_frame(name, *shape):
        rows = _np.asarray(r["out_" + name]).T
        return rows[:SEQ].reshape(*shape[0]), rows[SEQ:].reshape(*shape[1])

    y_p, y_s = by_frame("yT_out", (1, SEQ, D), (1, DEC, D))
    k_p, k_s = by_frame("kT_out", (1, 1, SEQ, NH, 2, HD), (1, 1, DEC, NH, 2, HD))
    v_p, v_s = by_frame("vT_out", (1, 1, SEQ, NH, P), (1, 1, DEC, NH, P))
    s = _np.asarray(r["out_s_out"]).reshape(2, 1, 1, GH, P, 256)
    return y_p, y_s, k_p, v_p, s[0], k_s, v_s, s[1]
```

```python
from contextlib import ExitStack

import numpy as np

import concourse.bass as bass
from concourse import mybir

F32 = mybir.dt.float32
F32R = mybir.dt.float32r
U32 = mybir.dt.uint32
ALU = mybir.AluOpType
ACT = mybir.ActivationFunctionType
AX = mybir.AxisListType

P = 128
D = 1024
KT = D // P
SEQ = 512
DEC = 64
PAST = 256
TOK = SEQ + DEC
HALF = TOK // 2
NC_T = 5
NH = 8
HD = 64
GH = 4
EPS = 1e-6
NEG = -1e30
RANK = 16
LEVELS = [64, 32, 16, 8, 4, 2, 1]
CHUNK_TOK = 64
N_KEYS = 128
TOPK = 16
ROUTE_U = 6
EARLY = 72
CLOSING = 6
PH = 8
LAM_INIT = 0.2

T_Q, T_K, T_V, T_GQ, T_GK, T_GV, T_GR = 0, 8, 16, 24, 28, 32, 40
T_GA, T_GB, T_WA, T_WB, T_WO, T_PQ, T_END = 48, 56, 64, 72, 80, 88, 104

C_ID, C_BLK, C_ROT, C_IOTA, C_COS, C_SIN, C_RST, C_MSK = 0, 128, 256, 384, 512, 1088, 1664, 2240
N_MASK = len(LEVELS) + 1
C_END = C_MSK + N_MASK * P
G_N1, G_N2, G_QK, G_SUB, G_GLA, G_BG, G_LAM, G_END = 0, 8, 16, 32, 33, 35, 39, 43


def token_cols(c):
    return c * P, (P if c < 4 else DEC)


def bcast(ap, axis, n):
    ap = ap.unsqueeze(axis)
    shape = list(ap.shape)
    shape[axis] = n
    return ap.to_broadcast(shape)


def apart(eng, S):
    eng.sem_inc(S["passed"], 1)


def load_w(sp, S, i, c):
    t = 2 * i + c
    if not (isinstance(t, int) and t < 2):
        sp.wait_ge(S["w_split"], t - 1)
    sp.dma_start(S["w_raw"][:, c % 2, :], S["w_all"][:, bass.ds(t, 1), :]).then_inc(S["w_loaded"][c % 2], 16)


def split_hi(nc, act, S, i, c):
    u, t = c % 2, 2 * i + c
    act.wait_ge(S["w_loaded"][u], 16 * (i + c // 2 + 1))
    if not (isinstance(t, int) and t < 2):
        act.wait_ge(S["tile_done"], t - 1)
    nc.scalar.activation(S["w_hi"][:, u, :], S["w_raw"][:, u, :], ACT.Copy).then_inc(S["w_hi_done"], 1)


def split_lo(nc, dve, S, i, c):
    u, t = c % 2, 2 * i + c
    dve.wait_ge(S["w_hi_done"], t + 1)
    nc.vector.tensor_tensor(S["w_lo"][:, u, :], S["w_raw"][:, u, :], S["w_hi"][:, u, :].bitcast(F32),
                            ALU.subtract).then_inc(S["w_split"], 1)


def product3(nc, out, wh, wl, xh, xl, first, last):
    nc.tensor.matmul(out, wh, xh, start=first, stop=False)
    nc.tensor.matmul(out, wh, xl, start=False, stop=False)
    return nc.tensor.matmul(out, wl, xh, start=False, stop=last)


def dense_tile(nc, pe, S, i, c):
    u, t = c % 2, 2 * i + c
    pe.wait_ge(S["w_split"], t + 1)
    if not (isinstance(t, int) and t < 2):
        pe.wait_ge(S["evacuated"], t - 1)
    for f in range(2):
        cols = slice(f * HALF, (f + 1) * HALF)
        for k in range(KT):
            w = slice(k * P, (k + 1) * P)
            ins = product3(nc, S["mm"][u][:, f, 0:HALF], S["w_hi"][:, u, w], S["w_lo"][:, u, w],
                           S["x_hi"][:, k, cols], S["x_lo"][:, k, cols], k == 0, k == KT - 1)
    ins.then_inc(S["tile_done"], 1)


def halves(ap):
    return ap.rearrange("p (f n) -> p f n", f=2)


def feat(S, j):
    return S["big"][:, bass.ds(j * TOK, TOK)]


def split_activation_hi(nc, act, S, src, ready, count):
    act.wait_ge(ready, count)
    nc.scalar.activation(S["x_hi"][:, :, :], src, ACT.Copy).then_inc(S["x_hi_done"], 1)


def split_activation_lo(nc, dve, S, src, count):
    dve.wait_ge(S["x_hi_done"], count)
    nc.vector.tensor_tensor(S["x_lo"][:, :, :], src, S["x_hi"][:, :, :].bitcast(F32),
                            ALU.subtract).then_inc(S["x_split"], 1)


def matmul_tok(nc, out, lhsT, rhs, first, last):
    nc.tensor.matmul(out[:, 0, 0:HALF], lhsT, rhs[:, 0:HALF], start=first, stop=last)
    return nc.tensor.matmul(out[:, 1, 0:HALF], lhsT, rhs[:, HALF:TOK], start=first, stop=last)


def as3(ap):
    return ap.rearrange("p (k n) -> p k n", n=TOK)


def rms_squares(nc, act, S, ready, count):
    act.wait_ge(ready, count)
    nc.scalar.activation(S["big"][:, 0:KT * TOK], S["res"][:, :], ACT.Square).then_inc(S["n_sq"], 1)


def rms_sum(nc, pe, S, r):
    pe.wait_ge(S["n_sq"], r + 1)
    for k in range(KT):
        ins = matmul_tok(nc, S["aux"], S["ones"][:, :], S["big"][:, k * TOK:(k + 1) * TOK], k == 0, k == KT - 1)
    ins.then_inc(S["n_sum"], 1)


def rms_root(nc, act, S, r):
    act.wait_ge(S["n_sum"], r + 1)
    nc.scalar.activation(halves(S["root"][:, :]), S["aux"][:, :, 0:HALF], ACT.Sqrt, bias=S["eps"][:, 0:1],
                         scale=1.0 / D).then_inc(S["n_root"], 1)


def rms_apply(nc, dve, S, r, gain):
    dve.wait_ge(S["n_root"], r + 1)
    nc.vector.reciprocal(S["rinv"][:, :], S["root"][:, :]).then_inc(S["n_rinv"], 1)
    dve.wait_ge(S["n_rinv"], r + 1)
    for k in range(KT):
        ins = nc.vector.scalar_tensor_tensor(
            out=S["big"][:, (8 + k) * TOK:(9 + k) * TOK], in0=S["res"][:, k * TOK:(k + 1) * TOK],
            scalar=S["gains"][:, gain + k:gain + k + 1], in1=S["rinv"][:, :], op0=ALU.mult, op1=ALU.mult)
    ins.then_inc(S["n_done"], 1)


FROM_ONE = {
    "tensor": "a_turned a_pv g_at g_kT g_o g_osum t_turned e_mm e_mm y_mm",
    "scalar": "a_exp a_wT g_root o_root t_tab e_out e_out u_gel u_gel",
    "vector": "a_w g_fin g_gated g_oc o_done o_evac q_roped q_rsin r_top t_ij y_add y_add",
    "gpsimd": "r_kept",
    "sync": "g_out",
}


def start_at_one(eng, S, engine):
    for name in FROM_ONE[engine].split():
        eng.sem_inc(S[name], 1)


def stage_norm1(nc, S, A):
    with nc.Block() as block:
        @block.sync
        def _(sp):
            sp.dma_start(S["res"][:, :], A["xT"]).then_inc(S["x_in"], 16)
            start_at_one(sp, S, "sync")
            for store in S["e_store"] + S["h_out"]:
                sp.sem_inc(store, 1)
            for dst, src in ((S["gains"][:, :], A["gains"]), (S["const"][:, :], A["const"]),
                             (S["w_glr"][:, :], A["w_glr"]), (S["w_gate"][0:RANK, :], A["w_gate"])):
                sp.dma_start(dst, src).then_inc(S["c_in"], 16)
            load_w(sp, S, 0, 0)
            load_w(sp, S, 0, 1)
            load_w(sp, S, 0, 2)

        @block.scalar
        def _(act):
            start_at_one(act, S, "scalar")
            rms_squares(nc, act, S, S["x_in"], 16)
            rms_root(nc, act, S, 0)
            split_hi(nc, act, S, 0, 0)
            split_activation_hi(nc, act, S, as3(S["big"][:, 8 * TOK:16 * TOK]), S["n_done"], 1)
            act.wait_ge(S["lam_sum"], 1)
            nc.scalar.activation(S["lam"][:, 2:4], S["aux2"][:, 0, 0:2], ACT.Exp).then_inc(S["lam_exp"], 1)
            act.wait_ge(S["glr_mm"], 1)
            nc.scalar.activation(halves(S["glr"][0:RANK, :]), S["mm"][0][0:RANK, :, 0:HALF],
                                 ACT.Copy).then_inc(S["glr_done"], 1)

        @block.vector
        def _(dve):
            start_at_one(dve, S, "vector")
            nc.vector.memset(S["ones"][:, :], 1.0).then_inc(S["d_init"], 1)
            nc.vector.memset(S["eps"][:, :], EPS).then_inc(S["d_init"], 1)
            dve.wait_ge(S["c_in"], 64)
            nc.vector.tensor_tensor(S["lam"][0:HD, 0:1], S["gains"][0:HD, G_LAM:G_LAM + 1],
                                    S["gains"][0:HD, G_LAM + 1:G_LAM + 2], ALU.mult).then_inc(S["d_init"], 1)
            nc.vector.tensor_tensor(S["lam"][0:HD, 1:2], S["gains"][0:HD, G_LAM + 2:G_LAM + 3],
                                    S["gains"][0:HD, G_LAM + 3:G_LAM + 4], ALU.mult).then_inc(S["d_init"], 1)
            nc.vector.tensor_scalar(S["gqk"][:, 0:8], S["gains"][:, G_QK:G_QK + 8], HD ** -0.5, None,
                                    ALU.mult).then_inc(S["d_init"], 1)
            nc.vector.tensor_copy(S["gqk"][:, 8:16], S["gains"][:, G_QK + 8:G_QK + 16]).then_inc(S["d_init"], 1)
            nc.vector.tensor_scalar(S["gsub"][:, :], S["gains"][:, G_SUB:G_SUB + 1], 1.0 - LAM_INIT, None,
                                    ALU.mult).then_inc(S["d_init"], 1)
            split_lo(nc, dve, S, 0, 0)
            rms_apply(nc, dve, S, 0, G_N1)
            split_activation_lo(nc, dve, S, as3(S["big"][:, 8 * TOK:16 * TOK]), 1)
            dve.wait_ge(S["lam_exp"], 1)
            nc.vector.tensor_tensor(S["lam"][:, 4:5], S["lam"][:, 3:4], S["lam"][:, 2:3],
                                    ALU.subtract).then_inc(S["lam_d"], 1)
            dve.wait_ge(S["lam_d"], 1)
            nc.vector.tensor_scalar(S["neglam"][:, :], S["lam"][:, 4:5], LAM_INIT, None,
                                    ALU.subtract).then_inc(S["lam_d"], 1)

        @block.gpsimd
        def _(pool):
            start_at_one(pool, S, "gpsimd")

        @block.tensor
        def _(pe):
            start_at_one(pe, S, "tensor")
            pe.wait_ge(S["d_init"], 7)
            rms_sum(nc, pe, S, 0)
            nc.tensor.matmul(S["aux2"][:, 0, 0:2], S["ones"][0:HD, :], S["lam"][0:HD, 0:2], start=True,
                             stop=True).then_inc(S["lam_sum"], 1)
            pe.wait_ge(S["n_done"], 1)
            for k in range(KT):
                ins = matmul_tok(nc, S["mm"][0][0:RANK], S["w_glr"][:, k * RANK:(k + 1) * RANK],
                                 S["big"][:, (8 + k) * TOK:(9 + k) * TOK], k == 0, k == KT - 1)
            ins.then_inc(S["glr_mm"], 1)


def stage_qkv(nc, S, A):
    with nc.Block() as block:
        @block.sync
        def _(sp):
            with sp.Fori(0, 12) as i:
                load_w(sp, S, i, 3)
                load_w(sp, S, i, 4)

        def hi_square_root(act, i, u, square=True, root=True):
            t = 2 * i + u
            split_hi(nc, act, S, i, u + 1)
            if square:
                act.wait_ge(S["evacuated"], t + 1)
                if not isinstance(t, int):
                    act.wait_ge(S["q_sum"], t - 1)
                nc.scalar.activation(S["sq"][:, u, :], feat(S, t), ACT.Square).then_inc(S["q_sq"], 1)
            if root:
                act.wait_ge(S["q_sum"], t)
                if not (isinstance(t, int) and t < 2):
                    act.wait_ge(S["q_norm"], t - 1)
                nc.scalar.activation(halves(S["root"][:, :]), S["aux"][:, :, 0:HALF], ACT.Sqrt,
                                     bias=S["eps"][:, 0:1], scale=1.0 / HD).then_inc(S["q_root"], 1)

        @block.scalar
        def _(act):
            hi_square_root(act, 0, 0, root=False)
            hi_square_root(act, 0, 1)
            with act.Fori(1, 8) as i:
                hi_square_root(act, i, 0)
                hi_square_root(act, i, 1)
            hi_square_root(act, 8, 0, square=False)
            hi_square_root(act, 8, 1, square=False, root=False)
            with act.Fori(9, 12) as i:
                split_hi(nc, act, S, i, 1)
                split_hi(nc, act, S, i, 2)

        def evacuate(dve, i, u):
            t = 2 * i + u
            split_lo(nc, dve, S, i, u + 1)
            dve.wait_ge(S["tile_done"], t + 1)
            nc.vector.tensor_copy(halves(feat(S, t)), S["mm"][u][:, :, 0:HALF]).then_inc(S["evacuated"], 1)

        def norm(dve, i, u):
            n = 2 * i + u
            dve.wait_ge(S["q_root"], n + 1)
            dve.wait_ge(S["q_norm"], n)
            nc.vector.reciprocal(S["rinv"][:, :], S["root"][:, :]).then_inc(S["q_rinv"], 1)
            dve.wait_ge(S["q_rinv"], n + 1)
            nc.vector.scalar_tensor_tensor(out=S["nq"][:, u, :], in0=feat(S, n), scalar=S["gqk"][:, bass.ds(n, 1)],
                                           in1=S["rinv"][:, :], op0=ALU.mult,
                                           op1=ALU.mult).then_inc(S["q_norm"], 1)

        def rotate(dve, i, u):
            n = 2 * i + u
            dve.wait_ge(S["q_swap"], n + 1)
            dve.wait_ge(S["q_roped"], 1 + n)
            nc.vector.tensor_tensor(halves(S["rsin"][:, :]), S["aux2"][:, :, 0:HALF],
                                    halves(S["const"][:, C_SIN:C_SIN + TOK]), ALU.mult).then_inc(S["q_rsin"], 1)
            dve.wait_ge(S["q_rsin"], 1 + n + 1)
            dve.wait_ge(S["q_cos"], n + 1)
            nc.vector.tensor_tensor(feat(S, n), S["rsin"][:, :], S["ncos"][:, u, :],
                                    ALU.add).then_inc(S["q_roped"], 1)

        @block.vector
        def _(dve):
            evacuate(dve, 0, 0)
            evacuate(dve, 0, 1)
            norm(dve, 0, 0)
            with dve.Fori(1, 8) as i:
                evacuate(dve, i, 0)
                norm(dve, i - 1, 1)
                rotate(dve, i - 1, 0)
                evacuate(dve, i, 1)
                norm(dve, i, 0)
                rotate(dve, i - 1, 1)
            evacuate(dve, 8, 0)
            norm(dve, 7, 1)
            rotate(dve, 7, 0)
            evacuate(dve, 8, 1)
            rotate(dve, 7, 1)
            with dve.Fori(9, 12) as i:
                evacuate(dve, i, 0)
                evacuate(dve, i, 1)

        @block.gpsimd
        def _(pool):
            def ncos(i, u):
                n = 2 * i + u
                pool.wait_ge(S["q_norm"], n + 1)
                if not isinstance(n, int):
                    pool.wait_ge(S["q_roped"], 1 + n - 1)
                    apart(pool, S)
                nc.gpsimd.tensor_tensor(S["ncos"][:, u, :], S["nq"][:, u, :], S["const"][:, C_COS:C_COS + TOK],
                                        ALU.mult).then_inc(S["q_cos"], 1)
            ncos(0, 0)
            ncos(0, 1)
            with pool.Fori(1, 8) as i:
                ncos(i, 0)
                ncos(i, 1)

        def head_sum(pe, i, u):
            n = 2 * i + u
            pe.wait_ge(S["q_sq"], n + 1)
            if not (isinstance(n, int) and n < 1):
                pe.wait_ge(S["q_root"], n)
            matmul_tok(nc, S["aux"], S["const"][:, C_BLK:C_BLK + P], S["sq"][:, u, :], True, True).then_inc(S["q_sum"], 1)

        def swap(pe, i, u):
            n = 2 * i + u
            pe.wait_ge(S["q_norm"], n + 1)
            if not (isinstance(n, int) and n < 1):
                pe.wait_ge(S["q_rsin"], 1 + n)
            matmul_tok(nc, S["aux2"], S["const"][:, C_ROT:C_ROT + P], S["nq"][:, u, :], True, True).then_inc(S["q_swap"], 1)

        @block.tensor
        def _(pe):
            pe.wait_ge(S["x_split"], 1)
            dense_tile(nc, pe, S, 0, 0)
            dense_tile(nc, pe, S, 0, 1)
            head_sum(pe, 0, 0)
            with pe.Fori(1, 8) as i:
                dense_tile(nc, pe, S, i, 0)
                head_sum(pe, i - 1, 1)
                swap(pe, i - 1, 0)
                dense_tile(nc, pe, S, i, 1)
                head_sum(pe, i, 0)
                swap(pe, i - 1, 1)
            dense_tile(nc, pe, S, 8, 0)
            head_sum(pe, 7, 1)
            swap(pe, 7, 0)
            dense_tile(nc, pe, S, 8, 1)
            swap(pe, 7, 1)
            with pe.Fori(9, 12) as i:
                dense_tile(nc, pe, S, i, 0)
                dense_tile(nc, pe, S, i, 1)


def stage_attention(nc, S, A, B):
    keys = [P * (j + 1) for j in range(4)] + [PAST + DEC]

    with nc.Block() as block:
        @block.sync
        def _(sp):
            sp.dma_start(A["kT_out"], as3(S["big"][:, 8 * TOK:16 * TOK])).then_inc(S["out_kv"], 16)
            sp.dma_start(A["vT_out"], as3(S["big"][:, 16 * TOK:24 * TOK])).then_inc(S["out_kv"], 16)
            def cache(i, u):
                h = 2 * i + u
                if not isinstance(h, int):
                    sp.wait_ge(S["a_pv"], 1 + 5 * (h - 1))
                sp.dma_start(B["ck"][:, u, :], A["ckT"][:, bass.ds(h, 1), :]).then_inc(S["a_cache"][u], 16)
                sp.dma_start(B["cv"][:, u, :], A["cv"][:, bass.ds(h, 1), :]).then_inc(S["a_cache"][u], 16)
            cache(0, 0)
            cache(0, 1)
            with sp.Fori(1, 4) as i:
                cache(i, 0)
                cache(i, 1)

        @block.gpsimd
        def _(pool):
            def stage(i, u):
                h = 2 * i + u
                if not isinstance(h, int):
                    pool.wait_ge(S["a_pv"], 1 + 5 * (h - 1))
                    apart(pool, S)
                for dst, j in ((B["qs"], 0), (B["ks"], 8), (B["vs"], 16)):
                    nc.gpsimd.tensor_copy(dst[:, u, :], feat(S, h + j)).then_inc(S["a_staged"], 1)
            stage(0, 0)
            stage(0, 1)
            with pool.Fori(1, 4) as i:
                stage(i, 0)
                stage(i, 1)

        @block.tensor
        def _(pe):
            def scores(i, u, j):
                h = 2 * i + u
                if j == 0:
                    pe.wait_ge(S["a_staged"], 3 * (h + 1))
                    pe.wait_ge(S["a_exp"], 1 + 5 * h)
                elif j == 1:
                    pe.wait_ge(S["o_root"], 1 + h)
                else:
                    pe.wait_ge(S["a_exp"], 1 + 5 * h + j - 1)
                apart(pe, S)
                q0, nq = token_cols(j)
                for m in range(2):
                    rows = slice(HD * m, HD * (m + 1))
                    q = B["qs"][rows, u, q0:q0 + nq]
                    out = B["s"][j % 2][0:nq, m]
                    if j < 4:
                        ins = nc.tensor.matmul(out[:, 0:keys[j]], q, B["ks"][rows, u, 0:keys[j]],
                                               start=True, stop=True)
                    else:
                        pe.wait_ge(S["a_cache"][u], 32 * (i + 1))
                        apart(pe, S)
                        nc.tensor.matmul(out[:, 0:PAST], q, B["ck"][rows, u, :], start=True, stop=True)
                        ins = nc.tensor.matmul(out[:, PAST:PAST + DEC], q, B["ks"][rows, u, SEQ:TOK],
                                               start=True, stop=True)
                ins.then_inc(S["a_scores"], 1)

            def turn_v(i, u):
                h = 2 * i + u
                pe.wait_ge(S["a_wT"], 1 + 5 * h)
                for c in range(NC_T):
                    t0, n = token_cols(c)
                    out = B["tr"][0][:, t0:t0 + P] if c < 4 else B["tr"][1][0:DEC, 0:P]
                    ins = nc.tensor.transpose(out, B["vs"][:, u, t0:t0 + n], S["ident"])
                ins.then_inc(S["a_vT"], 1)

            def turn_w(i, u, j):
                h = 2 * i + u
                pe.wait_ge(S["a_w"], 1 + 5 * h + j + 1)
                if j < 2:
                    pe.wait_ge(S["a_vtok"], 2 * (h + 1))
                else:
                    pe.wait_ge(S["a_wT"], 1 + 5 * h + j - 1)
                apart(pe, S)
                nq = token_cols(j)[1]
                for k in range((keys[j] + P - 1) // P):
                    nk = min(P, keys[j] - k * P)
                    ins = nc.tensor.transpose(B["tr"][j % 2][0:nk, k * nq:(k + 1) * nq],
                                              B["w"][0:nq, j % 2, k * P:k * P + nk], S["ident"][0:nq, 0:nq])
                ins.then_inc(S["a_turned"], 1)

            def times_v(i, u, j):
                h = 2 * i + u
                pe.wait_ge(S["a_wT"], 1 + 5 * h + j + 1)
                if j == 0:
                    pe.wait_ge(S["a_vtok"], 2 * (h + 1))
                    pe.wait_ge(S["o_evac"], 1 + h)
                nq = token_cols(j)[1]
                n_k = (keys[j] + P - 1) // P
                for k in range(n_k):
                    w = B["wT"][:, j % 2, k * nq:(k + 1) * nq]
                    if j < 4:
                        out, v = B["o"][:, 0, j * P:(j + 1) * P], B["vtok"][:, u, k * P:(k + 1) * P]
                    else:
                        out = B["o"][:, 1, 0:DEC]
                        v = B["cv"][:, u, k * P:(k + 1) * P] if k < 2 else B["vtok"][0:DEC, u, SEQ:SEQ + P]
                        w = w if k < 2 else w[0:DEC]
                    ins = nc.tensor.matmul(out, v, w, start=k == 0, stop=k == n_k - 1)
                ins.then_inc(S["a_pv"], 1)

            with pe.Fori(0, 4) as i:
                for u in range(2):
                    scores(i, u, 0)
                    turn_v(i, u)
                    for j in range(5):
                        if j < 4:
                            scores(i, u, j + 1)
                        turn_w(i, u, j)
                        times_v(i, u, j)
                    pe.wait_ge(S["o_sq"], 2 * i + u + 1)
                    nc.tensor.matmul(B["s"][1][:, 0, :], S["ones"][:, :], B["osq"][:, 0:SEQ], start=True, stop=True)
                    nc.tensor.matmul(B["s"][1][:, 1, 0:DEC], S["ones"][:, :], B["osq"][:, SEQ:TOK], start=True,
                                     stop=True).then_inc(S["o_sum"], 1)

        @block.scalar
        def _(act):
            def exps(i, u, j):
                n = 5 * (2 * i + u) + j
                act.wait_ge(S["a_max"], n + 1)
                nq = token_cols(j)[1]
                act.wait_ge(S["a_w"], 1 + (n - j if j < 2 else n - 1))
                for m in range(2):
                    ins = nc.scalar.activation(B["p"][0:nq, j % 2, m, 0:keys[j]], B["s"][j % 2][0:nq, m, 0:keys[j]],
                                               ACT.Exp, bias=B["nmax"][0:nq, j % 2, m:m + 1],
                                               accum_out=B["z"][0:nq, j % 2, m:m + 1])
                ins.then_inc(S["a_exp"], 1)

            def evac_wT(i, u, j):
                n = 5 * (2 * i + u) + j
                act.wait_ge(S["a_turned"], 1 + n + 1)
                act.wait_ge(S["a_pv"], 1 + (n - j if j < 2 else n - 1))
                if j < 4:
                    nc.scalar.activation(B["wT"][:, j % 2, 0:keys[j]], B["tr"][j % 2][:, 0:keys[j]],
                                         ACT.Copy).then_inc(S["a_wT"], 1)
                else:
                    nc.scalar.activation(B["wT"][:, 0, 0:2 * DEC], B["tr"][0][:, 0:2 * DEC], ACT.Copy)
                    nc.scalar.activation(B["wT"][0:DEC, 0, 2 * DEC:3 * DEC], B["tr"][0][0:DEC, 2 * DEC:3 * DEC],
                                         ACT.Copy).then_inc(S["a_wT"], 1)

            with act.Fori(0, 4) as i:
                for u in range(2):
                    h = 2 * i + u
                    exps(i, u, 0)
                    act.wait_ge(S["a_vT"], h + 1)
                    nc.scalar.activation(B["vtok"][:, u, 0:SEQ], B["tr"][0][:, :], ACT.Copy).then_inc(S["a_vtok"], 1)
                    nc.scalar.activation(B["vtok"][0:DEC, u, SEQ:SEQ + P], B["tr"][1][0:DEC, 0:P],
                                         ACT.Copy).then_inc(S["a_vtok"], 1)
                    for j in range(5):
                        if j < 4:
                            exps(i, u, j + 1)
                        evac_wT(i, u, j)
                    act.wait_ge(S["o_evac"], 1 + h + 1)
                    nc.scalar.activation(B["osq"][:, :], B["osb"][:, :], ACT.Square).then_inc(S["o_sq"], 1)
                    act.wait_ge(S["o_sum"], h + 1)
                    nc.scalar.activation(S["root"][:, 0:SEQ], B["s"][1][:, 0, :], ACT.Sqrt, bias=S["eps"][:, 0:1],
                                         scale=1.0 / P)
                    nc.scalar.activation(S["root"][:, SEQ:TOK], B["s"][1][:, 1, 0:DEC], ACT.Sqrt,
                                         bias=S["eps"][:, 0:1], scale=1.0 / P).then_inc(S["o_root"], 1)

        @block.vector
        def _(dve):
            def neg_max(i, u, j):
                n = 5 * (2 * i + u) + j
                dve.wait_ge(S["a_scores"], n + 1)
                nq = token_cols(j)[1]
                if j < 4:
                    nc.vector.memset(B["s"][j % 2][0:HD, :, P * j + HD:P * (j + 1)], NEG).then_inc(S["a_mask"], 1)
                    dve.wait_ge(S["a_mask"], 4 * (2 * i + u) + j + 1)
                nc.vector.tensor_reduce(B["nmax"][0:nq, j % 2, :], B["s"][j % 2][0:nq, :, 0:keys[j]], AX.X, ALU.max,
                                        negate=True).then_inc(S["a_max"], 1)

            def weights(i, u, j):
                n = 5 * (2 * i + u) + j
                nq = token_cols(j)[1]
                dve.wait_ge(S["a_exp"], 1 + n + 1)
                dve.wait_ge(S["a_w"], 1 + (n - j if j < 2 else n - 1))
                nc.vector.reciprocal(B["rz"][0:nq, j % 2, :], B["z"][0:nq, j % 2, :]).then_inc(S["a_rz"], 1)
                dve.wait_ge(S["a_rz"], 2 * n + 1)
                nc.vector.tensor_scalar(B["rz2"][0:nq, j % 2, 0:1], B["rz"][0:nq, j % 2, 1:2], S["neglam"][0:nq, 0:1], None,
                                        ALU.mult).then_inc(S["a_rz"], 1)
                dve.wait_ge(S["a_turned"], 1 + (n - j if j < 2 else n - 1))
                k = slice(0, keys[j])
                nc.vector.tensor_scalar(B["w"][0:nq, j % 2, k], B["p"][0:nq, j % 2, 0, k], B["rz"][0:nq, j % 2, 0:1], None,
                                        ALU.mult).then_inc(S["a_w1"], 1)
                dve.wait_ge(S["a_rz"], 2 * n + 2)
                dve.wait_ge(S["a_w1"], n + 1)
                nc.vector.scalar_tensor_tensor(out=B["w"][0:nq, j % 2, k], in0=B["p"][0:nq, j % 2, 1, k],
                                               scalar=B["rz2"][0:nq, j % 2, 0:1], in1=B["w"][0:nq, j % 2, k],
                                               op0=ALU.mult, op1=ALU.add).then_inc(S["a_w"], 1)

            with dve.Fori(0, 4) as i:
                for u in range(2):
                    h = 2 * i + u
                    neg_max(i, u, 0)
                    for j in range(5):
                        if j < 4:
                            neg_max(i, u, j + 1)
                        weights(i, u, j)
                    dve.wait_ge(S["a_pv"], 1 + 5 * (h + 1))
                    dve.wait_ge(S["o_done"], 1 + h)
                    nc.vector.tensor_copy(B["osb"][:, 0:SEQ], B["o"][:, 0, :])
                    nc.vector.tensor_copy(B["osb"][:, SEQ:TOK], B["o"][:, 1, 0:DEC]).then_inc(S["o_evac"], 1)
                    dve.wait_ge(S["o_root"], 1 + h + 1)
                    nc.vector.reciprocal(S["rinv"][:, :], S["root"][:, :]).then_inc(S["o_rinv"], 1)
                    dve.wait_ge(S["o_rinv"], h + 1)
                    nc.vector.scalar_tensor_tensor(out=S["res"][:, bass.ds(h * TOK, TOK)], in0=B["osb"][:, :],
                                                   scalar=S["gsub"][:, 0:1], in1=S["rinv"][:, :],
                                                   op0=ALU.mult, op1=ALU.mult).then_inc(S["o_done"], 1)


def stage_gla_inputs(nc, S, A):
    with nc.Block() as block:
        @block.sync
        def _(sp):
            with sp.Fori(T_GQ // 2, T_GA // 2) as i:
                load_w(sp, S, i, 3)
                load_w(sp, S, i, 4)

        @block.scalar
        def _(act):
            with act.Fori(T_GQ // 2, T_GR // 2) as i:
                split_hi(nc, act, S, i, 1)
                split_hi(nc, act, S, i, 2)
            with act.Fori(T_GR // 2, T_GA // 2) as i:
                for u in range(2):
                    split_hi(nc, act, S, i, u + 1)
                    act.wait_ge(S["tile_done"], 2 * i + u + 1)
                    nc.scalar.activation(halves(feat(S, 2 * i + u - T_GQ)), S["mm"][u][:, :, 0:HALF],
                                         ACT.Silu).then_inc(S["evacuated"], 1)

        @block.vector
        def _(dve):
            with dve.Fori(T_GQ // 2, T_GR // 2) as i:
                for u in range(2):
                    split_lo(nc, dve, S, i, u + 1)
                    dve.wait_ge(S["tile_done"], 2 * i + u + 1)
                    nc.vector.tensor_copy(halves(feat(S, 2 * i + u - T_GQ)),
                                          S["mm"][u][:, :, 0:HALF]).then_inc(S["evacuated"], 1)
            with dve.Fori(T_GR // 2, T_GA // 2) as i:
                split_lo(nc, dve, S, i, 1)
                split_lo(nc, dve, S, i, 2)

        @block.tensor
        def _(pe):
            for a, b in ((T_GQ, T_GR), (T_GR, T_GA)):
                pe.wait_ge(S["evacuated"], a)
                with pe.Fori(a // 2, b // 2) as i:
                    dense_tile(nc, pe, S, i, 0)
                    dense_tile(nc, pe, S, i, 1)


def stage_gla(nc, S, A, G):
    dk_scale = float(P) ** -0.5
    tau = 1.0 / 16.0
    n_lv = len(LEVELS)

    with nc.Block() as block:
        @block.sync
        def _(sp):
            with sp.Fori(0, GH) as h:
                sp.wait_ge(S["g_o"], 1 + 2 * h)
                apart(sp, S)
                sp.wait_ge(S["g_fin"], 1 + h)
                apart(sp, S)
                sp.dma_start(G["st"][:, 4, :], A["state_in"][:, bass.ds(h, 1), :]).then_inc(S["g_state"], 16)
                sp.wait_ge(S["g_chain"], 4 * h + 4)
                apart(sp, S)
                sp.dma_start(A["s_out"][:, bass.ds(h, 1), :], G["st"][:, 0, :]).then_inc(S["g_out"], 16)
                sp.wait_ge(S["g_fin"], 1 + h + 1)
                apart(sp, S)
                sp.dma_start(A["s_out"][:, bass.ds(h + GH, 1), :], G["s_fin"][:, :]).then_inc(S["g_out"], 16)

        @block.gpsimd
        def _(pool):
            with pool.Fori(0, GH) as h:
                pool.wait_ge(S["g_osum"], 1 + h)
                apart(pool, S)
                for v in range(2):
                    nc.gpsimd.tensor_copy(G["vs"][:, v, :], feat(S, 8 + 2 * h + v)).then_inc(S["g_vs"], 1)
                for n in range(n_lv + 2):
                    s = n % 2
                    w = SEQ if n == 0 else TOK
                    if n != n_lv:
                        pool.wait_ge(S["g_e"], (n_lv + 1) * h + min(n, n_lv) + 1 if n < n_lv else (n_lv + 1) * (h + 1))
                    if n >= 2:
                        pool.wait_ge(S["g_at"], 1 + n_lv * h + h + n - 1)
                    else:
                        pool.wait_ge(S["g_kT"], 1 + h)
                    apart(pool, S)
                    k = S["big"][:, bass.ds((GH + h) * TOK, w)]
                    if n == n_lv:
                        nc.gpsimd.tensor_copy(G["kl"][:, s, 0:w], k).then_inc(S["g_kl"], 1)
                    else:
                        nc.gpsimd.tensor_tensor(G["kl"][:, s, 0:w], k, G["e"][:, s, 0:w], ALU.mult).then_inc(S["g_kl"], 1)

        @block.scalar
        def _(act):
            act.wait_ge(S["g_z"], GH)
            for h in range(GH):
                pb = [S["mm"][0], S["mm"][1], S["aux"], S["aux2"]][h]
                ins = nc.scalar.activation(halves(G["b"][:, h * TOK:(h + 1) * TOK]), pb[:, :, 0:HALF], ACT.Identity,
                                           bias=S["gains"][:, G_BG + h:G_BG + h + 1])
            ins.then_inc(S["g_zb"], 1)
            act.wait_ge(S["g_zb"], 1)
            nc.scalar.activation(G["la"][:, :], G["b"][:, :], ACT.Abs).then_inc(S["g_la"], 1)
            act.wait_ge(S["g_la"], 1)
            nc.scalar.activation(G["la"][:, :], G["la"][:, :], ACT.Exp, scale=-1.0).then_inc(S["g_la"], 1)
            act.wait_ge(S["g_la"], 2)
            nc.scalar.activation(G["la"][:, :], G["la"][:, :], ACT.Ln, bias=1.0).then_inc(S["g_la"], 1)
            with act.Fori(0, GH) as h:
                bh = G["b"][:, bass.ds(h * TOK, TOK)]
                act.wait_ge(S["g_cum"], GH)
                act.wait_ge(S["g_at"], 1 + (n_lv + 1) * h)
                act.wait_ge(S["g_gated"], 1 + 2 * h)
                nc.scalar.activation(G["qb"][:, :], bh, ACT.Exp, scale=tau).then_inc(S["g_eb"], 1)
                bl = G["b"][:, bass.ds(h * TOK, SEQ)].rearrange("p (c n) -> p c n", n=P)[:, :, P - 1]
                nc.scalar.activation(G["el"][:, 0:4], bl, ACT.Exp, scale=tau).then_inc(S["g_eb"], 1)
                nc.scalar.activation(G["el"][:, 4:5], G["b"][:, bass.ds(h * TOK + TOK - 1, 1)], ACT.Exp,
                                     scale=tau).then_inc(S["g_eb"], 1)
                for v in range(2):
                    act.wait_ge(S["g_vT"], 2 * h + v + 1)
                    tr = [S["aux"], S["aux2"]][v]
                    cols = slice(v * P, (v + 1) * P)
                    nc.scalar.activation(G["vt"][:, 0:4, cols], tr[:, 0, :].rearrange("p (c n) -> p c n", n=P),
                                         ACT.Copy).then_inc(S["g_vt"], 1)
                    nc.scalar.activation(G["vt"][0:DEC, 4, cols], tr[0:DEC, 1, 0:P], ACT.Copy).then_inc(S["g_vt"], 1)
                for n in range(n_lv + 1):
                    s = n % 2 if n < n_lv else (n + 1) % 2
                    w = SEQ if n == 0 else TOK
                    act.wait_ge(S["g_d"], (n_lv + 1) * h + n + 1)
                    if n >= 2:
                        act.wait_ge(S["g_kl"], (n_lv + 2) * h + (n - 1 if n < n_lv else n_lv))
                        act.wait_ge(S["g_ql"], (n_lv + 1) * h + (n - 1 if n < n_lv else n_lv))
                    if n < n_lv:
                        nc.scalar.activation(G["e"][:, s, 0:w], G["dd"][:, n % 2, 0:w], ACT.Abs).then_inc(S["g_abs"], 1)
                        act.wait_ge(S["g_abs"], n_lv * h + n + 1)
                        nc.scalar.activation(G["e"][:, s, 0:w], G["e"][:, s, 0:w], ACT.Exp,
                                             scale=-tau).then_inc(S["g_e"], 1)
                    else:
                        nc.scalar.activation(G["e"][:, s, 0:w], G["dd"][:, n % 2, 0:w], ACT.Exp,
                                             scale=tau).then_inc(S["g_e"], 1)
                act.wait_ge(S["g_kT"], 1 + h + 1)
                nc.scalar.activation(G["kt"][:, 0:4, :], S["aux"][:, 0, :].rearrange("p (c n) -> p c n", n=P),
                                     ACT.Copy).then_inc(S["g_kt"], 1)
                nc.scalar.activation(G["kt"][0:DEC, 4, :], S["aux"][0:DEC, 1, 0:P], ACT.Copy).then_inc(S["g_kt"], 1)
                for v in range(2):
                    act.wait_ge(S["g_oc"], 1 + 2 * h + v + 1)
                    nc.scalar.activation(G["osq"][:, v, :], G["oc"][:, v, :], ACT.Square).then_inc(S["g_osq"], 1)
                act.wait_ge(S["g_osum"], 1 + h + 1)
                nc.scalar.activation(halves(S["root"][:, :]), S["aux"][:, :, 0:HALF], ACT.Sqrt, bias=S["eps"][:, 0:1],
                                     scale=1.0 / (2 * P)).then_inc(S["g_root"], 1)

        @block.vector
        def _(dve):
            dve.wait_ge(S["g_la"], 3)
            nc.vector.scalar_tensor_tensor(out=G["la"][:, :], in0=G["b"][:, :], scalar=0.0, in1=G["la"][:, :],
                                           op0=ALU.min, op1=ALU.subtract).then_inc(S["g_ls"], 1)
            dve.wait_ge(S["g_ls"], 1)
            for h in range(GH):
                nc.vector.tensor_tensor_scan(G["b"][:, h * TOK:(h + 1) * TOK], S["const"][:, C_RST:C_RST + TOK],
                                             G["la"][:, h * TOK:(h + 1) * TOK], 0.0, ALU.mult,
                                             ALU.add).then_inc(S["g_cum"], 1)
            with dve.Fori(0, GH) as h:
                q = S["big"][:, bass.ds(h * TOK, TOK)]
                dve.wait_ge(S["g_cum"], GH)
                dve.wait_ge(S["g_osum"], 1 + h)
                dve.wait_ge(S["g_gated"], 1 + 2 * h)
                nc.vector.memset(G["at"][:, :], 0.0).then_inc(S["g_at0"], 1)

                def delta(n):
                    s = n % 2
                    if n == n_lv:
                        dve.wait_ge(S["g_e"], (n_lv + 1) * h + n - 1)
                        bv = G["b"][:, bass.ds(h * TOK, SEQ)].rearrange("p (c n) -> p c n", n=P)
                        nc.vector.tensor_tensor(G["dd"][:, s, 0:SEQ].rearrange("p (c n) -> p c n", n=P),
                                                bcast(bv[:, :, P - 1], 2, P), bv, ALU.subtract)
                        bl = G["b"][:, bass.ds(h * TOK + TOK - 1, 1)]
                        nc.vector.tensor_tensor(G["dd"][:, s, SEQ:TOK], bl.to_broadcast([P, DEC]),
                                                G["b"][:, bass.ds(h * TOK + SEQ, DEC)],
                                                ALU.subtract).then_inc(S["g_d"], 1)
                        return
                    m = LEVELS[n]
                    w = SEQ if n == 0 else TOK
                    if n >= 2:
                        dve.wait_ge(S["g_e"], (n_lv + 1) * h + n - 1)
                    bv = G["b"][:, bass.ds(h * TOK, w)].rearrange("p (c n) -> p c n", n=2 * m)
                    nc.vector.tensor_tensor(G["dd"][:, s, 0:w].rearrange("p (c n) -> p c n", n=2 * m), bv,
                                            bcast(bv[:, :, m - 1], 2, 2 * m), ALU.subtract).then_inc(S["g_d"], 1)

                def merge(n):
                    s = n % 2
                    dve.wait_ge(S["g_at"], 1 + (n_lv + 1) * h + n + 1)
                    if n == 0:
                        dve.wait_ge(S["g_at0"], h + 1)
                    else:
                        dve.wait_ge(S["g_merge"], (n_lv + 1) * h + n)
                    apart(dve, S)
                    mask = S["const"][:, C_MSK + n * P:C_MSK + (n + 1) * P].bitcast(U32)
                    ins = nc.vector.copy_predicated(G["at"][:, 0:SEQ].rearrange("p (c n) -> p c n", n=P),
                                                    bcast(mask, 1, 4),
                                                    S["mm"][s][:, 0, :].rearrange("p (c n) -> p c n", n=P))
                    if n:
                        ins = nc.vector.copy_predicated(G["at"][0:DEC, SEQ:TOK], mask[0:DEC, 0:DEC],
                                                        S["mm"][s][0:DEC, 1, 0:DEC])
                    ins.then_inc(S["g_merge"], 1)

                delta(0)
                for n in range(n_lv + 1):
                    delta(n + 1) if n + 1 <= n_lv else None
                    s = n % 2
                    w = SEQ if n == 0 else TOK
                    if n >= 2:
                        dve.wait_ge(S["g_at"], 1 + (n_lv + 1) * h + n - 1)
                    qw = S["big"][:, bass.ds(h * TOK, w)]
                    if n < n_lv:
                        dve.wait_ge(S["g_e"], (n_lv + 1) * h + n + 1)
                        nc.vector.scalar_tensor_tensor(out=G["ql"][:, s, 0:w], in0=qw, scalar=dk_scale,
                                                       in1=G["e"][:, s, 0:w], op0=ALU.mult,
                                                       op1=ALU.mult).then_inc(S["g_ql"], 1)
                    else:
                        nc.vector.tensor_scalar(G["ql"][:, s, 0:w], qw, dk_scale, None, ALU.mult).then_inc(S["g_ql"], 1)
                    if n:
                        merge(n - 1)
                merge(n_lv)
                dve.wait_ge(S["g_eb"], 3 * h + 3)
                nc.vector.scalar_tensor_tensor(out=G["qb"][:, :], in0=q, scalar=dk_scale, in1=G["qb"][:, :],
                                               op0=ALU.mult, op1=ALU.mult).then_inc(S["g_qb"], 1)
                dve.wait_ge(S["g_ds"], h + 1)
                dve.wait_ge(S["g_out"], 1 + 32 * h)
                nc.vector.tensor_copy(G["st"][:, 1, :], S["aux2"][:, 0, 0:256]).then_inc(S["g_chain"], 1)
                for c in range(1, 4):
                    dve.wait_ge(S["g_chain"], 4 * h + c)
                    nc.vector.scalar_tensor_tensor(out=G["st"][:, (c + 1) % 4, :], in0=G["st"][:, c, :],
                                                   scalar=G["el"][:, c:c + 1],
                                                   in1=S["aux2"][:, c // 2, (c % 2) * 256:(c % 2) * 256 + 256],
                                                   op0=ALU.mult, op1=ALU.add).then_inc(S["g_chain"], 1)
                dve.wait_ge(S["g_state"], 16 * (h + 1))
                nc.vector.scalar_tensor_tensor(out=G["s_fin"][:, :], in0=G["st"][:, 4, :], scalar=G["el"][:, 4:5],
                                               in1=S["aux"][:, 0, 0:256], op0=ALU.mult,
                                               op1=ALU.add).then_inc(S["g_fin"], 1)
                for v in range(2):
                    dve.wait_ge(S["g_o"], 1 + 2 * h + v + 1)
                    nc.vector.tensor_copy(G["oc"][:, v, 0:SEQ], S["mm"][v][:, 0, :])
                    nc.vector.tensor_copy(G["oc"][:, v, SEQ:TOK], S["mm"][v][:, 1, 0:DEC]).then_inc(S["g_oc"], 1)
                dve.wait_ge(S["g_root"], 1 + h + 1)
                nc.vector.reciprocal(S["rinv"][:, :], S["root"][:, :]).then_inc(S["g_rinv"], 1)
                dve.wait_ge(S["g_rinv"], h + 1)
                for v in range(2):
                    nc.vector.scalar_tensor_tensor(out=G["oc"][:, v, :], in0=G["oc"][:, v, :],
                                                   scalar=S["gains"][:, G_GLA + v:G_GLA + v + 1], in1=S["rinv"][:, :],
                                                   op0=ALU.mult, op1=ALU.mult).then_inc(S["g_on"], 1)
                for v in range(2):
                    gate = feat(S, 16 + 2 * h + v)
                    dve.wait_ge(S["g_on"], 2 * h + v + 1)
                    nc.vector.tensor_tensor(gate, gate, G["oc"][:, v, :], ALU.mult).then_inc(S["g_gated"], 1)

        @block.tensor
        def _(pe):
            for h in range(GH):
                pb = [S["mm"][0], S["mm"][1], S["aux"], S["aux2"]][h]
                matmul_tok(nc, pb, S["w_gate"][0:RANK, h * P:(h + 1) * P], S["glr"][0:RANK, :], True,
                           True).then_inc(S["g_z"], 1)
            with pe.Fori(0, GH) as h:
                pe.wait_ge(S["g_vs"], 2 * h + 2)
                pe.wait_ge(S["g_zb"], 1)
                pe.wait_ge(S["g_root"], 1 + h)
                pe.wait_ge(S["g_fin"], 1 + h)
                for v in range(2):
                    tr = [S["aux"], S["aux2"]][v]
                    for c in range(NC_T):
                        t0, n = token_cols(c)
                        out = tr[:, 0, t0:t0 + P] if c < 4 else tr[0:DEC, 1, 0:P]
                        ins = nc.tensor.transpose(out, G["vs"][:, v, t0:t0 + n], S["ident"])
                    ins.then_inc(S["g_vT"], 1)
                for n in range(n_lv + 1):
                    s = n % 2
                    pe.wait_ge(S["g_ql"], (n_lv + 1) * h + n + 1)
                    pe.wait_ge(S["g_kl"], (n_lv + 2) * h + n + 1)
                    if n >= 2:
                        pe.wait_ge(S["g_merge"], (n_lv + 1) * h + n - 1)
                    else:
                        pe.wait_ge(S["g_oc"], 1 + 2 * h)
                    for c in range(4 if n == 0 else 5):
                        t0, w = token_cols(c)
                        out = S["mm"][s][:, 0, t0:t0 + P] if c < 4 else S["mm"][s][0:DEC, 1, 0:DEC]
                        ins = nc.tensor.matmul(out, G["kl"][:, s, t0:t0 + w], G["ql"][:, s, t0:t0 + w], start=True,
                                               stop=True)
                    ins.then_inc(S["g_at"], 1)
                s = (n_lv + 1) % 2
                pe.wait_ge(S["g_kl"], (n_lv + 2) * (h + 1))
                pe.wait_ge(S["g_vt"], 4 * (h + 1))
                for c in range(NC_T):
                    t0, n = token_cols(c)
                    out = S["aux"][:, 0, t0:t0 + P] if c < 4 else S["aux"][0:DEC, 1, 0:P]
                    ins = nc.tensor.transpose(out, G["kl"][:, s, t0:t0 + n], S["ident"])
                ins.then_inc(S["g_kT"], 1)
                pe.wait_ge(S["g_kt"], 2 * (h + 1))
                for c in range(4):
                    nc.tensor.matmul(S["aux2"][:, c // 2, (c % 2) * 256:(c % 2) * 256 + 256], G["kt"][:, c, :],
                                     G["vt"][:, c, :], start=True, stop=True)
                nc.tensor.matmul(S["aux"][:, 0, 0:256], G["kt"][0:DEC, 4, :], G["vt"][0:DEC, 4, :], start=True,
                                 stop=True).then_inc(S["g_ds"], 1)
                pe.wait_ge(S["g_merge"], (n_lv + 1) * (h + 1))
                pe.wait_ge(S["g_qb"], h + 1)
                pe.wait_ge(S["g_fin"], 1 + h + 1)
                for v in range(2):
                    vc = slice(v * P, (v + 1) * P)
                    for c in range(NC_T):
                        t0, n = token_cols(c)
                        out = S["mm"][v][:, 0, t0:t0 + P] if c < 4 else S["mm"][v][:, 1, 0:DEC]
                        ins = nc.tensor.matmul(out, G["vt"][0:n, c, vc], G["at"][0:n, t0:t0 + n], start=True,
                                               stop=c == 0)
                        if c:
                            ins = nc.tensor.matmul(out, G["st"][:, c, vc], G["qb"][:, t0:t0 + n], start=False,
                                                   stop=True)
                    ins.then_inc(S["g_o"], 1)
                for v in range(2):
                    pe.wait_ge(S["g_osq"], 2 * h + v + 1)
                    ins = matmul_tok(nc, S["aux"], S["ones"][:, :], G["osq"][:, v, :], v == 0, v == 1)
                ins.then_inc(S["g_osum"], 1)


def stage_mix(nc, S, A):
    res3 = as3(S["res"][:, :])
    ob3 = as3(S["big"][:, 16 * TOK:24 * TOK])
    mix3 = as3(S["big"][:, 0:8 * TOK])

    with nc.Block() as block:
        @block.sync
        def _(sp):
            with sp.Fori(T_GA // 2, T_PQ // 2) as i:
                load_w(sp, S, i, 3)
                load_w(sp, S, i, 4)

        @block.gpsimd
        def _(pool):
            pool.wait_ge(S["x_split"], 2)
            pool.dma_start(S["res"][:, :], A["xT"]).then_inc(S["x_again"], 16)

        @block.scalar
        def _(act):
            with act.Fori(T_GA // 2, T_WA // 2) as i:
                for u in range(2):
                    split_hi(nc, act, S, i, u + 1)
                    act.wait_ge(S["tile_done"], 2 * i + u + 1)
                    nc.scalar.activation(halves(feat(S, 2 * i + u - T_GA)), S["mm"][u][:, :, 0:HALF],
                                         ACT.Sigmoid).then_inc(S["evacuated"], 1)
            split_activation_hi(nc, act, S, res3, S["tile_done"], T_WA)
            with act.Fori(T_WA // 2, T_WB // 2) as i:
                split_hi(nc, act, S, i, 1)
                split_hi(nc, act, S, i, 2)
            split_activation_hi(nc, act, S, ob3, S["tile_done"], T_WB)
            with act.Fori(T_WB // 2, T_WO // 2) as i:
                split_hi(nc, act, S, i, 1)
                split_hi(nc, act, S, i, 2)
            split_activation_hi(nc, act, S, mix3, S["evacuated"], T_WO)
            with act.Fori(T_WO // 2, T_PQ // 2) as i:
                split_hi(nc, act, S, i, 1)
                split_hi(nc, act, S, i, 2)
            rms_squares(nc, act, S, S["evacuated"], T_PQ)
            rms_root(nc, act, S, 1)
            split_activation_hi(nc, act, S, as3(S["big"][:, 8 * TOK:16 * TOK]), S["n_done"], 2)

        @block.vector
        def _(dve):
            with dve.Fori(T_GA // 2, T_WA // 2) as i:
                split_lo(nc, dve, S, i, 1)
                split_lo(nc, dve, S, i, 2)
            split_activation_lo(nc, dve, S, res3, 2)
            with dve.Fori(T_WA // 2, T_WB // 2) as i:
                for u in range(2):
                    gate = halves(feat(S, 2 * i + u - T_WA))
                    split_lo(nc, dve, S, i, u + 1)
                    dve.wait_ge(S["tile_done"], 2 * i + u + 1)
                    nc.vector.tensor_tensor(gate, gate, S["mm"][u][:, :, 0:HALF], ALU.mult).then_inc(S["evacuated"], 1)
            split_activation_lo(nc, dve, S, ob3, 3)
            with dve.Fori(T_WB // 2, T_WO // 2) as i:
                for u in range(2):
                    n = 2 * i + u - T_WB
                    split_lo(nc, dve, S, i, u + 1)
                    dve.wait_ge(S["evacuated"], 2 * i + u)
                    dve.wait_ge(S["tile_done"], 2 * i + u + 1)
                    nc.vector.tensor_tensor(halves(S["rsin"][:, :]), halves(feat(S, n + 8)), S["mm"][u][:, :, 0:HALF],
                                            ALU.mult).then_inc(S["m_tmp"], 1)
                    dve.wait_ge(S["m_tmp"], n + 1)
                    nc.vector.tensor_tensor(feat(S, n), feat(S, n), S["rsin"][:, :],
                                            ALU.add).then_inc(S["evacuated"], 1)
            split_activation_lo(nc, dve, S, mix3, 4)
            dve.wait_ge(S["x_again"], 16)
            with dve.Fori(T_WO // 2, T_PQ // 2) as i:
                for u in range(2):
                    h = halves(S["res"][:, bass.ds((2 * i + u - T_WO) * TOK, TOK)])
                    split_lo(nc, dve, S, i, u + 1)
                    dve.wait_ge(S["tile_done"], 2 * i + u + 1)
                    nc.vector.tensor_tensor(h, h, S["mm"][u][:, :, 0:HALF], ALU.add).then_inc(S["evacuated"], 1)
            rms_apply(nc, dve, S, 1, G_N2)
            split_activation_lo(nc, dve, S, as3(S["big"][:, 8 * TOK:16 * TOK]), 5)

        @block.tensor
        def _(pe):
            for n, (a, b) in enumerate(((T_GA, T_WA), (T_WA, T_WB), (T_WB, T_WO), (T_WO, T_PQ))):
                pe.wait_ge(S["x_split"], n + 1)
                pe.wait_ge(S["evacuated"], a)
                with pe.Fori(a // 2, b // 2) as i:
                    dense_tile(nc, pe, S, i, 0)
                    dense_tile(nc, pe, S, i, 1)
            rms_sum(nc, pe, S, 1)


def stage_keys(nc, S, A, R):
    with nc.Block() as block:
        @block.sync
        def _(sp):
            sp.dma_start(R["sk"][:, :], A["skT"]).then_inc(S["r_sk"], 16)
            with sp.Fori(T_PQ // 2, T_END // 2 - 2) as i:
                load_w(sp, S, i, 3)
                load_w(sp, S, i, 4)
            load_w(sp, S, T_END // 2 - 2, 3)

        @block.scalar
        def _(act):
            def query(i, u, last=False):
                t = 2 * i + u
                if not last:
                    split_hi(nc, act, S, i, u + 1)
                act.wait_ge(S["tile_done"], t + 1)
                act.wait_ge(S["r_mm"], t - T_PQ - 1) if not (isinstance(t, int) and t < T_PQ + 2) else None
                nc.scalar.activation(halves(R["qp"][:, u, :]), S["mm"][u][:, :, 0:HALF], ACT.Copy).then_inc(S["evacuated"], 1)

            def scores(i, u):
                n = 2 * i + u - T_PQ
                act.wait_ge(S["r_mm"], n + 1)
                if not (isinstance(n, int) and n < 2):
                    act.wait_ge(S["r_top"], 1 + n - 1)
                nc.scalar.activation(R["s"][:, u, 0:SEQ], S["aux"][:, 0, :], ACT.Copy)
                nc.scalar.activation(R["s"][0:DEC, u, SEQ:SEQ + P], S["aux"][0:DEC, 1, 0:P],
                                     ACT.Copy).then_inc(S["r_s"], 1)
            b = T_PQ // 2
            query(b, 0)
            query(b, 1)
            scores(b, 0)
            with act.Fori(b + 1, T_END // 2 - 1) as i:
                query(i, 0)
                scores(i - 1, 1)
                query(i, 1)
                scores(i, 0)
            e = T_END // 2 - 1
            query(e, 0)
            scores(e - 1, 1)
            query(e, 1, last=True)
            scores(e, 0)
            scores(e, 1)

        @block.tensor
        def _(pe):
            def scores(i, u):
                n = 2 * i + u - T_PQ
                pe.wait_ge(S["evacuated"], 2 * i + u + 1)
                if not (isinstance(n, int) and n < 1):
                    pe.wait_ge(S["r_s"], n)
                for c in range(NC_T):
                    t0, w = token_cols(c)
                    out = S["aux"][:, 0, t0:t0 + P] if c < 4 else S["aux"][0:DEC, 1, 0:P]
                    ins = nc.tensor.matmul(out, R["qp"][:, u, t0:t0 + w], R["sk"][:, bass.ds(n * P, P)], start=True,
                                           stop=True)
                ins.then_inc(S["r_mm"], 1)
            pe.wait_ge(S["x_split"], 5)
            pe.wait_ge(S["evacuated"], T_PQ)
            pe.wait_ge(S["r_sk"], 16)
            b = T_PQ // 2
            dense_tile(nc, pe, S, b, 0)
            dense_tile(nc, pe, S, b, 1)
            scores(b, 0)
            with pe.Fori(b + 1, T_END // 2) as i:
                dense_tile(nc, pe, S, i, 0)
                scores(i - 1, 1)
                dense_tile(nc, pe, S, i, 1)
                scores(i, 0)
            scores(T_END // 2 - 1, 1)

        @block.vector
        def _(dve):
            def top16(i, u):
                n = 2 * i + u - T_PQ
                dve.wait_ge(S["r_s"], n + 1)
                if not (isinstance(n, int) and n < 2):
                    dve.wait_ge(S["r_kept"], 1 + 2 * n - 2)
                if not (isinstance(n, int) and n < 1):
                    dve.wait_ge(S["r_top"], 1 + n)
                apart(dve, S)
                rows = [P] * 4 + [DEC]

                def sc(c):
                    return R["s"][0:rows[c], u, c * P:(c + 1) * P]
                for c in range(NC_T):
                    ins = nc.vector.max(R["tv"][0:rows[c], u, c * 16:c * 16 + 8], sc(c))
                ins.then_inc(S["r_c"], 1)
                dve.wait_ge(S["r_c"], 3 * n + 1)
                apart(dve, S)
                for c in range(NC_T):
                    ins = nc.vector.match_replace(R["s2"][0:rows[c], c * P:(c + 1) * P],
                                                  R["tv"][0:rows[c], u, c * 16:c * 16 + 8], sc(c), NEG)
                ins.then_inc(S["r_c"], 1)
                for c in range(NC_T):
                    nc.vector.max_index(R["ti"][0:rows[c], u, c * 16:c * 16 + 8],
                                        R["tv"][0:rows[c], u, c * 16:c * 16 + 8], sc(c))
                dve.wait_ge(S["r_c"], 3 * n + 2)
                apart(dve, S)
                for c in range(NC_T):
                    ins = nc.vector.max(R["tv"][0:rows[c], u, c * 16 + 8:c * 16 + 16],
                                        R["s2"][0:rows[c], c * P:(c + 1) * P])
                ins.then_inc(S["r_c"], 1)
                dve.wait_ge(S["r_c"], 3 * n + 3)
                apart(dve, S)
                for c in range(NC_T):
                    ins = nc.vector.max_index(R["ti"][0:rows[c], u, c * 16 + 8:c * 16 + 16],
                                              R["tv"][0:rows[c], u, c * 16 + 8:c * 16 + 16],
                                              R["s2"][0:rows[c], c * P:(c + 1) * P])
                ins.then_inc(S["r_top"], 1)
            nc.vector.memset(R["tv"][:, :, :], 0.0).then_inc(S["r_init"], 1)
            nc.vector.memset(R["ti"][:, :, :], 0).then_inc(S["r_init"], 1)
            dve.wait_ge(S["r_init"], 2)
            b = T_PQ // 2
            split_lo(nc, dve, S, b, 1)
            split_lo(nc, dve, S, b, 2)
            top16(b, 0)
            with dve.Fori(b + 1, T_END // 2 - 1) as i:
                split_lo(nc, dve, S, i, 1)
                top16(i - 1, 1)
                split_lo(nc, dve, S, i, 2)
                top16(i, 0)
            e = T_END // 2 - 1
            split_lo(nc, dve, S, e, 1)
            top16(e - 1, 1)
            top16(e, 0)
            top16(e, 1)

        @block.gpsimd
        def _(pool):
            with pool.Fori(0, 2 * PH // 2) as i:
                for u in range(2):
                    n = 2 * i + u
                    pool.wait_ge(S["r_top"], 1 + n + 1)
                    apart(pool, S)
                    nc.gpsimd.tensor_copy(R["sv"][:, :, bass.ds(n * 16, 16)],
                                          R["tv"][:, u, :].rearrange("p (c k) -> p c k", k=16)).then_inc(S["r_kept"], 1)
                    nc.gpsimd.tensor_copy(R["si"][:, :, bass.ds(n * 16, 16)],
                                          R["ti"][:, u, :].rearrange("p (c k) -> p c k", k=16)).then_inc(S["r_kept"], 1)


def load_u(sp, S, A, base, r):
    e = base + r
    if not (isinstance(e, int) and e < 2):
        sp.wait_ge(S["u_lo"], e - 1)
    sp.dma_start(S["w_raw"][:, r % 2, :], A["u"][:, bass.ds(e, 1), :]).then_inc(S["u_in"][r % 2], 16)


def u_hi(nc, act, S, base, r):
    e = base + r
    act.wait_ge(S["u_in"][r % 2], 8 * (base + r - r % 2) + 16)
    if not (isinstance(e, int) and e < 2):
        act.wait_ge(S["u_mm"], e - 1)
    nc.scalar.activation(S["w_hi"][:, r % 2, :], S["w_raw"][:, r % 2, :], ACT.Copy).then_inc(S["u_hi"], 1)


def u_lo(nc, dve, S, base, r):
    dve.wait_ge(S["u_hi"], base + r + 1)
    nc.vector.tensor_tensor(S["w_lo"][:, r % 2, :], S["w_raw"][:, r % 2, :], S["w_hi"][:, r % 2, :].bitcast(F32),
                            ALU.subtract).then_inc(S["u_lo"], 1)


def run_u(nc, pe, S, base, r, banks):
    e = base + r
    pe.wait_ge(S["u_lo"], e + 1)
    pe.wait_ge(S["u_gel"], 2 + e - 1)
    for f in range(2):
        cols = slice(f * HALF, (f + 1) * HALF)
        for k in range(KT):
            w = slice(k * P, (k + 1) * P)
            ins = product3(nc, banks[r % 2][:, f, 0:HALF], S["w_hi"][:, r % 2, w], S["w_lo"][:, r % 2, w],
                           S["x_hi"][:, k, cols], S["x_lo"][:, k, cols], k == 0, k == KT - 1)
    ins.then_inc(S["u_mm"], 1)


def early_gelu(nc, act, S, R, base, r):
    act.wait_ge(S["u_mm"], base + r + 1)
    act.wait_ge(S["h_out"][r % 2], 1 + 8 * (base + r - r % 2))
    nc.scalar.activation(halves(R["hst"][:, r % 2, :]), early_banks(S)[r % 2][:, :, 0:HALF],
                         ACT.Gelu).then_inc(S["u_gel"], 1)
    u_hi(nc, act, S, base, r + 2)


def early_dma(sp, S, A, R, base, r):
    e = base + r
    sp.wait_ge(S["u_gel"], 2 + e + 1)
    sp.dma_start(A["h"][:, bass.ds(e, 1), :], R["hst"][:, r % 2, :]).then_inc(S["h_out"][r % 2], 16)
    load_u(sp, S, A, base, r + 4)


def early_banks(S):
    return [S["aux"], S["aux2"]]


def stage_route(nc, S, A, R):
    hk = PH * TOPK
    with nc.Block() as block:
        @block.sync
        def _(sp):
            for r in range(4):
                load_u(sp, S, A, 0, r)
            with sp.Fori(0, NC_T) as c:
                for r in range(ROUTE_U):
                    early_dma(sp, S, A, R, ROUTE_U * c, r)

        @block.vector
        def _(dve):
            u_lo(nc, dve, S, 0, 0)
            u_lo(nc, dve, S, 0, 1)
            with dve.Fori(0, NC_T) as c:
                def early(r):
                    u_lo(nc, dve, S, ROUTE_U * c, r + 2)

                def picks(table, half):
                    v = table[:, bass.ds(c, 1), :].rearrange("p o (h q k) -> p (o h) q k", h=PH, q=2)
                    return v[:, :, half, :]
                dve.wait_ge(S["t_ij"], 1 + 2 * c)
                cand4 = R["cand"][:, :].rearrange("p (h a b) -> p h a b", h=PH, a=TOPK)
                nc.vector.tensor_tensor(cand4, bcast(picks(R["sv"], 0), 3, TOPK), bcast(picks(R["sv"], 1), 2, TOPK),
                                        ALU.add).then_inc(S["t_cand"], 1)
                dve.wait_ge(S["t_cand"], c + 1)
                apart(dve, S)

                def cols(h):
                    return slice(h * 256, (h + 1) * 256)
                for h in range(PH):
                    ins = nc.vector.max(R["v2"][:, h * 16:h * 16 + 8], R["cand"][:, cols(h)])
                ins.then_inc(S["t_c"], 1)
                dve.wait_ge(S["t_c"], 3 * c + 1)
                apart(dve, S)
                for h in range(PH):
                    ins = nc.vector.match_replace(R["cand2"][:, cols(h)], R["v2"][:, h * 16:h * 16 + 8],
                                                  R["cand"][:, cols(h)], NEG)
                ins.then_inc(S["t_c"], 1)
                for h in range(PH):
                    nc.vector.max_index(R["i2"][:, h * 16:h * 16 + 8], R["v2"][:, h * 16:h * 16 + 8], R["cand"][:, cols(h)])
                early(0)
                dve.wait_ge(S["t_c"], 3 * c + 2)
                apart(dve, S)
                for h in range(PH):
                    ins = nc.vector.max(R["v2"][:, h * 16 + 8:h * 16 + 16], R["cand2"][:, cols(h)])
                ins.then_inc(S["t_c"], 1)
                early(1)
                dve.wait_ge(S["t_c"], 3 * c + 3)
                apart(dve, S)
                for h in range(PH):
                    ins = nc.vector.max_index(R["i2"][:, h * 16 + 8:h * 16 + 16], R["v2"][:, h * 16 + 8:h * 16 + 16],
                                              R["cand2"][:, cols(h)])
                ins.then_inc(S["t_idx"], 1)
                v3 = R["v2"][:, :].rearrange("p (h k) -> p h k", h=PH)
                g3 = R["gij"][:, 0, :].rearrange("p (h k) -> p h k", h=PH)
                nc.vector.tensor_tensor(R["e2"][:, :].rearrange("p (h k) -> p h k", h=PH), v3,
                                        bcast(v3[:, :, 0], 2, TOPK), ALU.subtract).then_inc(S["t_sub"], 1)
                dve.wait_ge(S["t_idx"], c + 1)
                nc.vector.tensor_scalar(R["ab"][:, 0, :], R["i2"][:, :], 4, None, ALU.logical_shift_right).then_inc(S["t_ab"], 1)
                nc.vector.tensor_scalar(R["ab"][:, 1, :], R["i2"][:, :], 15, None, ALU.bitwise_and).then_inc(S["t_ab"], 1)
                dve.wait_ge(S["t_ab"], 4 * c + 2)
                nc.vector.tensor_copy(R["abf"][:, 0, :], R["ab"][:, 0, :]).then_inc(S["t_ab"], 1)
                nc.vector.tensor_copy(R["abf"][:, 1, :], R["ab"][:, 1, :]).then_inc(S["t_ab"], 1)
                dve.wait_ge(S["t_ab"], 4 * c + 4)
                early(2)
                iota16 = S["const"][:, C_IOTA:C_IOTA + TOPK]
                for q in range(2):
                    eq = R["cand2"] if q else R["cand"]
                    nc.vector.tensor_tensor(eq[:, :].rearrange("p (n a) -> p n a", a=TOPK),
                                            bcast(R["abf"][:, q, :], 2, TOPK), bcast(iota16, 1, hk),
                                            ALU.is_equal).then_inc(S["t_eq"], 1)
                dve.wait_ge(S["t_exp"], c + 1)
                nc.vector.tensor_reduce(R["z2"][:, 0:PH], R["e2"][:, :].rearrange("p (h k) -> p h k", h=PH), AX.X,
                                        ALU.add).then_inc(S["t_z"], 1)
                dve.wait_ge(S["t_z"], 2 * c + 1)
                nc.vector.reciprocal(R["z2"][:, PH:2 * PH], R["z2"][:, 0:PH]).then_inc(S["t_z"], 1)
                dve.wait_ge(S["t_z"], 2 * c + 2)
                dve.wait_ge(S["t_turned"], 1 + c)
                nc.vector.tensor_tensor(g3, R["e2"][:, :].rearrange("p (h k) -> p h k", h=PH),
                                        bcast(R["z2"][:, PH:2 * PH], 2, TOPK), ALU.mult).then_inc(S["t_g"], 1)
                early(3)
                for q in range(2):
                    eq = R["cand2"] if q else R["cand"]
                    e4 = eq[:, :].rearrange("p (h k a) -> p h k a", h=PH, k=TOPK)
                    dve.wait_ge(S["t_eq"], 4 * c + q + 1)
                    nc.vector.tensor_tensor(e4, e4, bcast(picks(R["si"], q), 2, TOPK), ALU.mult).then_inc(S["t_eq"], 1)
                early(4)
                for q in range(2):
                    eq = R["cand2"] if q else R["cand"]
                    dve.wait_ge(S["t_eq"], 4 * c + q + 3)
                    nc.vector.tensor_reduce(R["gij"][:, 1 + q, :], eq[:, :].rearrange("p (n a) -> p n a", a=TOPK),
                                            AX.X, ALU.add).then_inc(S["t_ij"], 1)
                early(5)

        @block.scalar
        def _(act):
            u_hi(nc, act, S, 0, 0)
            u_hi(nc, act, S, 0, 1)
            with act.Fori(0, NC_T) as c:
                for r in range(3):
                    early_gelu(nc, act, S, R, ROUTE_U * c, r)
                act.wait_ge(S["t_sub"], c + 1)
                nc.scalar.activation(R["e2"][:, :], R["e2"][:, :], ACT.Exp).then_inc(S["t_exp"], 1)
                for r in range(3, ROUTE_U):
                    early_gelu(nc, act, S, R, ROUTE_U * c, r)
                act.wait_ge(S["t_turned"], 1 + c + 1)
                nc.scalar.activation(R["tab"][:, :, bass.ds(c * P, P)],
                                     S["mm"][0][:, 0, 0:3 * P].rearrange("p (q n) -> p q n", q=3),
                                     ACT.Copy).then_inc(S["t_tab"], 1)

        @block.tensor
        def _(pe):
            with pe.Fori(0, NC_T) as c:
                for r in range(ROUTE_U):
                    run_u(nc, pe, S, ROUTE_U * c, r, early_banks(S))
                pe.wait_ge(S["t_ij"], 1 + 2 * c + 2)
                pe.wait_ge(S["t_g"], c + 1)
                pe.wait_ge(S["t_tab"], 1 + c)
                for q in range(3):
                    ins = nc.tensor.transpose(S["mm"][0][:, 0, q * P:(q + 1) * P], R["gij"][:, q, :], S["ident"])
                ins.then_inc(S["t_turned"], 1)


def stage_gates(nc, S, A, R, Q):
    GRP = 8
    n_grp = CHUNK_TOK // GRP
    n_chunk = TOK // CHUNK_TOK
    bodies = n_chunk * n_grp // 4
    e0 = ROUTE_U * NC_T
    iota = S["const"][:, C_IOTA:C_IOTA + P]
    banks = [S["mm"][0], S["mm"][1]]
    on_dve = 3
    closing = range(EARLY - CLOSING, EARLY)

    with nc.Block() as block:
        @block.vector
        def _(dve):
            def weighted(b, q):
                g, u = 4 * b + q, q % 2
                dve.wait_ge(S["e_mm"], 2 + g - 1)
                for j in range(GRP):
                    ins = nc.vector.tensor_scalar(Q["a"][:, u, j * P:(j + 1) * P], iota,
                                                  R["tab"][:, 1, bass.ds(g * GRP + j, 1)],
                                                  R["tab"][:, 0, bass.ds(g * GRP + j, 1)], ALU.is_equal, ALU.mult)
                for j in range(on_dve):
                    ins = nc.vector.tensor_scalar(Q["b"][:, u, j * P:(j + 1) * P], iota,
                                                  R["tab"][:, 2, bass.ds(g * GRP + j, 1)], None, ALU.is_equal)
                ins.then_inc(S["e_a"], 1)
            weighted(0, 0)
            weighted(0, 1)
            with dve.Fori(0, bodies - 1) as b:
                for half in range(2):
                    weighted(b, 2 * half + 2)
                    weighted(b, 2 * half + 3)
                    u_lo(nc, dve, S, e0 + 2 * b, half + 2)
            weighted(bodies - 1, 2)
            weighted(bodies - 1, 3)
            for e in range(e0 + 2 * bodies - 2, EARLY):
                u_lo(nc, dve, S, 0, e + 2)

        @block.gpsimd
        def _(pool):
            with pool.Fori(0, 2 * bodies) as i:
                for u in range(2):
                    g = 2 * i + u
                    pool.wait_ge(S["e_mm"], 2 + g - 1)
                    apart(pool, S)
                    nc.gpsimd.tensor_copy(Q["i2"][:, u, :], R["tab"][:, 2, bass.ds(g * GRP, GRP)]).then_inc(S["e_i2"], 1)
                    pool.wait_ge(S["e_i2"], g + 1)
                    apart(pool, S)
                    for j in range(on_dve, GRP):
                        ins = nc.gpsimd.tensor_scalar(Q["b"][:, u, j * P:(j + 1) * P], iota, Q["i2"][:, u, j:j + 1],
                                                      None, ALU.is_equal)
                    ins.then_inc(S["e_b"], 1)

        @block.tensor
        def _(pe):
            def products(b, q):
                g, u = 4 * b + q, q % 2
                pe.wait_ge(S["e_a"], g + 1)
                pe.wait_ge(S["e_b"], g + 1)
                pe.wait_ge(S["e_out"], 2 + g - 1)
                for j in range(GRP):
                    ins = nc.tensor.matmul(banks[u][:, j // 4, (j % 4) * P:(j % 4 + 1) * P],
                                           Q["b"][:, u, j * P:(j + 1) * P], Q["a"][:, u, j * P:(j + 1) * P],
                                           start=True, stop=True)
                ins.then_inc(S["e_mm"], 1)

            with pe.Fori(0, bodies) as b:
                for half in range(2):
                    products(b, 2 * half)
                    products(b, 2 * half + 1)
                    run_u(nc, pe, S, e0 + 2 * b, half, early_banks(S))
            for e in closing:
                run_u(nc, pe, S, 0, e, early_banks(S))

        @block.scalar
        def _(act):
            def out(g, u, q, half):
                act.wait_ge(S["e_mm"], 2 + g + 1)
                src = banks[u][:, :, :].rearrange("p q (j n) -> p n (q j)", n=P)
                dst = Q["ring"][:, half, :, bass.ds(q * GRP, GRP)]
                nc.scalar.activation(dst, src, ACT.Copy).then_inc(S["e_out"], 1)

            def body(k2, half, b2):
                g = k2 * (2 * n_grp) + half * n_grp + 4 * b2
                e = k2 * n_grp + half * n_grp // 2 + 2 * b2 + e0
                for v in range(2):
                    out(g + 2 * v, 0, 4 * b2 + 2 * v, half)
                    out(g + 2 * v + 1, 1, 4 * b2 + 2 * v + 1, half)
                    early_gelu(nc, act, S, R, e, v)

            with act.Fori(0, n_chunk // 2) as k2:
                for half in range(2):
                    act.wait_ge(S["e_store"][half], 1 + 16 * k2)
                    with act.Fori(0, 2) as b2:
                        body(k2, half, b2)
            act.wait_ge(S["e_store"][0], 1 + 16 * (n_chunk // 2))
            body(n_chunk // 2, 0, 0)
            body(n_chunk // 2, 0, 1)
            for e in closing:
                early_gelu(nc, act, S, R, 0, e)

        @block.sync
        def _(sp):
            def store(k2, half):
                sp.wait_ge(S["e_out"], 2 + n_grp * (2 * k2 + half + 1))
                sp.dma_start(A["gate"][:, bass.ds(2 * k2 + half, 1), :, :],
                             Q["ring"][:, half, :, :]).then_inc(S["e_store"][half], 16)

            with sp.Fori(0, n_chunk // 2) as k2:
                for half in range(2):
                    with sp.Fori(0, 2) as b2:
                        for v in range(2):
                            early_dma(sp, S, A, R, k2 * n_grp + half * n_grp // 2 + 2 * b2 + e0, v)
                    store(k2, half)
            for e in range(e0 + 2 * bodies - 4, e0 + 2 * bodies):
                early_dma(sp, S, A, R, 0, e)
            store(n_chunk // 2, 0)
            for e in closing:
                early_dma(sp, S, A, R, 0, e)
            for u in range(2):
                sp.wait_ge(S["h_out"][u], 1 + 16 * (EARLY // 2))
            sp.wait_ge(S["e_store"][0], 1 + 16 * (n_chunk // 2 + 1))
            sp.wait_ge(S["e_store"][1], 1 + 16 * (n_chunk // 2))


def load_gv(sp, S, A, E, base, r):
    e = base + r
    if not (isinstance(e, int) and e < 2):
        sp.wait_ge(S["u_p"], e - 1)
    sp.dma_start(E["gate"][:, r % 2, :], A["gate"][:, :, bass.ds(e, 1), :]).then_inc(S["g_in"][r % 2], 16)
    if not (isinstance(e, int) and e < 2):
        sp.wait_ge(S["v_lo"], e - 1)
    sp.dma_start(E["v_raw"][:, r % 2, :], A["v"][:, bass.ds(e, 1), :]).then_inc(S["v_in"][r % 2], 16)


def loaded(base, r):
    return 8 * (base + r - r % 2) + 16


def v_hi(nc, act, S, E, base, r, slot):
    act.wait_ge(S["v_in"][r % 2], loaded(base, r))
    nc.scalar.activation(E["v_hi"][:, slot, :], E["v_raw"][:, r % 2, :], ACT.Copy).then_inc(S["v_hi"], 1)


def p_hi(nc, act, S, E, base, r, slot):
    act.wait_ge(S["u_p"], base + r + 1)
    nc.scalar.activation(E["p_hi"][:, slot, :], E["p"][:, :], ACT.Copy).then_inc(S["u_phi"], 1)


def gated(nc, dve, S, E, base, r, gel):
    e = base + r
    if not (isinstance(e, int) and e < 1):
        dve.wait_ge(S["u_plo"], e)
    dve.wait_ge(S["g_in"][r % 2], loaded(base, r))
    nc.vector.tensor_tensor(E["p"][:, :], gel, E["gate"][:, r % 2, :], ALU.mult).then_inc(S["u_p"], 1)


def p_lo(nc, dve, S, E, base, r, slot):
    dve.wait_ge(S["u_phi"], base + r + 1)
    nc.vector.tensor_tensor(E["p_lo"][:, slot, :], E["p"][:, :], E["p_hi"][:, slot, :].bitcast(F32),
                            ALU.subtract).then_inc(S["u_plo"], 1)


def v_lo(nc, dve, S, E, base, r, slot):
    dve.wait_ge(S["v_hi"], base + r + 1)
    nc.vector.tensor_tensor(E["v_lo"][:, slot, :], E["v_raw"][:, r % 2, :], E["v_hi"][:, slot, :].bitcast(F32),
                            ALU.subtract).then_inc(S["v_lo"], 1)


def add_y(nc, dve, S, g, d):
    r = halves(S["res"][:, d * TOK:(d + 1) * TOK])
    dve.wait_ge(S["y_mm"], 1 + KT * g + d + 1)
    nc.vector.tensor_tensor(r, r, [S["aux"], S["aux2"]][d % 2][:, :, 0:HALF], ALU.add).then_inc(S["y_add"], 1)


def run_y(nc, pe, S, E, g, slot0):
    pe.wait_ge(S["u_plo"], 4 * (g + 1))
    pe.wait_ge(S["v_lo"], 4 * (g + 1))
    for d in range(KT):
        pe.wait_ge(S["y_add"], 2 + KT * g + d - 1)
        w = slice(d * P, (d + 1) * P)
        for f in range(2):
            cols = slice(f * HALF, (f + 1) * HALF)
            for j in range(4):
                ins = product3(nc, [S["aux"], S["aux2"]][d % 2][:, f, 0:HALF], E["v_hi"][:, slot0 + j, w],
                               E["v_lo"][:, slot0 + j, w], E["p_hi"][:, slot0 + j, cols],
                               E["p_lo"][:, slot0 + j, cols], j == 0, j == 3)
        ins.then_inc(S["y_mm"], 1)


def stage_experts_early(nc, S, A, E):
    groups = EARLY // 4
    with nc.Block() as block:
        @block.sync
        def _(sp):
            def load(base, r):
                e = base + r
                if not (isinstance(e, int) and e < 2):
                    sp.wait_ge(S["u_p"], e - 1)
                sp.dma_start(E["h"][:, r % 2, :], A["h"][:, bass.ds(e, 1), :]).then_inc(S["h_in"][r % 2], 16)
                load_gv(sp, S, A, E, base, r)
            load(0, 0)
            load(0, 1)
            with sp.Fori(1, EARLY // 2) as i:
                load(2 * i, 0)
                load(2 * i, 1)
            load_gv(sp, S, A, E, EARLY, 0)
            load_gv(sp, S, A, E, EARLY, 1)

        @block.scalar
        def _(act):
            def prepare(g, parity):
                if not isinstance(g, int):
                    act.wait_ge(S["y_mm"], 1 + KT * (g - 1))
                for j in range(4):
                    v_hi(nc, act, S, E, 4 * g, j, 4 * parity + j)
                    p_hi(nc, act, S, E, 4 * g, j, 4 * parity + j)
            prepare(0, 0)
            with act.Fori(0, groups // 2 - 1) as i:
                prepare(2 * i + 1, 1)
                prepare(2 * i + 2, 0)
            act.wait_ge(S["y_mm"], 1 + KT * (groups - 2))
            prepare(groups - 1, 1)

        @block.vector
        def _(dve):
            def prepare(g, parity, j):
                slot = 4 * parity + j
                dve.wait_ge(S["h_in"][j % 2], loaded(4 * g, j))
                gated(nc, dve, S, E, 4 * g, j, E["h"][:, j % 2, :])
                v_lo(nc, dve, S, E, 4 * g, j, slot)
                p_lo(nc, dve, S, E, 4 * g, j, slot)

            def during_y(g, parity, ahead=True):
                for j in range(4):
                    if ahead:
                        prepare(g + 1, 1 - parity, j)
                    add_y(nc, dve, S, g, 2 * j)
                    add_y(nc, dve, S, g, 2 * j + 1)
            for j in range(4):
                prepare(0, 0, j)
            with dve.Fori(0, groups // 2 - 1) as i:
                during_y(2 * i, 0)
                during_y(2 * i + 1, 1)
            during_y(groups - 2, 0)
            during_y(groups - 1, 1, ahead=False)

        @block.tensor
        def _(pe):
            run_u(nc, pe, S, EARLY, 0, S["mm"])
            run_u(nc, pe, S, EARLY, 1, S["mm"])
            with pe.Fori(0, groups // 2) as i:
                run_y(nc, pe, S, E, 2 * i, 0)
                run_y(nc, pe, S, E, 2 * i + 1, 4)


def stage_experts(nc, S, A, E):
    first, groups = EARLY // 4, N_KEYS // 4

    def last(g, c, ahead):
        e = 4 * g + c
        return isinstance(e, int) and e + ahead >= N_KEYS

    with nc.Block() as block:
        @block.sync
        def _(sp):
            def step(g, c):
                if not last(g, c, 4):
                    load_u(sp, S, A, 4 * g, c + 4)
                if not last(g, c, 2):
                    load_gv(sp, S, A, E, 4 * g, c + 2)
            step(first, 0)
            with sp.Fori(first, groups - 2) as g:
                for c in range(1, 5):
                    step(g, c)
            for c in range(1, 5):
                step(groups - 2, c)
            step(groups - 1, 1)
            sp.wait_ge(S["y_add"], 2 + KT * groups)
            sp.dma_start(A["yT_out"], as3(S["res"][:, :])).then_inc(S["out_y"], 16)
            sp.wait_ge(S["out_y"], 16)
            sp.wait_ge(S["out_kv"], 32)
            sp.wait_ge(S["g_out"], 1 + 32 * GH)

        @block.scalar
        def _(act):
            def step(g, c):
                act.wait_ge(S["u_mm"], 4 * g + c + 1)
                nc.scalar.activation(halves(E["gel"][:, :]), S["mm"][c % 2][:, :, 0:HALF], ACT.Gelu).then_inc(S["u_gel"], 1)
                if not last(g, c, 2):
                    u_hi(nc, act, S, 4 * g, c + 2)
                if c == 4:
                    act.wait_ge(S["y_mm"], 1 + KT * (g + 1))
                p_hi(nc, act, S, E, 4 * g, c, c % 4)
                v_hi(nc, act, S, E, 4 * g, c, c % 4)
            step(first, 0)
            with act.Fori(first, groups - 1) as g:
                for c in range(1, 5):
                    step(g, c)
            for c in range(1, 4):
                step(groups - 1, c)

        @block.vector
        def _(dve):
            def step(g, c):
                if not last(g, c, 2):
                    u_lo(nc, dve, S, 4 * g, c + 2)
                if c == 4:
                    for d in range(KT):
                        add_y(nc, dve, S, g, d)
                dve.wait_ge(S["u_gel"], 2 + 4 * g + c + 1)
                gated(nc, dve, S, E, 4 * g, c, E["gel"][:, :])
                p_lo(nc, dve, S, E, 4 * g, c, c % 4)
                v_lo(nc, dve, S, E, 4 * g, c, c % 4)
            step(first, 0)
            with dve.Fori(first, groups - 1) as g:
                for c in range(1, 5):
                    step(g, c)
            for c in range(1, 4):
                step(groups - 1, c)
            for d in range(KT):
                add_y(nc, dve, S, groups - 1, d)

        @block.tensor
        def _(pe):
            for c in range(2, 5):
                run_u(nc, pe, S, 4 * first, c, S["mm"])
            run_y(nc, pe, S, E, first, 0)
            with pe.Fori(first + 1, groups - 1) as g:
                for c in range(1, 5):
                    run_u(nc, pe, S, 4 * g, c, S["mm"])
                run_y(nc, pe, S, E, g, 0)
            for c in range(1, 4):
                run_u(nc, pe, S, 4 * (groups - 1), c, S["mm"])
            run_y(nc, pe, S, E, groups - 1, 0)


SEMS = """passed x_in x_again c_in w_split w_hi_done tile_done evacuated x_hi_done x_split n_sq n_sum n_root n_rinv
n_done d_init lam_sum lam_exp lam_d glr_mm glr_done q_sq q_sum q_root q_rinv q_norm q_swap q_cos q_rsin
q_roped out_kv a_staged a_scores a_mask a_max a_exp a_rz a_w1 a_w a_vT a_vtok a_turned a_wT a_pv o_evac
o_sq o_sum o_root o_rinv o_done g_z g_zb g_la g_ls g_cum g_state g_out g_vs g_vT g_vt g_eb g_at0 g_d
g_abs g_e g_kl g_ql g_at g_merge g_kT g_kt g_ds g_chain g_fin g_qb g_o g_oc g_osq g_osum g_root
g_rinv g_on g_gated m_tmp r_sk r_mm r_s r_c r_top r_kept r_init t_cand t_c t_idx t_sub t_exp t_z t_g
t_ab t_eq t_ij t_turned t_tab e_mm e_a e_i2 e_b e_out u_lo u_hi u_mm u_gel u_p u_phi u_plo v_hi v_lo
y_mm y_add out_y""".split()
PAIR_SEMS = "w_loaded a_cache e_store u_in g_in v_in h_out h_in".split()


def build(nc, A):
    with ExitStack() as ctx:
        S = {}
        for name in SEMS:
            S[name] = ctx.enter_context(nc.semaphore(name))
        for name in PAIR_SEMS:
            S[name] = [ctx.enter_context(nc.semaphore(f"{name}{i}")) for i in range(2)]

        def make(stack, ns, stage, **shapes):
            for name, (shape, dt) in shapes.items():
                ns[name] = stack.enter_context(nc.sbuf_tensor(f"{stage}_{name}", [P] + shape, dt))

        psum = [ctx.enter_context(nc.psum_tensor(f"bank{i}", [P, 2, 512], F32)) for i in range(4)]
        S["mm"], S["aux"], S["aux2"] = psum[0:2], psum[2], psum[3]
        S["w_all"] = A["w_all"]
        make(ctx, S, "all",
             res=([KT * TOK], F32),
             x_hi=([KT, TOK], F32R), x_lo=([KT, TOK], F32R),
             w_raw=([2, D], F32), w_hi=([2, D], F32R), w_lo=([2, D], F32R),
             gains=([G_END], F32), gqk=([16], F32), gsub=([1], F32),
             lam=([5], F32), neglam=([1], F32), eps=([1], F32), ones=([P], F32))
        before = ctx.enter_context(ExitStack())
        make(before, S, "before", const=([C_END], F32), root=([TOK], F32), rinv=([TOK], F32), rsin=([TOK], F32))
        S["ident"] = S["const"][:, C_ID:C_ID + P]
        with ExitStack() as mixers:
            make(mixers, S, "mix", w_glr=([KT * RANK], F32), w_gate=([D // 2], F32), glr=([TOK], F32),
                 big=([24 * TOK], F32))
            stage_norm1(nc, S, A)
            with ExitStack() as here:
                make(here, S, "qkv", sq=([2, TOK], F32), nq=([2, TOK], F32), ncos=([2, TOK], F32))
                stage_qkv(nc, S, A)
            with ExitStack() as here:
                B = {}
                make(here, B, "att", qs=([2, TOK], F32), ks=([2, TOK], F32), vs=([2, TOK], F32), ck=([2, PAST], F32),
                     cv=([2, PAST], F32), vtok=([2, NC_T * P], F32), p=([2, 2, 512], F32), w=([2, 512], F32),
                     wT=([2, 512], F32), nmax=([2, 2], F32), z=([2, 2], F32), rz=([2, 2], F32),
                     rz2=([2, 1], F32), osb=([TOK], F32), osq=([TOK], F32))
                B["s"], B["o"] = S["mm"], S["aux2"]
                B["tr"] = [S["aux"][:, 0, :], S["aux"][:, 1, :]]
                stage_attention(nc, S, A, B)
            stage_gla_inputs(nc, S, A)
            with ExitStack() as here:
                G = {}
                make(here, G, "gla", b=([GH * TOK], F32), la=([GH * TOK], F32), e=([2, TOK], F32), dd=([2, TOK], F32),
                     qb=([TOK], F32), at=([TOK], F32), vt=([NC_T, 256], F32), kt=([NC_T, P], F32),
                     st=([5, 256], F32), s_fin=([256], F32), el=([5], F32))
                G["kl"] = G["la"][:, 0:2 * TOK].rearrange("p (s n) -> p s n", s=2)
                G["ql"] = G["la"][:, 2 * TOK:4 * TOK].rearrange("p (s n) -> p s n", s=2)
                G["vs"] = G["osq"] = G["e"]
                G["oc"] = G["dd"]
                stage_gla(nc, S, A, G)
            stage_mix(nc, S, A)
        R = {}
        with ExitStack() as routing:
            make(routing, R, "route", tab=([3, NC_T * P], F32), hst=([2, TOK], F32))
            with ExitStack() as here:
                make(here, R, "keys", sk=([2 * PH * P], F32), qp=([2, TOK], F32), s=([2, NC_T * P], F32),
                     s2=([NC_T * P], F32), tv=([2, NC_T * 16], F32), ti=([2, NC_T * 16], U32),
                     sv=([NC_T, 2 * PH * 16], F32), si=([NC_T, 2 * PH * 16], F32), cand=([PH * 256], F32),
                     cand2=([PH * 256], F32), v2=([P], F32), i2=([P], U32), e2=([P], F32), z2=([2 * PH], F32),
                     ab=([2, P], U32), abf=([2, P], F32), gij=([3, P], F32))
                stage_keys(nc, S, A, R)
                stage_route(nc, S, A, R)
            with ExitStack() as here:
                Q = {}
                make(here, Q, "gates", a=([2, 8 * P], F32), b=([2, 8 * P], F32), i2=([2, 8], F32), ring=([2, N_KEYS, CHUNK_TOK], F32))
                stage_gates(nc, S, A, R, Q)
        before.close()
        E = {}
        make(ctx, E, "exp", v_raw=([2, D], F32), v_hi=([8, D], F32R), v_lo=([8, D], F32R), gate=([2, TOK], F32),
             h=([2, TOK], F32), p=([TOK], F32), p_hi=([8, TOK], F32R), p_lo=([8, TOK], F32R))
        E["gel"] = E["h"][:, 0, :]
        stage_experts_early(nc, S, A, E)
        stage_experts(nc, S, A, E)


def const_table():
    t = np.zeros((P, C_END), np.float32)
    idx = np.arange(P)
    t[:, C_ID:C_ID + P] = np.eye(P)
    t[:, C_BLK:C_BLK + P] = idx[:, None] // HD == idx[None, :] // HD
    d = idx % HD
    for m in range(P):
        if d[m] < HD // 2:
            t[m + HD // 2, C_ROT + m] = -1.0
        else:
            t[m - HD // 2, C_ROT + m] = 1.0
    t[:, C_IOTA:C_IOTA + P] = idx[None, :]
    half = HD // 2
    inv = np.float32(10000.0) ** (-np.arange(half, dtype=np.float32) / np.float32(half))
    pos = np.concatenate([np.arange(SEQ), PAST + np.arange(DEC)]).astype(np.float32)
    ang = pos[None, :] * inv[idx % half][:, None]
    t[:, C_COS:C_COS + TOK] = np.cos(ang)
    t[:, C_SIN:C_SIN + TOK] = np.sin(ang)
    t[:, C_RST:C_RST + TOK] = (np.arange(TOK) % P != 0)[None, :]
    j, i = idx[:, None], idx[None, :]
    for n, m in enumerate(LEVELS):
        t[:, C_MSK + n * P:C_MSK + (n + 1) * P] = (
            (j // (2 * m) == i // (2 * m)) & (j % (2 * m) < m) & (i % (2 * m) >= m))
    n = len(LEVELS)
    t[:, C_MSK + n * P:C_MSK + (n + 1) * P] = np.eye(P)
    return t


def kernel(**inputs):
    import numpy as _np
    import concourse.bacc as _bacc
    from concourse import mybir as _mybir
    from concourse.bass_utils import run_bass_kernel_spmd as _run

    x = {k: _np.asarray(v) for k, v in inputs.items()}

    def tiles(w):
        n = w.shape[1] // P
        return w.reshape(KT, P, n, P).transpose(2, 1, 0, 3).reshape(n, P, D)

    def columns(v):
        return v.reshape(-1, P).T

    w_in = x["w_in"][0]
    starts = _np.cumsum([0, D, D, D, D // 2, D // 2, D, RANK, D, D, D])
    dq, dk, dv, gq, gk, gv, glr, gr, ga, gb = [w_in[:, a:b] for a, b in zip(starts[:-1], starts[1:])]
    w_all = _np.concatenate([tiles(w) for w in (dq, dk, dv, gq, gk, gv, gr, ga, gb, x["w_branch_a"][0],
                                                x["w_branch_b"][0], x["w_out"][0], x["peer_w_q"][0])])
    frames = _np.concatenate([x["x_prompt"][0], x["x_sample"][0]])
    qk = x["qk_norm_g"][0]
    lam = _np.zeros((P, 4), _np.float32)
    lam[:HD] = x["da_lambda"][0].T
    gains = _np.concatenate([
        columns(x["norm1_g"][0]), columns(x["norm2_g"][0]),
        _np.tile(_np.concatenate([qk[0], qk[0]])[:, None], (1, 8)),
        _np.tile(_np.concatenate([qk[1], qk[1]])[:, None], (1, 8)),
        columns(x["da_subln_g"][0]), columns(x["gla_norm_g"][0]), columns(x["gla_b_gate"][0]), lam], axis=1)
    arrays = {
        "xT": frames.T.reshape(KT, P, TOK).transpose(1, 0, 2).reshape(P, KT * TOK),
        "w_all": w_all,
        "gains": gains,
        "const": const_table(),
        "w_glr": glr.reshape(KT, P, RANK).transpose(1, 0, 2).reshape(P, KT * RANK),
        "w_gate": x["gla_w_gate2"][0],
        "ckT": x["cache_k"][0, 0].reshape(PAST, NH, P).transpose(2, 1, 0),
        "cv": x["cache_v"][0, 0].reshape(2, P, NH, P).transpose(1, 2, 0, 3).reshape(P, NH, PAST),
        "state_in": x["state_gla"][0, 0].transpose(1, 0, 2),
        "skT": x["peer_sub_keys"][0].reshape(2 * PH, N_KEYS, P).transpose(2, 0, 1).reshape(P, 2 * PH * N_KEYS),
        "u": x["peer_u"][0].reshape(N_KEYS, N_KEYS, KT, P).transpose(0, 3, 2, 1).reshape(N_KEYS, P, D),
        "v": x["peer_v"][0].reshape(N_KEYS, N_KEYS, D),
    }
    arrays = {k: _np.ascontiguousarray(v) for k, v in arrays.items()}

    nc = _bacc.Bacc("TRN2", target_bir_lowering=False, num_devices=1)
    A = {}
    for name, a in arrays.items():
        A[name] = nc.dram_tensor("in_" + name, a.shape, _mybir.dt.from_np(a.dtype), kind="ExternalInput").ap()
    for name in ("w_all", "u", "v"):
        A[name] = A[name].rearrange("t p n -> p t n")
    outs = {"kT_out": (D, TOK), "vT_out": (D, TOK), "yT_out": (D, TOK), "s_out": (2 * GH, P, 256)}
    for name, shape in outs.items():
        ap = nc.dram_tensor("out_" + name, shape, _mybir.dt.float32, kind="ExternalOutput").ap()
        A[name] = (ap.rearrange("h p n -> p h n") if name == "s_out"
                            else ap.rearrange("(k p) n -> p k n", p=P))
    A["gate"] = nc.dram_tensor("gate_by_expert", (N_KEYS, TOK // CHUNK_TOK, N_KEYS, CHUNK_TOK), _mybir.dt.float32,
                               kind="Internal").ap()
    h = nc.dram_tensor("early_gelu", (EARLY, N_KEYS, TOK), _mybir.dt.float32, kind="Internal").ap()
    A["h"] = h.rearrange("i j t -> j i t")
    build(nc, A)
    r = _run(nc, [{"in_" + k: v for k, v in arrays.items()}], core_ids=[0]).results[0]

    def by_frame(name, *shape):
        rows = _np.asarray(r["out_" + name]).T
        return rows[:SEQ].reshape(*shape[0]), rows[SEQ:].reshape(*shape[1])

    y_p, y_s = by_frame("yT_out", (1, SEQ, D), (1, DEC, D))
    k_p, k_s = by_frame("kT_out", (1, 1, SEQ, NH, 2, HD), (1, 1, DEC, NH, 2, HD))
    v_p, v_s = by_frame("vT_out", (1, 1, SEQ, NH, P), (1, 1, DEC, NH, P))
    s = _np.asarray(r["out_s_out"]).reshape(2, 1, 1, GH, P, 256)
    return y_p, y_s, k_p, v_p, s[0], k_s, v_s, s[1]
```

```python
from contextlib import ExitStack

import numpy as np

import concourse.bass as bass
from concourse import mybir

F32 = mybir.dt.float32
F32R = mybir.dt.float32r
U32 = mybir.dt.uint32
ALU = mybir.AluOpType
ACT = mybir.ActivationFunctionType
AX = mybir.AxisListType

P = 128
D = 1024
KT = D // P
SEQ = 512
DEC = 64
PAST = 256
TOK = SEQ + DEC
HALF = TOK // 2
NC_T = 5
NH = 8
HD = 64
GH = 4
EPS = 1e-6
NEG = -1e30
RANK = 16
LEVELS = [64, 32, 16, 8, 4, 2, 1]
CHUNK_TOK = 64
N_KEYS = 128
TOPK = 16
ROUTE_U = 6
EARLY = 72
CLOSING = 4
PH = 8
LAM_INIT = 0.2

T_Q, T_K, T_V, T_GLA = 0, 8, 16, 24
T_GA, T_WA, T_WB, T_WO, T_PQ, T_END = 48, 64, 72, 80, 88, 104

C_ID, C_BLK, C_ROT, C_IOTA, C_COS, C_SIN, C_RST, C_MSK = 0, 128, 256, 384, 512, 1088, 1664, 2240
N_MASK = len(LEVELS) + 1
C_END = C_MSK + N_MASK * P
G_N1, G_N2, G_QK, G_SUB, G_GLA, G_BG, G_LAM, G_END = 0, 8, 16, 32, 33, 35, 39, 43


def token_cols(c):
    return c * P, (P if c < 4 else DEC)


def bcast(ap, axis, n):
    ap = ap.unsqueeze(axis)
    shape = list(ap.shape)
    shape[axis] = n
    return ap.to_broadcast(shape)


def apart(eng, S):
    eng.sem_inc(S["passed"], 1)


def load_w(sp, S, i, c):
    t = 2 * i + c
    if not (isinstance(t, int) and t < 2):
        sp.wait_ge(S["w_split"], t - 1)
    sp.dma_start(S["w_raw"][:, c % 2, :], S["w_all"][:, bass.ds(t, 1), :]).then_inc(S["w_loaded"][c % 2], 16)


def split_hi(nc, act, S, i, c):
    u, t = c % 2, 2 * i + c
    act.wait_ge(S["w_loaded"][u], 16 * (i + c // 2 + 1))
    if not (isinstance(t, int) and t < 2):
        act.wait_ge(S["tile_done"], t - 1)
    nc.scalar.activation(S["w_hi"][:, u, :], S["w_raw"][:, u, :], ACT.Copy).then_inc(S["w_hi_done"], 1)


def split_lo(nc, dve, S, i, c):
    u, t = c % 2, 2 * i + c
    dve.wait_ge(S["w_hi_done"], t + 1)
    nc.vector.tensor_tensor(S["w_lo"][:, u, :], S["w_raw"][:, u, :], S["w_hi"][:, u, :].bitcast(F32),
                            ALU.subtract).then_inc(S["w_split"], 1)


def product3(nc, out, wh, wl, xh, xl, first, last):
    nc.tensor.matmul(out, wh, xh, start=first, stop=False)
    nc.tensor.matmul(out, wh, xl, start=False, stop=False)
    return nc.tensor.matmul(out, wl, xh, start=False, stop=last)


def dense_tile(nc, pe, S, i, c, source="x", x_before=None):
    u, t = c % 2, 2 * i + c
    pe.wait_ge(S["w_split"], t + 1)
    if not (isinstance(t, int) and t < 2):
        pe.wait_ge(S["evacuated"], t - 1)
    for f in range(2):
        cols = slice(f * HALF, (f + 1) * HALF)
        for k in range(KT):
            w = slice(k * P, (k + 1) * P)
            if x_before is not None and f == 0:
                pe.wait_ge(S["x_split"], x_before + k + 1)
            ins = product3(nc, S["mm"][u][:, f, 0:HALF], S["w_hi"][:, u, w], S["w_lo"][:, u, w],
                           S[source + "_hi"][:, k, cols], S[source + "_lo"][:, k, cols], k == 0, k == KT - 1)
    ins.then_inc(S["tile_done"], 1)


def halves(ap):
    return ap.rearrange("p (f n) -> p f n", f=2)


def feat(S, j):
    return S["big"][:, bass.ds(j * TOK, TOK)]


def row(ap, k):
    return ap[:, bass.ds(k, 1), :].rearrange("p k n -> p (k n)")


def activation_hi(nc, act, S, name, k, src):
    nc.scalar.activation(row(S[name + "_hi"], k), src, ACT.Copy).then_inc(S["x_hi_done"], 1)


def activation_lo(nc, dve, S, name, k, src, before):
    dve.wait_ge(S["x_hi_done"], before + k + 1)
    nc.vector.tensor_tensor(row(S[name + "_lo"], k), src, row(S[name + "_hi"], k).bitcast(F32),
                            ALU.subtract).then_inc(S["x_split"], 1)


def matmul_tok(nc, out, lhsT, rhs, first, last):
    nc.tensor.matmul(out[:, 0, 0:HALF], lhsT, rhs[:, 0:HALF], start=first, stop=last)
    return nc.tensor.matmul(out[:, 1, 0:HALF], lhsT, rhs[:, HALF:TOK], start=first, stop=last)


def as3(ap):
    return ap.rearrange("p (k n) -> p k n", n=TOK)


def res_tile(S, k):
    return S["res"][:, bass.ds(k * TOK, TOK)]


def rms_square(nc, act, S, k):
    nc.scalar.activation(feat(S, k), res_tile(S, k), ACT.Square).then_inc(S["n_sq"], 1)


def rms_sum(nc, pe, S, r, k, first=False, last=False):
    pe.wait_ge(S["n_sq"], KT * r + k + 1)
    ins = matmul_tok(nc, S["aux"], S["ones"][:, :], feat(S, k), first, last)
    if last:
        ins.then_inc(S["n_sum"], 1)


def rms_root(nc, act, S, r):
    act.wait_ge(S["n_sum"], r + 1)
    nc.scalar.activation(halves(S["root"][:, :]), S["aux"][:, :, 0:HALF], ACT.Sqrt, bias=S["eps"][:, 0:1],
                         scale=1.0 / D).then_inc(S["n_root"], 1)


def rms_apply(nc, dve, S, r, gain, before):
    dve.wait_ge(S["n_root"], r + 1)
    nc.vector.reciprocal(S["rinv"][:, :], S["root"][:, :]).then_inc(S["n_rinv"], 1)
    dve.wait_ge(S["n_rinv"], r + 1)
    for k in range(KT + 1):
        if k < KT:
            nc.vector.scalar_tensor_tensor(out=feat(S, 8 + k), in0=res_tile(S, k),
                                           scalar=S["gains"][:, gain + k:gain + k + 1], in1=S["rinv"][:, :],
                                           op0=ALU.mult, op1=ALU.mult).then_inc(S["n_done"], 1)
        if k > 0:
            activation_lo(nc, dve, S, "x", k - 1, feat(S, 8 + k - 1), before)


def rms_split_hi(nc, act, S, r):
    for k in range(KT):
        act.wait_ge(S["n_done"], KT * r + k + 1)
        activation_hi(nc, act, S, "x", k, feat(S, 8 + k))


FROM_ONE = {
    "tensor": "a_turned a_pv g_at g_kT g_o g_osum t_turned e_mm e_mm y_mm",
    "scalar": "a_exp a_wT g_root o_root t_tab e_out e_out u_gel u_gel",
    "vector": "a_w g_fin g_gated g_oc o_done o_evac q_roped q_rsin r_top t_ij y_add y_add",
    "gpsimd": "r_kept",
    "sync": "g_out",
}


def start_at_one(eng, S, engine):
    for name in FROM_ONE[engine].split():
        eng.sem_inc(S[name], 1)


def stage_norm1(nc, S, A):
    with nc.Block() as block:
        @block.sync
        def _(sp):
            for k in range(KT):
                sp.dma_start(res_tile(S, k), A["xT"][:, k * TOK:(k + 1) * TOK]).then_inc(S["x_in"][k], 16)
            start_at_one(sp, S, "sync")
            for store in S["e_store"] + S["h_out"] + S["z_out"] + S["z_in"]:
                sp.sem_inc(store, 1)
            for dst, src in ((S["gains"][:, :], A["gains"]), (S["const"][:, :], A["const"]),
                             (S["w_glr"][:, :], A["w_glr"]), (S["w_gate"][0:RANK, :], A["w_gate"])):
                sp.dma_start(dst, src).then_inc(S["c_in"], 16)
            load_w(sp, S, 0, 0)
            load_w(sp, S, 0, 1)
            load_w(sp, S, 0, 2)

        @block.scalar
        def _(act):
            start_at_one(act, S, "scalar")
            for k in range(KT):
                act.wait_ge(S["x_in"][k], 16)
                rms_square(nc, act, S, k)
            rms_root(nc, act, S, 0)
            split_hi(nc, act, S, 0, 0)
            rms_split_hi(nc, act, S, 0)
            act.wait_ge(S["lam_sum"], 1)
            nc.scalar.activation(S["lam"][:, 2:4], S["aux2"][:, 0, 0:2], ACT.Exp).then_inc(S["lam_exp"], 1)
            act.wait_ge(S["glr_mm"], 1)
            nc.scalar.activation(halves(S["glr"][0:RANK, :]), S["aux"][0:RANK, :, 0:HALF],
                                 ACT.Copy).then_inc(S["glr_done"], 1)

        @block.vector
        def _(dve):
            start_at_one(dve, S, "vector")
            nc.vector.memset(S["ones"][:, :], 1.0).then_inc(S["d_init"], 1)
            nc.vector.memset(S["eps"][:, :], EPS).then_inc(S["d_init"], 1)
            dve.wait_ge(S["c_in"], 64)
            nc.vector.tensor_tensor(S["lam"][0:HD, 0:1], S["gains"][0:HD, G_LAM:G_LAM + 1],
                                    S["gains"][0:HD, G_LAM + 1:G_LAM + 2], ALU.mult).then_inc(S["d_init"], 1)
            nc.vector.tensor_tensor(S["lam"][0:HD, 1:2], S["gains"][0:HD, G_LAM + 2:G_LAM + 3],
                                    S["gains"][0:HD, G_LAM + 3:G_LAM + 4], ALU.mult).then_inc(S["d_init"], 1)
            nc.vector.tensor_scalar(S["gqk"][:, 0:8], S["gains"][:, G_QK:G_QK + 8], HD ** -0.5, None,
                                    ALU.mult).then_inc(S["d_init"], 1)
            nc.vector.tensor_copy(S["gqk"][:, 8:16], S["gains"][:, G_QK + 8:G_QK + 16]).then_inc(S["d_init"], 1)
            nc.vector.tensor_scalar(S["gsub"][:, :], S["gains"][:, G_SUB:G_SUB + 1], 1.0 - LAM_INIT, None,
                                    ALU.mult).then_inc(S["d_init"], 1)
            for k in range(KT):
                dve.wait_ge(S["x_in"][k], 16)
            split_lo(nc, dve, S, 0, 0)
            rms_apply(nc, dve, S, 0, G_N1, 0)
            dve.wait_ge(S["lam_exp"], 1)
            nc.vector.tensor_tensor(S["lam"][:, 4:5], S["lam"][:, 3:4], S["lam"][:, 2:3],
                                    ALU.subtract).then_inc(S["lam_d"], 1)
            dve.wait_ge(S["lam_d"], 1)
            nc.vector.tensor_scalar(S["neglam"][:, :], S["lam"][:, 4:5], LAM_INIT, None,
                                    ALU.subtract).then_inc(S["lam_d"], 1)

        @block.gpsimd
        def _(pool):
            start_at_one(pool, S, "gpsimd")

        @block.tensor
        def _(pe):
            start_at_one(pe, S, "tensor")
            pe.wait_ge(S["d_init"], 2)
            for k in range(KT):
                rms_sum(nc, pe, S, 0, k, k == 0, k == KT - 1)
            pe.wait_ge(S["d_init"], 4)
            nc.tensor.matmul(S["aux2"][:, 0, 0:2], S["ones"][0:HD, :], S["lam"][0:HD, 0:2], start=True,
                             stop=True).then_inc(S["lam_sum"], 1)
            dense_tile(nc, pe, S, 0, 0, x_before=0)
            pe.wait_ge(S["n_done"], KT)
            pe.wait_ge(S["n_root"], 1)
            for k in range(KT):
                ins = matmul_tok(nc, S["aux"][0:RANK], S["w_glr"][:, k * RANK:(k + 1) * RANK],
                                 S["big"][:, (8 + k) * TOK:(9 + k) * TOK], k == 0, k == KT - 1)
            ins.then_inc(S["glr_mm"], 1)


def stage_qkv(nc, S, A):
    with nc.Block() as block:
        @block.sync
        def _(sp):
            with sp.Fori(0, 12) as i:
                load_w(sp, S, i, 3)
                load_w(sp, S, i, 4)

        def hi_square_root(act, i, u, square=True, root=True):
            t = 2 * i + u
            split_hi(nc, act, S, i, u + 1)
            if square:
                act.wait_ge(S["evacuated"], t + 1)
                if not isinstance(t, int):
                    act.wait_ge(S["q_sum"], t - 1)
                nc.scalar.activation(S["sq"][:, u, :], feat(S, t), ACT.Square).then_inc(S["q_sq"], 1)
            if root:
                act.wait_ge(S["q_sum"], t)
                if not (isinstance(t, int) and t < 2):
                    act.wait_ge(S["q_norm"], t - 1)
                nc.scalar.activation(halves(S["root"][:, :]), S["aux"][:, :, 0:HALF], ACT.Sqrt,
                                     bias=S["eps"][:, 0:1], scale=1.0 / HD).then_inc(S["q_root"], 1)

        @block.scalar
        def _(act):
            hi_square_root(act, 0, 0, root=False)
            hi_square_root(act, 0, 1)
            with act.Fori(1, 8) as i:
                hi_square_root(act, i, 0)
                hi_square_root(act, i, 1)
            hi_square_root(act, 8, 0, square=False)
            hi_square_root(act, 8, 1, square=False, root=False)
            with act.Fori(9, 12) as i:
                split_hi(nc, act, S, i, 1)
                split_hi(nc, act, S, i, 2)

        def evacuate(dve, i, u):
            t = 2 * i + u
            split_lo(nc, dve, S, i, u + 1)
            dve.wait_ge(S["tile_done"], t + 1)
            nc.vector.tensor_copy(halves(feat(S, t)), S["mm"][u][:, :, 0:HALF]).then_inc(S["evacuated"], 1)

        def norm(dve, i, u):
            n = 2 * i + u
            dve.wait_ge(S["q_root"], n + 1)
            dve.wait_ge(S["q_norm"], n)
            nc.vector.reciprocal(S["rinv"][:, :], S["root"][:, :]).then_inc(S["q_rinv"], 1)
            dve.wait_ge(S["q_rinv"], n + 1)
            nc.vector.scalar_tensor_tensor(out=S["nq"][:, u, :], in0=feat(S, n), scalar=S["gqk"][:, bass.ds(n, 1)],
                                           in1=S["rinv"][:, :], op0=ALU.mult,
                                           op1=ALU.mult).then_inc(S["q_norm"], 1)

        def rotate(dve, i, u):
            n = 2 * i + u
            dve.wait_ge(S["q_swap"], n + 1)
            dve.wait_ge(S["q_roped"], 1 + n)
            nc.vector.tensor_tensor(halves(S["rsin"][:, :]), S["aux2"][:, :, 0:HALF],
                                    halves(S["const"][:, C_SIN:C_SIN + TOK]), ALU.mult).then_inc(S["q_rsin"], 1)
            dve.wait_ge(S["q_rsin"], 1 + n + 1)
            dve.wait_ge(S["q_cos"], n + 1)
            nc.vector.tensor_tensor(feat(S, n), S["rsin"][:, :], S["ncos"][:, u, :],
                                    ALU.add).then_inc(S["q_roped"], 1)

        @block.vector
        def _(dve):
            evacuate(dve, 0, 0)
            evacuate(dve, 0, 1)
            norm(dve, 0, 0)
            with dve.Fori(1, 8) as i:
                evacuate(dve, i, 0)
                norm(dve, i - 1, 1)
                rotate(dve, i - 1, 0)
                evacuate(dve, i, 1)
                norm(dve, i, 0)
                rotate(dve, i - 1, 1)
            evacuate(dve, 8, 0)
            norm(dve, 7, 1)
            rotate(dve, 7, 0)
            evacuate(dve, 8, 1)
            rotate(dve, 7, 1)
            with dve.Fori(9, 12) as i:
                evacuate(dve, i, 0)
                evacuate(dve, i, 1)

        @block.gpsimd
        def _(pool):
            def ncos(i, u):
                n = 2 * i + u
                pool.wait_ge(S["q_norm"], n + 1)
                if not isinstance(n, int):
                    pool.wait_ge(S["q_roped"], 1 + n - 1)
                    apart(pool, S)
                nc.gpsimd.tensor_tensor(S["ncos"][:, u, :], S["nq"][:, u, :], S["const"][:, C_COS:C_COS + TOK],
                                        ALU.mult).then_inc(S["q_cos"], 1)
            ncos(0, 0)
            ncos(0, 1)
            with pool.Fori(1, 8) as i:
                ncos(i, 0)
                ncos(i, 1)

        def head_sum(pe, i, u):
            n = 2 * i + u
            pe.wait_ge(S["q_sq"], n + 1)
            if not (isinstance(n, int) and n < 1):
                pe.wait_ge(S["q_root"], n)
            matmul_tok(nc, S["aux"], S["const"][:, C_BLK:C_BLK + P], S["sq"][:, u, :], True, True).then_inc(S["q_sum"], 1)

        def swap(pe, i, u):
            n = 2 * i + u
            pe.wait_ge(S["q_norm"], n + 1)
            if not (isinstance(n, int) and n < 1):
                pe.wait_ge(S["q_rsin"], 1 + n)
            matmul_tok(nc, S["aux2"], S["const"][:, C_ROT:C_ROT + P], S["nq"][:, u, :], True, True).then_inc(S["q_swap"], 1)

        @block.tensor
        def _(pe):
            pe.wait_ge(S["x_split"], KT)
            dense_tile(nc, pe, S, 0, 1)
            head_sum(pe, 0, 0)
            with pe.Fori(1, 8) as i:
                dense_tile(nc, pe, S, i, 0)
                head_sum(pe, i - 1, 1)
                swap(pe, i - 1, 0)
                dense_tile(nc, pe, S, i, 1)
                head_sum(pe, i, 0)
                swap(pe, i - 1, 1)
            dense_tile(nc, pe, S, 8, 0)
            head_sum(pe, 7, 1)
            swap(pe, 7, 0)
            dense_tile(nc, pe, S, 8, 1)
            swap(pe, 7, 1)
            with pe.Fori(9, 12) as i:
                dense_tile(nc, pe, S, i, 0)
                dense_tile(nc, pe, S, i, 1)


def stage_attention(nc, S, A, B):
    keys = [P * (j + 1) for j in range(4)] + [PAST + DEC]
    dense_bank = S["mm"][1]
    w0 = T_GLA // 2

    def tile_args(i, u, k):
        return w0 + 3 * i, 3 * u + k

    with nc.Block() as block:
        @block.sync
        def _(sp):
            sp.dma_start(A["kT_out"], as3(S["big"][:, 8 * TOK:16 * TOK])).then_inc(S["out_kv"], 16)
            sp.dma_start(A["vT_out"], as3(S["big"][:, 16 * TOK:24 * TOK])).then_inc(S["out_kv"], 16)
            def cache(i, u):
                h = 2 * i + u
                if not isinstance(h, int):
                    sp.wait_ge(S["a_pv"], 1 + 5 * (h - 1))
                sp.dma_start(B["ck"][:, u, :], A["ckT"][:, bass.ds(h, 1), :]).then_inc(S["a_cache"][u], 16)
                sp.dma_start(B["cv"][:, u, :], A["cv"][:, bass.ds(h, 1), :]).then_inc(S["a_cache"][u], 16)
            cache(0, 0)
            cache(0, 1)
            with sp.Fori(0, 3) as i:
                for u in range(2):
                    for k in range(3):
                        load_w(sp, S, *tile_args(i, u, k + 3))
                    cache(i + 1, u)
            for u in range(2):
                for k in range(3):
                    load_w(sp, S, *tile_args(3, u, k + 3))

        @block.gpsimd
        def _(pool):
            def stage(i, u):
                h = 2 * i + u
                if not isinstance(h, int):
                    pool.wait_ge(S["a_pv"], 1 + 5 * (h - 1))
                    apart(pool, S)
                for dst, j in ((B["qs"], 0), (B["ks"], 8), (B["vs"], 16)):
                    nc.gpsimd.tensor_copy(dst[:, u, :], feat(S, h + j)).then_inc(S["a_staged"], 1)
            stage(0, 0)
            stage(0, 1)
            with pool.Fori(1, 4) as i:
                stage(i, 0)
                stage(i, 1)

        @block.tensor
        def _(pe):
            def scores(i, u, j):
                h = 2 * i + u
                if j == 0:
                    pe.wait_ge(S["a_staged"], 3 * (h + 1))
                pe.wait_ge(S["a_exp"], 1 + 5 * h + j)
                apart(pe, S)
                q0, nq = token_cols(j)
                for m in range(2):
                    rows = slice(HD * m, HD * (m + 1))
                    q = B["qs"][rows, u, q0:q0 + nq]
                    out = B["s"][0:nq, m]
                    if j < 4:
                        ins = nc.tensor.matmul(out[:, 0:keys[j]], q, B["ks"][rows, u, 0:keys[j]],
                                               start=True, stop=True)
                    else:
                        pe.wait_ge(S["a_cache"][u], 32 * (i + 1))
                        apart(pe, S)
                        nc.tensor.matmul(out[:, 0:PAST], q, B["ck"][rows, u, :], start=True, stop=True)
                        ins = nc.tensor.matmul(out[:, PAST:PAST + DEC], q, B["ks"][rows, u, SEQ:TOK],
                                               start=True, stop=True)
                ins.then_inc(S["a_scores"], 1)

            def turn_v(i, u):
                h = 2 * i + u
                pe.wait_ge(S["a_wT"], 1 + 5 * h)
                for c in range(NC_T):
                    t0, n = token_cols(c)
                    out = B["tr"][0][:, t0:t0 + P] if c < 4 else B["tr"][1][0:DEC, 0:P]
                    ins = nc.tensor.transpose(out, B["vs"][:, u, t0:t0 + n], S["ident"])
                ins.then_inc(S["a_vT"], 1)

            def turn_w(i, u, j):
                h = 2 * i + u
                pe.wait_ge(S["a_w"], 1 + 5 * h + j + 1)
                if j < 2:
                    pe.wait_ge(S["a_vtok"], 2 * (h + 1))
                else:
                    pe.wait_ge(S["a_wT"], 1 + 5 * h + j - 1)
                apart(pe, S)
                nq = token_cols(j)[1]
                for k in range((keys[j] + P - 1) // P):
                    nk = min(P, keys[j] - k * P)
                    ins = nc.tensor.transpose(B["tr"][j % 2][0:nk, k * nq:(k + 1) * nq],
                                              B["w"][0:nq, j % 2, k * P:k * P + nk], S["ident"][0:nq, 0:nq])
                ins.then_inc(S["a_turned"], 1)

            def times_v(i, u, j):
                h = 2 * i + u
                pe.wait_ge(S["a_wT"], 1 + 5 * h + j + 1)
                if j == 0:
                    pe.wait_ge(S["a_vtok"], 2 * (h + 1))
                    pe.wait_ge(S["o_root"], 1 + h)
                nq = token_cols(j)[1]
                n_k = (keys[j] + P - 1) // P
                for k in range(n_k):
                    w = B["wT"][:, j % 2, k * nq:(k + 1) * nq]
                    if j < 4:
                        out, v = B["o"][:, 0, j * P:(j + 1) * P], B["vtok"][:, u, k * P:(k + 1) * P]
                    else:
                        out = B["o"][:, 1, 0:DEC]
                        v = B["cv"][:, u, k * P:(k + 1) * P] if k < 2 else B["vtok"][0:DEC, u, SEQ:SEQ + P]
                        w = w if k < 2 else w[0:DEC]
                    ins = nc.tensor.matmul(out, v, w, start=k == 0, stop=k == n_k - 1)
                ins.then_inc(S["a_pv"], 1)

            def dense_half(i, u, n):
                t, f = T_GLA + 6 * i + 3 * u + n // 2, n % 2
                slot = (3 * u + n // 2) % 2
                if f == 0:
                    pe.wait_ge(S["w_split"], t + 1)
                    pe.wait_ge(S["evacuated"], t)
                cols = slice(f * HALF, (f + 1) * HALF)
                for k in range(KT):
                    w = slice(k * P, (k + 1) * P)
                    ins = product3(nc, dense_bank[:, f, 0:HALF], S["w_hi"][:, slot, w], S["w_lo"][:, slot, w],
                                   S["x_hi"][:, k, cols], S["x_lo"][:, k, cols], k == 0, k == KT - 1)
                if f == 1:
                    ins.then_inc(S["tile_done"], 1)

            with pe.Fori(0, 4) as i:
                for u in range(2):
                    scores(i, u, 0)
                    turn_v(i, u)
                    dense_half(i, u, 0)
                    for j in range(5):
                        if j < 4:
                            scores(i, u, j + 1)
                        turn_w(i, u, j)
                        if j < 4:
                            dense_half(i, u, j + 1)
                        times_v(i, u, j)
                    dense_half(i, u, 5)
                    pe.wait_ge(S["o_sq"], 2 * i + u + 1)
                    nc.tensor.matmul(B["o"][:, 0, :], S["ones"][:, :], B["osq"][:, 0:SEQ], start=True, stop=True)
                    nc.tensor.matmul(B["o"][:, 1, 0:DEC], S["ones"][:, :], B["osq"][:, SEQ:TOK], start=True,
                                     stop=True).then_inc(S["o_sum"], 1)

        @block.scalar
        def _(act):
            def exps(i, u, j):
                n = 5 * (2 * i + u) + j
                act.wait_ge(S["a_max"], n + 1)
                nq = token_cols(j)[1]
                act.wait_ge(S["a_w"], 1 + (n - j if j < 2 else n - 1))
                for m in range(2):
                    ins = nc.scalar.activation(B["p"][0:nq, j % 2, m, 0:keys[j]], B["s"][0:nq, m, 0:keys[j]],
                                               ACT.Exp, bias=B["nmax"][0:nq, j % 2, m:m + 1],
                                               accum_out=B["z"][0:nq, j % 2, m:m + 1])
                ins.then_inc(S["a_exp"], 1)

            def evac_wT(i, u, j):
                n = 5 * (2 * i + u) + j
                act.wait_ge(S["a_turned"], 1 + n + 1)
                act.wait_ge(S["a_pv"], 1 + (n - j if j < 2 else n - 1))
                if j < 4:
                    nc.scalar.activation(B["wT"][:, j % 2, 0:keys[j]], B["tr"][j % 2][:, 0:keys[j]],
                                         ACT.Copy).then_inc(S["a_wT"], 1)
                else:
                    nc.scalar.activation(B["wT"][:, 0, 0:2 * DEC], B["tr"][0][:, 0:2 * DEC], ACT.Copy)
                    nc.scalar.activation(B["wT"][0:DEC, 0, 2 * DEC:3 * DEC], B["tr"][0][0:DEC, 2 * DEC:3 * DEC],
                                         ACT.Copy).then_inc(S["a_wT"], 1)

            with act.Fori(0, 4) as i:
                for u in range(2):
                    h = 2 * i + u
                    act.wait_ge(S["a_vT"], h + 1)
                    nc.scalar.activation(B["vtok"][:, u, 0:SEQ], B["tr"][0][:, :], ACT.Copy).then_inc(S["a_vtok"], 1)
                    nc.scalar.activation(B["vtok"][0:DEC, u, SEQ:SEQ + P], B["tr"][1][0:DEC, 0:P],
                                         ACT.Copy).then_inc(S["a_vtok"], 1)
                    exps(i, u, 0)
                    split_hi(nc, act, S, *tile_args(i, u, 1))
                    for j in range(5):
                        evac_wT(i, u, j)
                        if j < 4:
                            exps(i, u, j + 1)
                        if j == 1:
                            split_hi(nc, act, S, *tile_args(i, u, 2))
                        if j == 2:
                            act.wait_ge(S["tile_done"], T_GLA + 3 * h + 2)
                            act.wait_ge(S["out_kv"], 32)
                            nc.scalar.activation(halves(feat(S, 2 * NH + h)), dense_bank[:, :, 0:HALF],
                                                 ACT.Silu).then_inc(S["evacuated"], 1)
                            split_hi(nc, act, S, *tile_args(i, u, 3))
                    act.wait_ge(S["o_evac"], 1 + h + 1)
                    nc.scalar.activation(B["osq"][:, :], B["osb"][:, :], ACT.Square).then_inc(S["o_sq"], 1)
                    act.wait_ge(S["o_sum"], h + 1)
                    nc.scalar.activation(S["root"][:, 0:SEQ], B["o"][:, 0, :], ACT.Sqrt, bias=S["eps"][:, 0:1],
                                         scale=1.0 / P)
                    nc.scalar.activation(S["root"][:, SEQ:TOK], B["o"][:, 1, 0:DEC], ACT.Sqrt,
                                         bias=S["eps"][:, 0:1], scale=1.0 / P).then_inc(S["o_root"], 1)

        @block.vector
        def _(dve):
            def neg_max(i, u, j):
                n = 5 * (2 * i + u) + j
                dve.wait_ge(S["a_scores"], n + 1)
                nq = token_cols(j)[1]
                if j < 4:
                    nc.vector.memset(B["s"][0:HD, :, P * j + HD:P * (j + 1)], NEG).then_inc(S["a_mask"], 1)
                    dve.wait_ge(S["a_mask"], 4 * (2 * i + u) + j + 1)
                nc.vector.tensor_reduce(B["nmax"][0:nq, j % 2, :], B["s"][0:nq, :, 0:keys[j]], AX.X, ALU.max,
                                        negate=True).then_inc(S["a_max"], 1)

            def weights(i, u, j):
                n = 5 * (2 * i + u) + j
                nq = token_cols(j)[1]
                dve.wait_ge(S["a_exp"], 1 + n + 1)
                dve.wait_ge(S["a_w"], 1 + (n - j if j < 2 else n - 1))
                nc.vector.reciprocal(B["rz"][0:nq, j % 2, :], B["z"][0:nq, j % 2, :]).then_inc(S["a_rz"], 1)
                dve.wait_ge(S["a_rz"], 2 * n + 1)
                nc.vector.tensor_scalar(B["rz2"][0:nq, j % 2, 0:1], B["rz"][0:nq, j % 2, 1:2], S["neglam"][0:nq, 0:1], None,
                                        ALU.mult).then_inc(S["a_rz"], 1)
                dve.wait_ge(S["a_turned"], 1 + (n - j if j < 2 else n - 1))
                k = slice(0, keys[j])
                nc.vector.tensor_scalar(B["w"][0:nq, j % 2, k], B["p"][0:nq, j % 2, 0, k], B["rz"][0:nq, j % 2, 0:1], None,
                                        ALU.mult).then_inc(S["a_w1"], 1)
                dve.wait_ge(S["a_rz"], 2 * n + 2)
                dve.wait_ge(S["a_w1"], n + 1)
                nc.vector.scalar_tensor_tensor(out=B["w"][0:nq, j % 2, k], in0=B["p"][0:nq, j % 2, 1, k],
                                               scalar=B["rz2"][0:nq, j % 2, 0:1], in1=B["w"][0:nq, j % 2, k],
                                               op0=ALU.mult, op1=ALU.add).then_inc(S["a_w"], 1)

            def evacuate(h, t, place):
                dve.wait_ge(S["tile_done"], t + 1)
                nc.vector.tensor_copy(halves(feat(S, place + h)), dense_bank[:, :, 0:HALF]).then_inc(S["evacuated"], 1)

            with dve.Fori(0, 4) as i:
                for u in range(2):
                    h = 2 * i + u
                    neg_max(i, u, 0)
                    for j in range(5):
                        weights(i, u, j)
                        if j == 1:
                            evacuate(h, T_GLA + 3 * h, 0)
                        if j < 4:
                            neg_max(i, u, j + 1)
                        if j in (0, 2, 3):
                            split_lo(nc, dve, S, *tile_args(i, u, {0: 1, 2: 2, 3: 3}[j]))
                    dve.wait_ge(S["a_pv"], 1 + 5 * (h + 1))
                    dve.wait_ge(S["o_done"], 1 + h)
                    nc.vector.tensor_copy(B["osb"][:, 0:SEQ], B["o"][:, 0, :])
                    nc.vector.tensor_copy(B["osb"][:, SEQ:TOK], B["o"][:, 1, 0:DEC]).then_inc(S["o_evac"], 1)
                    dve.wait_ge(S["out_kv"], 32)
                    evacuate(h, T_GLA + 3 * h + 2, NH)
                    dve.wait_ge(S["o_root"], 1 + h + 1)
                    nc.vector.reciprocal(S["rinv"][:, :], S["root"][:, :]).then_inc(S["o_rinv"], 1)
                    dve.wait_ge(S["o_rinv"], h + 1)
                    nc.vector.scalar_tensor_tensor(out=S["res"][:, bass.ds(h * TOK, TOK)], in0=B["osb"][:, :],
                                                   scalar=S["gsub"][:, 0:1], in1=S["rinv"][:, :],
                                                   op0=ALU.mult, op1=ALU.mult).then_inc(S["o_done"], 1)


def stage_gla(nc, S, A, G):
    dk_scale = float(P) ** -0.5
    tau = 1.0 / 16.0
    n_lv = len(LEVELS)
    dense_banks = [S["mm"][0], S["mm"][1], S["aux"], S["aux2"]]
    staging = [S["rsin"], S["glr"]]
    w0 = T_GA // 2

    with nc.Block() as block:
        @block.sync
        def _(sp):
            with sp.Fori(0, GH) as h:
                sp.wait_ge(S["g_o"], 1 + 2 * h)
                apart(sp, S)
                sp.wait_ge(S["g_fin"], 1 + h)
                apart(sp, S)
                sp.dma_start(G["st"][:, 4, :], A["state_in"][:, bass.ds(h, 1), :]).then_inc(S["g_state"], 16)
                for k in range(4):
                    t = T_GA + 4 * h + k
                    load_w(sp, S, w0 + 2 * h, k + 3)
                    sp.wait_ge(S["evacuated"], t + 1)
                    sp.dma_start(A["z"][:, bass.ds(4 * h + k, 1), :], staging[k % 2][:, :]).then_inc(S["z_out"][k % 2], 16)
                sp.wait_ge(S["g_chain"], 4 * h + 4)
                apart(sp, S)
                sp.dma_start(A["s_out"][:, bass.ds(h, 1), :], G["st"][:, 0, :]).then_inc(S["g_out"], 16)
                sp.wait_ge(S["g_fin"], 1 + h + 1)
                apart(sp, S)
                sp.dma_start(A["s_out"][:, bass.ds(h + GH, 1), :], G["s_fin"][:, :]).then_inc(S["g_out"], 16)
            for z in S["z_out"]:
                sp.wait_ge(z, 1 + 16 * 2 * GH)

        @block.gpsimd
        def _(pool):
            with pool.Fori(0, GH) as h:
                pool.wait_ge(S["g_osum"], 1 + h)
                apart(pool, S)
                for v in range(2):
                    nc.gpsimd.tensor_copy(G["vs"][:, v, :], feat(S, 8 + 2 * h + v)).then_inc(S["g_vs"], 1)
                for n in range(n_lv + 2):
                    s = n % 2
                    w = SEQ if n == 0 else TOK
                    if n != n_lv:
                        pool.wait_ge(S["g_e"], (n_lv + 1) * h + min(n, n_lv) + 1 if n < n_lv else (n_lv + 1) * (h + 1))
                    if n >= 2:
                        pool.wait_ge(S["g_at"], 1 + n_lv * h + h + n - 1)
                    else:
                        pool.wait_ge(S["g_kT"], 1 + h)
                    apart(pool, S)
                    k = S["big"][:, bass.ds((GH + h) * TOK, w)]
                    if n == n_lv:
                        nc.gpsimd.tensor_copy(G["kl"][:, s, 0:w], k).then_inc(S["g_kl"], 1)
                    else:
                        nc.gpsimd.tensor_tensor(G["kl"][:, s, 0:w], k, G["e"][:, s, 0:w], ALU.mult).then_inc(S["g_kl"], 1)

        @block.scalar
        def _(act):
            act.wait_ge(S["g_z"], GH)
            for h in range(GH):
                pb = [S["mm"][0], S["mm"][1], S["aux"], S["aux2"]][h]
                ins = nc.scalar.activation(halves(G["b"][:, h * TOK:(h + 1) * TOK]), pb[:, :, 0:HALF], ACT.Identity,
                                           bias=S["gains"][:, G_BG + h:G_BG + h + 1])
            ins.then_inc(S["g_zb"], 1)
            act.wait_ge(S["g_zb"], 1)
            nc.scalar.activation(G["la"][:, :], G["b"][:, :], ACT.Abs).then_inc(S["g_la"], 1)
            act.wait_ge(S["g_la"], 1)
            nc.scalar.activation(G["la"][:, :], G["la"][:, :], ACT.Exp, scale=-1.0).then_inc(S["g_la"], 1)
            act.wait_ge(S["g_la"], 2)
            nc.scalar.activation(G["la"][:, :], G["la"][:, :], ACT.Ln, bias=1.0).then_inc(S["g_la"], 1)
            def evacuate(h, k):
                act.wait_ge(S["tile_done"], T_GA + 4 * h + k + 1)
                act.wait_ge(S["z_out"][k % 2], 1 + 16 * (2 * h + k // 2))
                nc.scalar.activation(halves(staging[k % 2][:, :]), dense_banks[k][:, :, 0:HALF],
                                     ACT.Copy).then_inc(S["evacuated"], 1)

            with act.Fori(0, GH) as h:
                bh = G["b"][:, bass.ds(h * TOK, TOK)]
                split_hi(nc, act, S, w0 + 2 * h, 1)
                act.wait_ge(S["g_cum"], GH)
                act.wait_ge(S["g_at"], 1 + (n_lv + 1) * h)
                act.wait_ge(S["g_gated"], 1 + 2 * h)
                nc.scalar.activation(G["qb"][:, :], bh, ACT.Exp, scale=tau).then_inc(S["g_eb"], 1)
                bl = G["b"][:, bass.ds(h * TOK, SEQ)].rearrange("p (c n) -> p c n", n=P)[:, :, P - 1]
                nc.scalar.activation(G["el"][:, 0:4], bl, ACT.Exp, scale=tau).then_inc(S["g_eb"], 1)
                nc.scalar.activation(G["el"][:, 4:5], G["b"][:, bass.ds(h * TOK + TOK - 1, 1)], ACT.Exp,
                                     scale=tau).then_inc(S["g_eb"], 1)
                evacuate(h, 0)
                split_hi(nc, act, S, w0 + 2 * h, 2)
                for v in range(2):
                    act.wait_ge(S["g_vT"], 2 * h + v + 1)
                    tr = [S["aux"], S["aux2"]][v]
                    cols = slice(v * P, (v + 1) * P)
                    nc.scalar.activation(G["vt"][:, 0:4, cols], tr[:, 0, :].rearrange("p (c n) -> p c n", n=P),
                                         ACT.Copy).then_inc(S["g_vt"], 1)
                    nc.scalar.activation(G["vt"][0:DEC, 4, cols], tr[0:DEC, 1, 0:P], ACT.Copy).then_inc(S["g_vt"], 1)
                for n in range(n_lv + 1):
                    s = n % 2 if n < n_lv else (n + 1) % 2
                    w = SEQ if n == 0 else TOK
                    act.wait_ge(S["g_d"], (n_lv + 1) * h + n + 1)
                    if n >= 2:
                        act.wait_ge(S["g_kl"], (n_lv + 2) * h + (n - 1 if n < n_lv else n_lv))
                        act.wait_ge(S["g_ql"], (n_lv + 1) * h + (n - 1 if n < n_lv else n_lv))
                    if n < n_lv:
                        nc.scalar.activation(G["e"][:, s, 0:w], G["dd"][:, n % 2, 0:w], ACT.Abs).then_inc(S["g_abs"], 1)
                        act.wait_ge(S["g_abs"], n_lv * h + n + 1)
                        nc.scalar.activation(G["e"][:, s, 0:w], G["e"][:, s, 0:w], ACT.Exp,
                                             scale=-tau).then_inc(S["g_e"], 1)
                    else:
                        nc.scalar.activation(G["e"][:, s, 0:w], G["dd"][:, n % 2, 0:w], ACT.Exp,
                                             scale=tau).then_inc(S["g_e"], 1)
                    if n in (1, 4):
                        evacuate(h, 1 + n // 4)
                        split_hi(nc, act, S, w0 + 2 * h, 3 + n // 4)
                evacuate(h, 3)
                act.wait_ge(S["g_kT"], 1 + h + 1)
                nc.scalar.activation(G["kt"][:, 0:4, :], S["aux"][:, 0, :].rearrange("p (c n) -> p c n", n=P),
                                     ACT.Copy).then_inc(S["g_kt"], 1)
                nc.scalar.activation(G["kt"][0:DEC, 4, :], S["aux"][0:DEC, 1, 0:P], ACT.Copy).then_inc(S["g_kt"], 1)
                for v in range(2):
                    act.wait_ge(S["g_oc"], 1 + 2 * h + v + 1)
                    nc.scalar.activation(G["osq"][:, v, :], G["oc"][:, v, :], ACT.Square).then_inc(S["g_osq"], 1)
                act.wait_ge(S["g_osum"], 1 + h + 1)
                nc.scalar.activation(halves(S["root"][:, :]), S["aux"][:, :, 0:HALF], ACT.Sqrt, bias=S["eps"][:, 0:1],
                                     scale=1.0 / (2 * P)).then_inc(S["g_root"], 1)

        @block.vector
        def _(dve):
            dve.wait_ge(S["g_la"], 3)
            nc.vector.scalar_tensor_tensor(out=G["la"][:, :], in0=G["b"][:, :], scalar=0.0, in1=G["la"][:, :],
                                           op0=ALU.min, op1=ALU.subtract).then_inc(S["g_ls"], 1)
            dve.wait_ge(S["g_ls"], 1)
            for h in range(GH):
                nc.vector.tensor_tensor_scan(G["b"][:, h * TOK:(h + 1) * TOK], S["const"][:, C_RST:C_RST + TOK],
                                             G["la"][:, h * TOK:(h + 1) * TOK], 0.0, ALU.mult,
                                             ALU.add).then_inc(S["g_cum"], 1)
            with dve.Fori(0, GH) as h:
                q = S["big"][:, bass.ds(h * TOK, TOK)]
                dve.wait_ge(S["g_cum"], GH)
                dve.wait_ge(S["g_osum"], 1 + h)
                dve.wait_ge(S["g_gated"], 1 + 2 * h)
                nc.vector.memset(G["at"][:, :], 0.0).then_inc(S["g_at0"], 1)

                def delta(n):
                    s = n % 2
                    if n == n_lv:
                        dve.wait_ge(S["g_e"], (n_lv + 1) * h + n - 1)
                        bv = G["b"][:, bass.ds(h * TOK, SEQ)].rearrange("p (c n) -> p c n", n=P)
                        nc.vector.tensor_tensor(G["dd"][:, s, 0:SEQ].rearrange("p (c n) -> p c n", n=P),
                                                bcast(bv[:, :, P - 1], 2, P), bv, ALU.subtract)
                        bl = G["b"][:, bass.ds(h * TOK + TOK - 1, 1)]
                        nc.vector.tensor_tensor(G["dd"][:, s, SEQ:TOK], bl.to_broadcast([P, DEC]),
                                                G["b"][:, bass.ds(h * TOK + SEQ, DEC)],
                                                ALU.subtract).then_inc(S["g_d"], 1)
                        return
                    m = LEVELS[n]
                    w = SEQ if n == 0 else TOK
                    if n >= 2:
                        dve.wait_ge(S["g_e"], (n_lv + 1) * h + n - 1)
                    bv = G["b"][:, bass.ds(h * TOK, w)].rearrange("p (c n) -> p c n", n=2 * m)
                    nc.vector.tensor_tensor(G["dd"][:, s, 0:w].rearrange("p (c n) -> p c n", n=2 * m), bv,
                                            bcast(bv[:, :, m - 1], 2, 2 * m), ALU.subtract).then_inc(S["g_d"], 1)

                def merge(n):
                    s = n % 2
                    dve.wait_ge(S["g_at"], 1 + (n_lv + 1) * h + n + 1)
                    if n == 0:
                        dve.wait_ge(S["g_at0"], h + 1)
                    else:
                        dve.wait_ge(S["g_merge"], (n_lv + 1) * h + n)
                    apart(dve, S)
                    mask = S["const"][:, C_MSK + n * P:C_MSK + (n + 1) * P].bitcast(U32)
                    ins = nc.vector.copy_predicated(G["at"][:, 0:SEQ].rearrange("p (c n) -> p c n", n=P),
                                                    bcast(mask, 1, 4),
                                                    S["mm"][s][:, 0, :].rearrange("p (c n) -> p c n", n=P))
                    if n:
                        ins = nc.vector.copy_predicated(G["at"][0:DEC, SEQ:TOK], mask[0:DEC, 0:DEC],
                                                        S["mm"][s][0:DEC, 1, 0:DEC])
                    ins.then_inc(S["g_merge"], 1)

                delta(0)
                split_lo(nc, dve, S, w0 + 2 * h, 1)
                for n in range(n_lv + 1):
                    delta(n + 1) if n + 1 <= n_lv else None
                    s = n % 2
                    w = SEQ if n == 0 else TOK
                    if n >= 2:
                        dve.wait_ge(S["g_at"], 1 + (n_lv + 1) * h + n - 1)
                    qw = S["big"][:, bass.ds(h * TOK, w)]
                    if n < n_lv:
                        dve.wait_ge(S["g_e"], (n_lv + 1) * h + n + 1)
                        nc.vector.scalar_tensor_tensor(out=G["ql"][:, s, 0:w], in0=qw, scalar=dk_scale,
                                                       in1=G["e"][:, s, 0:w], op0=ALU.mult,
                                                       op1=ALU.mult).then_inc(S["g_ql"], 1)
                    else:
                        nc.vector.tensor_scalar(G["ql"][:, s, 0:w], qw, dk_scale, None, ALU.mult).then_inc(S["g_ql"], 1)
                    if n:
                        merge(n - 1)
                    if n in (0, 3, 6):
                        split_lo(nc, dve, S, w0 + 2 * h, 2 + n // 3)
                merge(n_lv)
                dve.wait_ge(S["g_eb"], 3 * h + 3)
                nc.vector.scalar_tensor_tensor(out=G["qb"][:, :], in0=q, scalar=dk_scale, in1=G["qb"][:, :],
                                               op0=ALU.mult, op1=ALU.mult).then_inc(S["g_qb"], 1)
                dve.wait_ge(S["g_ds"], h + 1)
                dve.wait_ge(S["g_out"], 1 + 32 * h)
                nc.vector.tensor_copy(G["st"][:, 1, :], S["aux2"][:, 0, 0:256]).then_inc(S["g_chain"], 1)
                for c in range(1, 4):
                    dve.wait_ge(S["g_chain"], 4 * h + c)
                    nc.vector.scalar_tensor_tensor(out=G["st"][:, (c + 1) % 4, :], in0=G["st"][:, c, :],
                                                   scalar=G["el"][:, c:c + 1],
                                                   in1=S["aux2"][:, c // 2, (c % 2) * 256:(c % 2) * 256 + 256],
                                                   op0=ALU.mult, op1=ALU.add).then_inc(S["g_chain"], 1)
                dve.wait_ge(S["g_state"], 16 * (h + 1))
                nc.vector.scalar_tensor_tensor(out=G["s_fin"][:, :], in0=G["st"][:, 4, :], scalar=G["el"][:, 4:5],
                                               in1=S["aux"][:, 0, 0:256], op0=ALU.mult,
                                               op1=ALU.add).then_inc(S["g_fin"], 1)
                for v in range(2):
                    dve.wait_ge(S["g_o"], 1 + 2 * h + v + 1)
                    nc.vector.tensor_copy(G["oc"][:, v, 0:SEQ], S["mm"][v][:, 0, :])
                    nc.vector.tensor_copy(G["oc"][:, v, SEQ:TOK], S["mm"][v][:, 1, 0:DEC]).then_inc(S["g_oc"], 1)
                dve.wait_ge(S["g_root"], 1 + h + 1)
                nc.vector.reciprocal(S["rinv"][:, :], S["root"][:, :]).then_inc(S["g_rinv"], 1)
                dve.wait_ge(S["g_rinv"], h + 1)
                for v in range(2):
                    nc.vector.scalar_tensor_tensor(out=G["oc"][:, v, :], in0=G["oc"][:, v, :],
                                                   scalar=S["gains"][:, G_GLA + v:G_GLA + v + 1], in1=S["rinv"][:, :],
                                                   op0=ALU.mult, op1=ALU.mult).then_inc(S["g_on"], 1)
                for v in range(2):
                    gate = feat(S, 16 + 2 * h + v)
                    dve.wait_ge(S["g_on"], 2 * h + v + 1)
                    nc.vector.tensor_tensor(gate, gate, G["oc"][:, v, :], ALU.mult).then_inc(S["g_gated"], 1)

        @block.tensor
        def _(pe):
            for h in range(GH):
                pb = [S["mm"][0], S["mm"][1], S["aux"], S["aux2"]][h]
                matmul_tok(nc, pb, S["w_gate"][0:RANK, h * P:(h + 1) * P], S["glr"][0:RANK, :], True,
                           True).then_inc(S["g_z"], 1)
            def dense_half(h, n):
                k, f = n // 2, n % 2
                t = T_GA + 4 * h + k
                if f == 0:
                    pe.wait_ge(S["w_split"], t + 1)
                    if k < 2:
                        pe.wait_ge(S["g_oc"], 1 + 2 * h)
                    else:
                        pe.wait_ge(S["g_vt"], 4 * h + 2 * k - 2)
                cols = slice(f * HALF, (f + 1) * HALF)
                for c in range(KT):
                    w = slice(c * P, (c + 1) * P)
                    ins = product3(nc, dense_banks[k][:, f, 0:HALF], S["w_hi"][:, k % 2, w],
                                   S["w_lo"][:, k % 2, w], S["x_hi"][:, c, cols], S["x_lo"][:, c, cols],
                                   c == 0, c == KT - 1)
                if f == 1:
                    ins.then_inc(S["tile_done"], 1)

            with pe.Fori(0, GH) as h:
                pe.wait_ge(S["g_zb"], 1)
                dense_half(h, 0)
                dense_half(h, 1)
                pe.wait_ge(S["g_vs"], 2 * h + 2)
                pe.wait_ge(S["g_root"], 1 + h)
                pe.wait_ge(S["g_fin"], 1 + h)
                for v in range(2):
                    tr = [S["aux"], S["aux2"]][v]
                    for c in range(NC_T):
                        t0, n = token_cols(c)
                        out = tr[:, 0, t0:t0 + P] if c < 4 else tr[0:DEC, 1, 0:P]
                        ins = nc.tensor.transpose(out, G["vs"][:, v, t0:t0 + n], S["ident"])
                    ins.then_inc(S["g_vT"], 1)
                dense_half(h, 2)
                dense_half(h, 3)
                for n in range(n_lv + 1):
                    s = n % 2
                    pe.wait_ge(S["g_ql"], (n_lv + 1) * h + n + 1)
                    pe.wait_ge(S["g_kl"], (n_lv + 2) * h + n + 1)
                    if n >= 2:
                        pe.wait_ge(S["g_merge"], (n_lv + 1) * h + n - 1)
                    else:
                        pe.wait_ge(S["evacuated"], T_GA + 4 * h + n + 1)
                    for c in range(4 if n == 0 else 5):
                        t0, w = token_cols(c)
                        out = S["mm"][s][:, 0, t0:t0 + P] if c < 4 else S["mm"][s][0:DEC, 1, 0:DEC]
                        ins = nc.tensor.matmul(out, G["kl"][:, s, t0:t0 + w], G["ql"][:, s, t0:t0 + w], start=True,
                                               stop=True)
                    ins.then_inc(S["g_at"], 1)
                    if n % 2 == 0:
                        dense_half(h, 4 + n // 2)
                s = (n_lv + 1) % 2
                pe.wait_ge(S["g_kl"], (n_lv + 2) * (h + 1))
                pe.wait_ge(S["g_vt"], 4 * (h + 1))
                pe.wait_ge(S["evacuated"], T_GA + 4 * h + 4)
                apart(pe, S)
                for c in range(NC_T):
                    t0, n = token_cols(c)
                    out = S["aux"][:, 0, t0:t0 + P] if c < 4 else S["aux"][0:DEC, 1, 0:P]
                    ins = nc.tensor.transpose(out, G["kl"][:, s, t0:t0 + n], S["ident"])
                ins.then_inc(S["g_kT"], 1)
                pe.wait_ge(S["g_kt"], 2 * (h + 1))
                for c in range(4):
                    nc.tensor.matmul(S["aux2"][:, c // 2, (c % 2) * 256:(c % 2) * 256 + 256], G["kt"][:, c, :],
                                     G["vt"][:, c, :], start=True, stop=True)
                nc.tensor.matmul(S["aux"][:, 0, 0:256], G["kt"][0:DEC, 4, :], G["vt"][0:DEC, 4, :], start=True,
                                 stop=True).then_inc(S["g_ds"], 1)
                pe.wait_ge(S["g_merge"], (n_lv + 1) * (h + 1))
                pe.wait_ge(S["g_qb"], h + 1)
                pe.wait_ge(S["g_fin"], 1 + h + 1)
                for v in range(2):
                    vc = slice(v * P, (v + 1) * P)
                    for c in range(NC_T):
                        t0, n = token_cols(c)
                        out = S["mm"][v][:, 0, t0:t0 + P] if c < 4 else S["mm"][v][:, 1, 0:DEC]
                        ins = nc.tensor.matmul(out, G["vt"][0:n, c, vc], G["at"][0:n, t0:t0 + n], start=True,
                                               stop=c == 0)
                        if c:
                            ins = nc.tensor.matmul(out, G["st"][:, c, vc], G["qb"][:, t0:t0 + n], start=False,
                                                   stop=True)
                    ins.then_inc(S["g_o"], 1)
                for v in range(2):
                    pe.wait_ge(S["g_osq"], 2 * h + v + 1)
                    ins = matmul_tok(nc, S["aux"], S["ones"][:, :], G["osq"][:, v, :], v == 0, v == 1)
                ins.then_inc(S["g_osum"], 1)


def stage_mix(nc, S, A):

    def tiles_of(eng, a, b, body):
        with eng.Fori(a // 2, b // 2) as i:
            for u in range(2):
                body(i, u, 2 * i + u - a)

    def tiles_of_rest(eng, a, b, body):
        with eng.Fori(a // 2 + 1, b // 2) as i:
            for u in range(2):
                body(i, u, 2 * i + u - a)

    with nc.Block() as block:
        @block.sync
        def _(sp):
            def branch_a(i, u, n):
                for q in range(2):
                    sp.wait_ge(S["z_in"][q], 1 + 16 * n)
                    sp.dma_start(feat(S, n + 8 * q), A["z"][:, bass.ds(n + 8 * q, 1), :]).then_inc(S["z_in"][q], 16)
                load_w(sp, S, i, u + 3)
            tiles_of(sp, T_WA, T_WB, branch_a)
            with sp.Fori(T_WB // 2, T_PQ // 2) as i:
                load_w(sp, S, i, 3)
                load_w(sp, S, i, 4)

        @block.gpsimd
        def _(pool):
            pool.wait_ge(S["x_split"], 2 * KT)
            pool.dma_start(S["res"][:, :], A["xT"]).then_inc(S["x_again"], 16)

        @block.scalar
        def _(act):
            for k in range(KT):
                activation_hi(nc, act, S, "y", k, res_tile(S, k))

            def branch_a(i, u, n):
                split_hi(nc, act, S, i, u + 1)
                for q in range(2):
                    act.wait_ge(S["z_in"][q], 1 + 16 * (n + 1))
                    nc.scalar.activation(feat(S, n + 8 * q), feat(S, n + 8 * q), ACT.Sigmoid).then_inc(S["m_sig"], 1)
                activation_hi(nc, act, S, "x", n, feat(S, n + 16))
            tiles_of(act, T_WA, T_WB, branch_a)

            def branch_b(i, u, n):
                split_hi(nc, act, S, i, u + 1)
                act.wait_ge(S["evacuated"], 2 * i + u + 1)
                activation_hi(nc, act, S, "y", n, feat(S, n))
            act.wait_ge(S["tile_done"], T_WB)
            tiles_of(act, T_WB, T_WO, branch_b)

            def project(i, u, n):
                split_hi(nc, act, S, i, u + 1)
                act.wait_ge(S["evacuated"], 2 * i + u)
                if not isinstance(n, int) or n > 0:
                    rms_square(nc, act, S, n - 1)
            project(T_WO // 2, 0, 0)
            project(T_WO // 2, 1, 1)
            tiles_of_rest(act, T_WO, T_PQ, project)
            act.wait_ge(S["evacuated"], T_PQ)
            rms_square(nc, act, S, KT - 1)
            rms_root(nc, act, S, 1)
            rms_split_hi(nc, act, S, 1)

        @block.vector
        def _(dve):
            for k in range(KT):
                activation_lo(nc, dve, S, "y", k, res_tile(S, k), KT)

            def branch_a(i, u, n):
                gate = halves(feat(S, n))
                split_lo(nc, dve, S, i, u + 1)
                dve.wait_ge(S["tile_done"], 2 * i + u + 1)
                dve.wait_ge(S["m_sig"], 2 * n + 1)
                nc.vector.tensor_tensor(gate, gate, S["mm"][u][:, :, 0:HALF], ALU.mult).then_inc(S["evacuated"], 1)
                activation_lo(nc, dve, S, "x", n, feat(S, n + 16), 2 * KT)
            tiles_of(dve, T_WA, T_WB, branch_a)

            def branch_b(i, u, n):
                split_lo(nc, dve, S, i, u + 1)
                dve.wait_ge(S["evacuated"], 2 * i + u)
                dve.wait_ge(S["tile_done"], 2 * i + u + 1)
                nc.vector.tensor_tensor(halves(S["rsin"][:, :]), halves(feat(S, n + 8)), S["mm"][u][:, :, 0:HALF],
                                        ALU.mult).then_inc(S["m_tmp"], 1)
                dve.wait_ge(S["m_tmp"], n + 1)
                nc.vector.tensor_tensor(feat(S, n), feat(S, n), S["rsin"][:, :],
                                        ALU.add).then_inc(S["evacuated"], 1)
                activation_lo(nc, dve, S, "y", n, feat(S, n), 3 * KT)
            dve.wait_ge(S["m_sig"], 2 * KT)
            tiles_of(dve, T_WB, T_WO, branch_b)

            def project(i, u, n):
                h = halves(res_tile(S, n))
                split_lo(nc, dve, S, i, u + 1)
                dve.wait_ge(S["tile_done"], 2 * i + u + 1)
                nc.vector.tensor_tensor(h, h, S["mm"][u][:, :, 0:HALF], ALU.add).then_inc(S["evacuated"], 1)
            dve.wait_ge(S["x_again"], 16)
            tiles_of(dve, T_WO, T_PQ, project)
            rms_apply(nc, dve, S, 1, G_N2, 4 * KT)

        @block.tensor
        def _(pe):
            def phase(a, b, source):
                pe.wait_ge(S["evacuated"], a)
                tiles_of(pe, a, b, lambda i, u, n: dense_tile(nc, pe, S, i, u, source))
            pe.wait_ge(S["evacuated"], T_WA)
            dense_tile(nc, pe, S, T_WA // 2, 0, "y", x_before=KT)
            dense_tile(nc, pe, S, T_WA // 2, 1, "y")
            tiles_of_rest(pe, T_WA, T_WB, lambda i, u, n: dense_tile(nc, pe, S, i, u, "y"))
            pe.wait_ge(S["x_split"], 3 * KT)
            phase(T_WB, T_WO, "x")
            dense_tile(nc, pe, S, T_WO // 2, 0, "y", x_before=3 * KT)
            dense_tile(nc, pe, S, T_WO // 2, 1, "y")
            rms_sum(nc, pe, S, 1, 0, first=True)

            def project(i, u, n):
                dense_tile(nc, pe, S, i, u, "y")
                rms_sum(nc, pe, S, 1, n - 1)
            tiles_of_rest(pe, T_WO, T_PQ, project)
            rms_sum(nc, pe, S, 1, KT - 1, last=True)
            dense_tile(nc, pe, S, T_PQ // 2, 0, x_before=4 * KT)


def load_u(sp, S, A, base, r):
    e = base + r
    if not (isinstance(e, int) and e < 2):
        sp.wait_ge(S["u_lo"], e - 1)
    sp.dma_start(S["w_raw"][:, r % 2, :], A["u"][:, bass.ds(e, 1), :]).then_inc(S["u_in"][r % 2], 16)


def u_hi(nc, act, S, base, r):
    e = base + r
    act.wait_ge(S["u_in"][r % 2], 8 * (base + r - r % 2) + 16)
    if not (isinstance(e, int) and e < 2):
        act.wait_ge(S["u_mm"], e - 1)
    nc.scalar.activation(S["w_hi"][:, r % 2, :], S["w_raw"][:, r % 2, :], ACT.Copy).then_inc(S["u_hi"], 1)


def u_lo(nc, dve, S, base, r):
    dve.wait_ge(S["u_hi"], base + r + 1)
    nc.vector.tensor_tensor(S["w_lo"][:, r % 2, :], S["w_raw"][:, r % 2, :], S["w_hi"][:, r % 2, :].bitcast(F32),
                            ALU.subtract).then_inc(S["u_lo"], 1)


def run_u(nc, pe, S, base, r, banks):
    e = base + r
    pe.wait_ge(S["u_lo"], e + 1)
    pe.wait_ge(S["u_gel"], 2 + e - 1)
    for f in range(2):
        cols = slice(f * HALF, (f + 1) * HALF)
        for k in range(KT):
            w = slice(k * P, (k + 1) * P)
            ins = product3(nc, banks[r % 2][:, f, 0:HALF], S["w_hi"][:, r % 2, w], S["w_lo"][:, r % 2, w],
                           S["x_hi"][:, k, cols], S["x_lo"][:, k, cols], k == 0, k == KT - 1)
    ins.then_inc(S["u_mm"], 1)


def early_gelu(nc, act, S, R, base, r):
    act.wait_ge(S["u_mm"], base + r + 1)
    act.wait_ge(S["h_out"][r % 2], 1 + 8 * (base + r - r % 2))
    nc.scalar.activation(halves(R["hst"][:, r % 2, :]), early_banks(S)[r % 2][:, :, 0:HALF],
                         ACT.Gelu).then_inc(S["u_gel"], 1)
    u_hi(nc, act, S, base, r + 2)


def early_dma(sp, S, A, R, base, r):
    e = base + r
    sp.wait_ge(S["u_gel"], 2 + e + 1)
    sp.dma_start(A["h"][:, bass.ds(e, 1), :], R["hst"][:, r % 2, :]).then_inc(S["h_out"][r % 2], 16)
    load_u(sp, S, A, base, r + 4)


def early_banks(S):
    return [S["aux"], S["aux2"]]


def stage_keys(nc, S, A, R):
    with nc.Block() as block:
        @block.sync
        def _(sp):
            sp.dma_start(R["sk"][:, :], A["skT"]).then_inc(S["r_sk"], 16)
            with sp.Fori(T_PQ // 2, T_END // 2 - 2) as i:
                load_w(sp, S, i, 3)
                load_w(sp, S, i, 4)
            load_w(sp, S, T_END // 2 - 2, 3)
            for r in range(2):
                sp.wait_ge(S["w_split"], T_END - 1 + r)
                load_u(sp, S, A, 0, r)
            load_u(sp, S, A, 0, 2)
            load_u(sp, S, A, 0, 3)

        @block.scalar
        def _(act):
            def query(i, u, last=False):
                t = 2 * i + u
                if not last:
                    split_hi(nc, act, S, i, u + 1)
                act.wait_ge(S["tile_done"], t + 1)
                act.wait_ge(S["r_mm"], t - T_PQ - 1) if not (isinstance(t, int) and t < T_PQ + 2) else None
                nc.scalar.activation(halves(R["qp"][:, u, :]), S["mm"][u][:, :, 0:HALF], ACT.Copy).then_inc(S["evacuated"], 1)

            def scores(i, u):
                n = 2 * i + u - T_PQ
                act.wait_ge(S["r_mm"], n + 1)
                if not (isinstance(n, int) and n < 2):
                    act.wait_ge(S["r_top"], 1 + n - 1)
                nc.scalar.activation(R["s"][:, u, 0:SEQ], S["aux"][:, 0, :], ACT.Copy)
                nc.scalar.activation(R["s"][0:DEC, u, SEQ:SEQ + P], S["aux"][0:DEC, 1, 0:P],
                                     ACT.Copy).then_inc(S["r_s"], 1)
            b = T_PQ // 2
            query(b, 0)
            query(b, 1)
            scores(b, 0)
            with act.Fori(b + 1, T_END // 2 - 1) as i:
                query(i, 0)
                scores(i - 1, 1)
                query(i, 1)
                scores(i, 0)
            e = T_END // 2 - 1
            query(e, 0)
            scores(e - 1, 1)
            u_hi(nc, act, S, 0, 0)
            query(e, 1, last=True)
            scores(e, 0)
            u_hi(nc, act, S, 0, 1)
            scores(e, 1)
            early_gelu(nc, act, S, R, 0, 0)
            early_gelu(nc, act, S, R, 0, 1)

        @block.tensor
        def _(pe):
            def scores(i, u):
                n = 2 * i + u - T_PQ
                pe.wait_ge(S["evacuated"], 2 * i + u + 1)
                if not (isinstance(n, int) and n < 1):
                    pe.wait_ge(S["r_s"], n)
                for c in range(NC_T):
                    t0, w = token_cols(c)
                    out = S["aux"][:, 0, t0:t0 + P] if c < 4 else S["aux"][0:DEC, 1, 0:P]
                    ins = nc.tensor.matmul(out, R["qp"][:, u, t0:t0 + w], R["sk"][:, bass.ds(n * P, P)], start=True,
                                           stop=True)
                ins.then_inc(S["r_mm"], 1)
            pe.wait_ge(S["x_split"], 5 * KT)
            pe.wait_ge(S["evacuated"], T_PQ)
            b = T_PQ // 2
            dense_tile(nc, pe, S, b, 1)
            pe.wait_ge(S["r_sk"], 16)
            scores(b, 0)
            with pe.Fori(b + 1, T_END // 2) as i:
                dense_tile(nc, pe, S, i, 0)
                scores(i - 1, 1)
                dense_tile(nc, pe, S, i, 1)
                scores(i, 0)
            scores(T_END // 2 - 1, 1)
            pe.wait_ge(S["r_s"], 2 * PH)
            run_u(nc, pe, S, 0, 0, early_banks(S))
            run_u(nc, pe, S, 0, 1, early_banks(S))

        @block.vector
        def _(dve):
            def top16(i, u):
                n = 2 * i + u - T_PQ
                dve.wait_ge(S["r_s"], n + 1)
                if not (isinstance(n, int) and n < 2):
                    dve.wait_ge(S["r_kept"], 1 + 2 * n - 2)
                if not (isinstance(n, int) and n < 1):
                    dve.wait_ge(S["r_top"], 1 + n)
                apart(dve, S)
                rows = [P] * 4 + [DEC]

                def sc(c):
                    return R["s"][0:rows[c], u, c * P:(c + 1) * P]
                for c in range(NC_T):
                    ins = nc.vector.max(R["tv"][0:rows[c], u, c * 16:c * 16 + 8], sc(c))
                ins.then_inc(S["r_c"], 1)
                dve.wait_ge(S["r_c"], 3 * n + 1)
                apart(dve, S)
                for c in range(NC_T):
                    ins = nc.vector.match_replace(R["s2"][0:rows[c], c * P:(c + 1) * P],
                                                  R["tv"][0:rows[c], u, c * 16:c * 16 + 8], sc(c), NEG)
                ins.then_inc(S["r_c"], 1)
                for c in range(NC_T):
                    nc.vector.max_index(R["ti"][0:rows[c], u, c * 16:c * 16 + 8],
                                        R["tv"][0:rows[c], u, c * 16:c * 16 + 8], sc(c))
                dve.wait_ge(S["r_c"], 3 * n + 2)
                apart(dve, S)
                for c in range(NC_T):
                    ins = nc.vector.max(R["tv"][0:rows[c], u, c * 16 + 8:c * 16 + 16],
                                        R["s2"][0:rows[c], c * P:(c + 1) * P])
                ins.then_inc(S["r_c"], 1)
                dve.wait_ge(S["r_c"], 3 * n + 3)
                apart(dve, S)
                for c in range(NC_T):
                    ins = nc.vector.max_index(R["ti"][0:rows[c], u, c * 16 + 8:c * 16 + 16],
                                              R["tv"][0:rows[c], u, c * 16 + 8:c * 16 + 16],
                                              R["s2"][0:rows[c], c * P:(c + 1) * P])
                ins.then_inc(S["r_top"], 1)
            nc.vector.memset(R["tv"][:, :, :], 0.0).then_inc(S["r_init"], 1)
            nc.vector.memset(R["ti"][:, :, :], 0).then_inc(S["r_init"], 1)
            dve.wait_ge(S["r_init"], 2)
            b = T_PQ // 2
            split_lo(nc, dve, S, b, 1)
            split_lo(nc, dve, S, b, 2)
            top16(b, 0)
            with dve.Fori(b + 1, T_END // 2 - 1) as i:
                split_lo(nc, dve, S, i, 1)
                top16(i - 1, 1)
                split_lo(nc, dve, S, i, 2)
                top16(i, 0)
            e = T_END // 2 - 1
            split_lo(nc, dve, S, e, 1)
            top16(e - 1, 1)
            u_lo(nc, dve, S, 0, 0)
            top16(e, 0)
            u_lo(nc, dve, S, 0, 1)
            top16(e, 1)

        @block.gpsimd
        def _(pool):
            with pool.Fori(0, 2 * PH // 2) as i:
                for u in range(2):
                    n = 2 * i + u
                    pool.wait_ge(S["r_top"], 1 + n + 1)
                    apart(pool, S)
                    nc.gpsimd.tensor_copy(R["sv"][:, :, bass.ds(n * 16, 16)],
                                          R["tv"][:, u, :].rearrange("p (c k) -> p c k", k=16)).then_inc(S["r_kept"], 1)
                    nc.gpsimd.tensor_copy(R["si"][:, :, bass.ds(n * 16, 16)],
                                          R["ti"][:, u, :].rearrange("p (c k) -> p c k", k=16)).then_inc(S["r_kept"], 1)


def stage_route(nc, S, A, R):
    hk = PH * TOPK
    with nc.Block() as block:
        @block.sync
        def _(sp):
            early_dma(sp, S, A, R, 0, 0)
            early_dma(sp, S, A, R, 0, 1)
            with sp.Fori(0, NC_T) as c:
                for r in range(ROUTE_U):
                    early_dma(sp, S, A, R, ROUTE_U * c + 2, r)

        @block.gpsimd
        def _(pool):
            def lo(base, r):
                pool.wait_ge(S["u_hi"], base + r + 1)
                apart(pool, S)
                nc.gpsimd.tensor_tensor(S["w_lo"][:, r % 2, :], S["w_raw"][:, r % 2, :],
                                        S["w_hi"][:, r % 2, :].bitcast(F32), ALU.subtract).then_inc(S["u_lo"], 1)
            lo(0, 2)
            lo(0, 3)
            with pool.Fori(0, NC_T) as c:
                for r in range(ROUTE_U):
                    lo(ROUTE_U * c + 2, r + 2)

        @block.vector
        def _(dve):
            with dve.Fori(0, NC_T) as c:
                def picks(table, half):
                    v = table[:, bass.ds(c, 1), :].rearrange("p o (h q k) -> p (o h) q k", h=PH, q=2)
                    return v[:, :, half, :]
                dve.wait_ge(S["t_ij"], 1 + 2 * c)
                cand4 = R["cand"][:, :].rearrange("p (h a b) -> p h a b", h=PH, a=TOPK)
                nc.vector.tensor_tensor(cand4, bcast(picks(R["sv"], 0), 3, TOPK), bcast(picks(R["sv"], 1), 2, TOPK),
                                        ALU.add).then_inc(S["t_cand"], 1)
                dve.wait_ge(S["t_cand"], c + 1)
                apart(dve, S)

                def cols(h):
                    return slice(h * 256, (h + 1) * 256)
                for h in range(PH):
                    ins = nc.vector.max(R["v2"][:, h * 16:h * 16 + 8], R["cand"][:, cols(h)])
                ins.then_inc(S["t_c"], 1)
                dve.wait_ge(S["t_c"], 3 * c + 1)
                apart(dve, S)
                for h in range(PH):
                    ins = nc.vector.match_replace(R["cand2"][:, cols(h)], R["v2"][:, h * 16:h * 16 + 8],
                                                  R["cand"][:, cols(h)], NEG)
                ins.then_inc(S["t_c"], 1)
                for h in range(PH):
                    nc.vector.max_index(R["i2"][:, h * 16:h * 16 + 8], R["v2"][:, h * 16:h * 16 + 8], R["cand"][:, cols(h)])
                dve.wait_ge(S["t_c"], 3 * c + 2)
                apart(dve, S)
                for h in range(PH):
                    ins = nc.vector.max(R["v2"][:, h * 16 + 8:h * 16 + 16], R["cand2"][:, cols(h)])
                ins.then_inc(S["t_c"], 1)
                dve.wait_ge(S["t_c"], 3 * c + 3)
                apart(dve, S)
                for h in range(PH):
                    ins = nc.vector.max_index(R["i2"][:, h * 16 + 8:h * 16 + 16], R["v2"][:, h * 16 + 8:h * 16 + 16],
                                              R["cand2"][:, cols(h)])
                ins.then_inc(S["t_idx"], 1)
                v3 = R["v2"][:, :].rearrange("p (h k) -> p h k", h=PH)
                g3 = R["gij"][:, 0, :].rearrange("p (h k) -> p h k", h=PH)
                nc.vector.tensor_tensor(R["e2"][:, :].rearrange("p (h k) -> p h k", h=PH), v3,
                                        bcast(v3[:, :, 0], 2, TOPK), ALU.subtract).then_inc(S["t_sub"], 1)
                dve.wait_ge(S["t_idx"], c + 1)
                nc.vector.tensor_scalar(R["ab"][:, 0, :], R["i2"][:, :], 4, None, ALU.logical_shift_right).then_inc(S["t_ab"], 1)
                nc.vector.tensor_scalar(R["ab"][:, 1, :], R["i2"][:, :], 15, None, ALU.bitwise_and).then_inc(S["t_ab"], 1)
                dve.wait_ge(S["t_ab"], 4 * c + 2)
                nc.vector.tensor_copy(R["abf"][:, 0, :], R["ab"][:, 0, :]).then_inc(S["t_ab"], 1)
                nc.vector.tensor_copy(R["abf"][:, 1, :], R["ab"][:, 1, :]).then_inc(S["t_ab"], 1)
                dve.wait_ge(S["t_ab"], 4 * c + 4)
                iota16 = S["const"][:, C_IOTA:C_IOTA + TOPK]
                for q in range(2):
                    eq = R["cand2"] if q else R["cand"]
                    nc.vector.tensor_tensor(eq[:, :].rearrange("p (n a) -> p n a", a=TOPK),
                                            bcast(R["abf"][:, q, :], 2, TOPK), bcast(iota16, 1, hk),
                                            ALU.is_equal).then_inc(S["t_eq"], 1)
                dve.wait_ge(S["t_exp"], c + 1)
                nc.vector.tensor_reduce(R["z2"][:, 0:PH], R["e2"][:, :].rearrange("p (h k) -> p h k", h=PH), AX.X,
                                        ALU.add).then_inc(S["t_z"], 1)
                dve.wait_ge(S["t_z"], 2 * c + 1)
                nc.vector.reciprocal(R["z2"][:, PH:2 * PH], R["z2"][:, 0:PH]).then_inc(S["t_z"], 1)
                dve.wait_ge(S["t_z"], 2 * c + 2)
                dve.wait_ge(S["t_turned"], 1 + c)
                nc.vector.tensor_tensor(g3, R["e2"][:, :].rearrange("p (h k) -> p h k", h=PH),
                                        bcast(R["z2"][:, PH:2 * PH], 2, TOPK), ALU.mult).then_inc(S["t_g"], 1)
                for q in range(2):
                    eq = R["cand2"] if q else R["cand"]
                    e4 = eq[:, :].rearrange("p (h k a) -> p h k a", h=PH, k=TOPK)
                    dve.wait_ge(S["t_eq"], 4 * c + q + 1)
                    nc.vector.tensor_tensor(e4, e4, bcast(picks(R["si"], q), 2, TOPK), ALU.mult).then_inc(S["t_eq"], 1)
                for q in range(2):
                    eq = R["cand2"] if q else R["cand"]
                    dve.wait_ge(S["t_eq"], 4 * c + q + 3)
                    nc.vector.tensor_reduce(R["gij"][:, 1 + q, :], eq[:, :].rearrange("p (n a) -> p n a", a=TOPK),
                                            AX.X, ALU.add).then_inc(S["t_ij"], 1)

        @block.scalar
        def _(act):
            with act.Fori(0, NC_T) as c:
                for r in range(3):
                    early_gelu(nc, act, S, R, ROUTE_U * c + 2, r)
                act.wait_ge(S["t_sub"], c + 1)
                nc.scalar.activation(R["e2"][:, :], R["e2"][:, :], ACT.Exp).then_inc(S["t_exp"], 1)
                for r in range(3, ROUTE_U):
                    early_gelu(nc, act, S, R, ROUTE_U * c + 2, r)
                act.wait_ge(S["t_turned"], 1 + c + 1)
                nc.scalar.activation(R["tab"][:, :, bass.ds(c * P, P)],
                                     S["mm"][0][:, 0, 0:3 * P].rearrange("p (q n) -> p q n", q=3),
                                     ACT.Copy).then_inc(S["t_tab"], 1)

        @block.tensor
        def _(pe):
            with pe.Fori(0, NC_T) as c:
                for r in range(ROUTE_U):
                    run_u(nc, pe, S, ROUTE_U * c + 2, r, early_banks(S))
                pe.wait_ge(S["t_ij"], 1 + 2 * c + 2)
                pe.wait_ge(S["t_g"], c + 1)
                pe.wait_ge(S["t_tab"], 1 + c)
                for q in range(3):
                    ins = nc.tensor.transpose(S["mm"][0][:, 0, q * P:(q + 1) * P], R["gij"][:, q, :], S["ident"])
                ins.then_inc(S["t_turned"], 1)


def stage_gates(nc, S, A, R, Q):
    GRP = 8
    n_grp = CHUNK_TOK // GRP
    n_chunk = TOK // CHUNK_TOK
    bodies = n_chunk * n_grp // 4
    e0 = 2 + ROUTE_U * NC_T
    iota = S["const"][:, C_IOTA:C_IOTA + P]
    banks = [S["mm"][0], S["mm"][1]]
    on_dve = 3
    closing = range(EARLY - CLOSING, EARLY)
    assert closing[0] == e0 + 2 * bodies

    with nc.Block() as block:
        @block.vector
        def _(dve):
            def weighted(b, q):
                g, u = 4 * b + q, q % 2
                dve.wait_ge(S["e_mm"], 2 + g - 1)
                for j in range(GRP):
                    ins = nc.vector.tensor_scalar(Q["a"][:, u, j * P:(j + 1) * P], iota,
                                                  R["tab"][:, 1, bass.ds(g * GRP + j, 1)],
                                                  R["tab"][:, 0, bass.ds(g * GRP + j, 1)], ALU.is_equal, ALU.mult)
                for j in range(on_dve):
                    ins = nc.vector.tensor_scalar(Q["b"][:, u, j * P:(j + 1) * P], iota,
                                                  R["tab"][:, 2, bass.ds(g * GRP + j, 1)], None, ALU.is_equal)
                ins.then_inc(S["e_a"], 1)
            weighted(0, 0)
            weighted(0, 1)
            with dve.Fori(0, bodies - 1) as b:
                for half in range(2):
                    u_lo(nc, dve, S, e0 + 2 * b, half + 2)
                    weighted(b, 2 * half + 2)
                    weighted(b, 2 * half + 3)
            u_lo(nc, dve, S, 0, e0 + 2 * bodies)
            weighted(bodies - 1, 2)
            weighted(bodies - 1, 3)
            for e in range(e0 + 2 * bodies - 1, EARLY):
                u_lo(nc, dve, S, 0, e + 2)

        @block.gpsimd
        def _(pool):
            with pool.Fori(0, 2 * bodies) as i:
                for u in range(2):
                    g = 2 * i + u
                    pool.wait_ge(S["e_mm"], 2 + g - 1)
                    apart(pool, S)
                    nc.gpsimd.tensor_copy(Q["i2"][:, u, :], R["tab"][:, 2, bass.ds(g * GRP, GRP)]).then_inc(S["e_i2"], 1)
                    pool.wait_ge(S["e_i2"], g + 1)
                    apart(pool, S)
                    for j in range(on_dve, GRP):
                        ins = nc.gpsimd.tensor_scalar(Q["b"][:, u, j * P:(j + 1) * P], iota, Q["i2"][:, u, j:j + 1],
                                                      None, ALU.is_equal)
                    ins.then_inc(S["e_b"], 1)

        @block.tensor
        def _(pe):
            def products(b, q):
                g, u = 4 * b + q, q % 2
                pe.wait_ge(S["e_a"], g + 1)
                pe.wait_ge(S["e_b"], g + 1)
                pe.wait_ge(S["e_out"], 2 + g - 1)
                for j in range(GRP):
                    ins = nc.tensor.matmul(banks[u][:, j // 4, (j % 4) * P:(j % 4 + 1) * P],
                                           Q["b"][:, u, j * P:(j + 1) * P], Q["a"][:, u, j * P:(j + 1) * P],
                                           start=True, stop=True)
                ins.then_inc(S["e_mm"], 1)

            with pe.Fori(0, bodies) as b:
                for half in range(2):
                    run_u(nc, pe, S, e0 + 2 * b, half, early_banks(S))
                    products(b, 2 * half)
                    products(b, 2 * half + 1)
            for e in closing:
                run_u(nc, pe, S, 0, e, early_banks(S))

        @block.scalar
        def _(act):
            def out(g, u, q, half):
                act.wait_ge(S["e_mm"], 2 + g + 1)
                src = banks[u][:, :, :].rearrange("p q (j n) -> p n (q j)", n=P)
                dst = Q["ring"][:, half, :, bass.ds(q * GRP, GRP)]
                nc.scalar.activation(dst, src, ACT.Copy).then_inc(S["e_out"], 1)

            def body(k2, half, b2):
                g = k2 * (2 * n_grp) + half * n_grp + 4 * b2
                e = k2 * n_grp + half * n_grp // 2 + 2 * b2 + e0
                for v in range(2):
                    early_gelu(nc, act, S, R, e, v)
                    out(g + 2 * v, 0, 4 * b2 + 2 * v, half)
                    out(g + 2 * v + 1, 1, 4 * b2 + 2 * v + 1, half)

            with act.Fori(0, n_chunk // 2) as k2:
                for half in range(2):
                    act.wait_ge(S["e_store"][half], 1 + 16 * k2)
                    with act.Fori(0, 2) as b2:
                        body(k2, half, b2)
            act.wait_ge(S["e_store"][0], 1 + 16 * (n_chunk // 2))
            body(n_chunk // 2, 0, 0)
            body(n_chunk // 2, 0, 1)
            for e in closing:
                early_gelu(nc, act, S, R, 0, e)

        @block.sync
        def _(sp):
            def store(k2, half):
                sp.wait_ge(S["e_out"], 2 + n_grp * (2 * k2 + half + 1))
                sp.dma_start(A["gate"][:, bass.ds(2 * k2 + half, 1), :, :],
                             Q["ring"][:, half, :, :]).then_inc(S["e_store"][half], 16)

            with sp.Fori(0, n_chunk // 2) as k2:
                for half in range(2):
                    with sp.Fori(0, 2) as b2:
                        for v in range(2):
                            early_dma(sp, S, A, R, k2 * n_grp + half * n_grp // 2 + 2 * b2 + e0, v)
                    store(k2, half)
            for e in range(e0 + 2 * bodies - 4, e0 + 2 * bodies):
                early_dma(sp, S, A, R, 0, e)
            store(n_chunk // 2, 0)
            for e in closing:
                early_dma(sp, S, A, R, 0, e)
            for u in range(2):
                sp.wait_ge(S["h_out"][u], 1 + 16 * (EARLY // 2))
            sp.wait_ge(S["e_store"][0], 1 + 16 * (n_chunk // 2 + 1))
            sp.wait_ge(S["e_store"][1], 1 + 16 * (n_chunk // 2))


def load_gv(sp, S, A, E, base, r):
    e = base + r
    if not (isinstance(e, int) and e < 2):
        sp.wait_ge(S["u_p"], e - 1)
    sp.dma_start(E["gate"][:, r % 2, :], A["gate"][:, :, bass.ds(e, 1), :]).then_inc(S["g_in"][r % 2], 16)
    if not (isinstance(e, int) and e < 2):
        sp.wait_ge(S["v_lo"], e - 1)
    sp.dma_start(E["v_raw"][:, r % 2, :], A["v"][:, bass.ds(e, 1), :]).then_inc(S["v_in"][r % 2], 16)


def loaded(base, r):
    return 8 * (base + r - r % 2) + 16


def v_hi(nc, act, S, E, base, r, slot):
    act.wait_ge(S["v_in"][r % 2], loaded(base, r))
    nc.scalar.activation(E["v_hi"][:, slot, :], E["v_raw"][:, r % 2, :], ACT.Copy).then_inc(S["v_hi"], 1)


def p_hi(nc, act, S, E, base, r, slot):
    act.wait_ge(S["u_p"], base + r + 1)
    nc.scalar.activation(E["p_hi"][:, slot, :], E["p"][:, :], ACT.Copy).then_inc(S["u_phi"], 1)


def gated(nc, dve, S, E, base, r, gel):
    e = base + r
    if not (isinstance(e, int) and e < 1):
        dve.wait_ge(S["u_plo"], e)
    dve.wait_ge(S["g_in"][r % 2], loaded(base, r))
    nc.vector.tensor_tensor(E["p"][:, :], gel, E["gate"][:, r % 2, :], ALU.mult).then_inc(S["u_p"], 1)


def p_lo(nc, dve, S, E, base, r, slot):
    dve.wait_ge(S["u_phi"], base + r + 1)
    nc.vector.tensor_tensor(E["p_lo"][:, slot, :], E["p"][:, :], E["p_hi"][:, slot, :].bitcast(F32),
                            ALU.subtract).then_inc(S["u_plo"], 1)


def v_lo(nc, dve, S, E, base, r, slot):
    dve.wait_ge(S["v_hi"], base + r + 1)
    nc.vector.tensor_tensor(E["v_lo"][:, slot, :], E["v_raw"][:, r % 2, :], E["v_hi"][:, slot, :].bitcast(F32),
                            ALU.subtract).then_inc(S["v_lo"], 1)


def add_y(nc, dve, S, g, d):
    r = halves(S["res"][:, d * TOK:(d + 1) * TOK])
    dve.wait_ge(S["y_mm"], 1 + KT * g + d + 1)
    nc.vector.tensor_tensor(r, r, [S["aux"], S["aux2"]][d % 2][:, :, 0:HALF], ALU.add).then_inc(S["y_add"], 1)


def run_y(nc, pe, S, E, g, slot0):
    pe.wait_ge(S["u_plo"], 4 * (g + 1))
    pe.wait_ge(S["v_lo"], 4 * (g + 1))
    for d in range(KT):
        pe.wait_ge(S["y_add"], 2 + KT * g + d - 1)
        w = slice(d * P, (d + 1) * P)
        for f in range(2):
            cols = slice(f * HALF, (f + 1) * HALF)
            for j in range(4):
                ins = product3(nc, [S["aux"], S["aux2"]][d % 2][:, f, 0:HALF], E["v_hi"][:, slot0 + j, w],
                               E["v_lo"][:, slot0 + j, w], E["p_hi"][:, slot0 + j, cols],
                               E["p_lo"][:, slot0 + j, cols], j == 0, j == 3)
        ins.then_inc(S["y_mm"], 1)


def stage_experts_early(nc, S, A, E):
    groups = EARLY // 4
    with nc.Block() as block:
        @block.sync
        def _(sp):
            def load(base, r):
                e = base + r
                if not (isinstance(e, int) and e < 2):
                    sp.wait_ge(S["u_p"], e - 1)
                sp.dma_start(E["h"][:, r % 2, :], A["h"][:, bass.ds(e, 1), :]).then_inc(S["h_in"][r % 2], 16)
                load_gv(sp, S, A, E, base, r)
            load(0, 0)
            load(0, 1)
            with sp.Fori(1, EARLY // 2) as i:
                load(2 * i, 0)
                load(2 * i, 1)
            load_gv(sp, S, A, E, EARLY, 0)
            load_gv(sp, S, A, E, EARLY, 1)

        @block.scalar
        def _(act):
            def prepare(g, parity):
                if not isinstance(g, int):
                    act.wait_ge(S["y_mm"], 1 + KT * (g - 1))
                for j in range(4):
                    v_hi(nc, act, S, E, 4 * g, j, 4 * parity + j)
                    p_hi(nc, act, S, E, 4 * g, j, 4 * parity + j)
            prepare(0, 0)
            with act.Fori(0, groups // 2 - 1) as i:
                prepare(2 * i + 1, 1)
                prepare(2 * i + 2, 0)
            act.wait_ge(S["y_mm"], 1 + KT * (groups - 2))
            prepare(groups - 1, 1)

        @block.vector
        def _(dve):
            def prepare(g, parity, j):
                slot = 4 * parity + j
                dve.wait_ge(S["h_in"][j % 2], loaded(4 * g, j))
                gated(nc, dve, S, E, 4 * g, j, E["h"][:, j % 2, :])
                v_lo(nc, dve, S, E, 4 * g, j, slot)
                p_lo(nc, dve, S, E, 4 * g, j, slot)

            def during_y(g, parity, ahead=True):
                for j in range(4):
                    if ahead:
                        prepare(g + 1, 1 - parity, j)
                    add_y(nc, dve, S, g, 2 * j)
                    add_y(nc, dve, S, g, 2 * j + 1)
            for j in range(4):
                prepare(0, 0, j)
            with dve.Fori(0, groups // 2 - 1) as i:
                during_y(2 * i, 0)
                during_y(2 * i + 1, 1)
            during_y(groups - 2, 0)
            during_y(groups - 1, 1, ahead=False)

        @block.tensor
        def _(pe):
            run_u(nc, pe, S, EARLY, 0, S["mm"])
            run_u(nc, pe, S, EARLY, 1, S["mm"])
            with pe.Fori(0, groups // 2) as i:
                run_y(nc, pe, S, E, 2 * i, 0)
                run_y(nc, pe, S, E, 2 * i + 1, 4)


def stage_experts(nc, S, A, E):
    first, groups = EARLY // 4, N_KEYS // 4

    def last(g, c, ahead):
        e = 4 * g + c
        return isinstance(e, int) and e + ahead >= N_KEYS

    with nc.Block() as block:
        @block.sync
        def _(sp):
            def step(g, c):
                if not last(g, c, 4):
                    load_u(sp, S, A, 4 * g, c + 4)
                if not last(g, c, 2):
                    load_gv(sp, S, A, E, 4 * g, c + 2)
            step(first, 0)
            with sp.Fori(first, groups - 2) as g:
                for c in range(1, 5):
                    step(g, c)
            for c in range(1, 5):
                step(groups - 2, c)
            step(groups - 1, 1)
            for d in range(KT):
                sp.wait_ge(S["y_add"], 2 + KT * (groups - 1) + d + 1)
                sp.dma_start(A["yT_out"][:, d:d + 1, :], res_tile(S, d)).then_inc(S["out_y"], 16)
            sp.wait_ge(S["out_y"], 16 * KT)
            sp.wait_ge(S["out_kv"], 32)
            sp.wait_ge(S["g_out"], 1 + 32 * GH)

        @block.scalar
        def _(act):
            def step(g, c):
                act.wait_ge(S["u_mm"], 4 * g + c + 1)
                nc.scalar.activation(halves(E["gel"][:, :]), S["mm"][c % 2][:, :, 0:HALF], ACT.Gelu).then_inc(S["u_gel"], 1)
                if not last(g, c, 2):
                    u_hi(nc, act, S, 4 * g, c + 2)
                if c == 4:
                    act.wait_ge(S["y_mm"], 1 + KT * (g + 1))
                p_hi(nc, act, S, E, 4 * g, c, c % 4)
                v_hi(nc, act, S, E, 4 * g, c, c % 4)
            step(first, 0)
            with act.Fori(first, groups - 1) as g:
                for c in range(1, 5):
                    step(g, c)
            for c in range(1, 4):
                step(groups - 1, c)

        @block.vector
        def _(dve):
            def step(g, c):
                if not last(g, c, 2):
                    u_lo(nc, dve, S, 4 * g, c + 2)
                if c == 4:
                    for d in range(KT):
                        add_y(nc, dve, S, g, d)
                dve.wait_ge(S["u_gel"], 2 + 4 * g + c + 1)
                gated(nc, dve, S, E, 4 * g, c, E["gel"][:, :])
                p_lo(nc, dve, S, E, 4 * g, c, c % 4)
                v_lo(nc, dve, S, E, 4 * g, c, c % 4)
            step(first, 0)
            with dve.Fori(first, groups - 1) as g:
                for c in range(1, 5):
                    step(g, c)
            for c in range(1, 4):
                step(groups - 1, c)
            for d in range(KT):
                add_y(nc, dve, S, groups - 1, d)

        @block.tensor
        def _(pe):
            for c in range(2, 5):
                run_u(nc, pe, S, 4 * first, c, S["mm"])
            run_y(nc, pe, S, E, first, 0)
            with pe.Fori(first + 1, groups - 1) as g:
                for c in range(1, 5):
                    run_u(nc, pe, S, 4 * g, c, S["mm"])
                run_y(nc, pe, S, E, g, 0)
            for c in range(1, 4):
                run_u(nc, pe, S, 4 * (groups - 1), c, S["mm"])
            run_y(nc, pe, S, E, groups - 1, 0)


SEMS = """passed x_again c_in w_split w_hi_done tile_done evacuated x_hi_done x_split n_sq n_sum n_root n_rinv
n_done d_init lam_sum lam_exp lam_d glr_mm glr_done q_sq q_sum q_root q_rinv q_norm q_swap q_cos q_rsin
q_roped out_kv a_staged a_scores a_mask a_max a_exp a_rz a_w1 a_w a_vT a_vtok a_turned a_wT a_pv o_evac
o_sq o_sum o_root o_rinv o_done g_z g_zb g_la g_ls g_cum g_state g_out g_vs g_vT g_vt g_eb g_at0 g_d
g_abs g_e g_kl g_ql g_at g_merge g_kT g_kt g_ds g_chain g_fin g_qb g_o g_oc g_osq g_osum g_root
g_rinv g_on g_gated m_tmp r_sk r_mm r_s r_c r_top r_kept r_init t_cand t_c t_idx t_sub t_exp t_z t_g
t_ab t_eq t_ij t_turned t_tab m_sig e_mm e_a e_i2 e_b e_out u_lo u_hi u_mm u_gel u_p u_phi u_plo v_hi v_lo
y_mm y_add out_y""".split()
PAIR_SEMS = "w_loaded a_cache e_store u_in g_in v_in h_out h_in z_out z_in".split()


def build(nc, A):
    with ExitStack() as ctx:
        S = {}
        for name in SEMS:
            S[name] = ctx.enter_context(nc.semaphore(name))
        for name in PAIR_SEMS:
            S[name] = [ctx.enter_context(nc.semaphore(f"{name}{i}")) for i in range(2)]

        S["x_in"] = [ctx.enter_context(nc.semaphore(f"x_in{k}")) for k in range(KT)]

        def make(stack, ns, stage, **shapes):
            for name, (shape, dt) in shapes.items():
                ns[name] = stack.enter_context(nc.sbuf_tensor(f"{stage}_{name}", [P] + shape, dt))

        psum = [ctx.enter_context(nc.psum_tensor(f"bank{i}", [P, 2, 512], F32)) for i in range(4)]
        S["mm"], S["aux"], S["aux2"] = psum[0:2], psum[2], psum[3]
        S["w_all"] = A["w_all"]
        make(ctx, S, "all",
             res=([KT * TOK], F32),
             x_hi=([KT, TOK], F32R), x_lo=([KT, TOK], F32R),
             w_raw=([2, D], F32), w_hi=([2, D], F32R), w_lo=([2, D], F32R),
             gains=([G_END], F32), gqk=([16], F32), gsub=([1], F32),
             lam=([5], F32), neglam=([1], F32), eps=([1], F32), ones=([P], F32))
        before = ctx.enter_context(ExitStack())
        make(before, S, "before", const=([C_END], F32), root=([TOK], F32), rinv=([TOK], F32), rsin=([TOK], F32))
        S["ident"] = S["const"][:, C_ID:C_ID + P]
        with ExitStack() as mixers:
            make(mixers, S, "mix", w_glr=([KT * RANK], F32), w_gate=([D // 2], F32), glr=([TOK], F32),
                 big=([24 * TOK], F32))
            stage_norm1(nc, S, A)
            with ExitStack() as here:
                make(here, S, "qkv", sq=([2, TOK], F32), nq=([2, TOK], F32), ncos=([2, TOK], F32))
                stage_qkv(nc, S, A)
            with ExitStack() as here:
                B = {}
                make(here, B, "att", qs=([2, TOK], F32), ks=([2, TOK], F32), vs=([2, TOK], F32), ck=([2, PAST], F32),
                     cv=([2, PAST], F32), vtok=([2, NC_T * P], F32), p=([2, 2, 512], F32), w=([2, 512], F32),
                     wT=([2, 512], F32), nmax=([2, 2], F32), z=([2, 2], F32), rz=([2, 2], F32),
                     rz2=([2, 1], F32), osb=([TOK], F32), osq=([TOK], F32))
                B["s"], B["o"] = S["mm"][0], S["aux2"]
                B["tr"] = [S["aux"][:, 0, :], S["aux"][:, 1, :]]
                stage_attention(nc, S, A, B)
            with ExitStack() as here:
                G = {}
                make(here, G, "gla", b=([GH * TOK], F32), la=([GH * TOK], F32), e=([2, TOK], F32), dd=([2, TOK], F32),
                     qb=([TOK], F32), at=([TOK], F32), vt=([NC_T, 256], F32), kt=([NC_T, P], F32),
                     st=([5, 256], F32), s_fin=([256], F32), el=([5], F32))
                G["kl"] = G["la"][:, 0:2 * TOK].rearrange("p (s n) -> p s n", s=2)
                G["ql"] = G["la"][:, 2 * TOK:4 * TOK].rearrange("p (s n) -> p s n", s=2)
                G["vs"] = G["osq"] = G["e"]
                G["oc"] = G["dd"]
                stage_gla(nc, S, A, G)
            with ExitStack() as here:
                make(here, S, "mixing", y_hi=([KT, TOK], F32R), y_lo=([KT, TOK], F32R))
                stage_mix(nc, S, A)
        R = {}
        with ExitStack() as routing:
            make(routing, R, "route", tab=([3, NC_T * P], F32), hst=([2, TOK], F32))
            with ExitStack() as here:
                make(here, R, "keys", sk=([2 * PH * P], F32), qp=([2, TOK], F32), s=([2, NC_T * P], F32),
                     s2=([NC_T * P], F32), tv=([2, NC_T * 16], F32), ti=([2, NC_T * 16], U32),
                     sv=([NC_T, 2 * PH * 16], F32), si=([NC_T, 2 * PH * 16], F32), cand=([PH * 256], F32),
                     cand2=([PH * 256], F32), v2=([P], F32), i2=([P], U32), e2=([P], F32), z2=([2 * PH], F32),
                     ab=([2, P], U32), abf=([2, P], F32), gij=([3, P], F32))
                stage_keys(nc, S, A, R)
                stage_route(nc, S, A, R)
            with ExitStack() as here:
                Q = {}
                make(here, Q, "gates", a=([2, 8 * P], F32), b=([2, 8 * P], F32), i2=([2, 8], F32), ring=([2, N_KEYS, CHUNK_TOK], F32))
                stage_gates(nc, S, A, R, Q)
        before.close()
        E = {}
        make(ctx, E, "exp", v_raw=([2, D], F32), v_hi=([8, D], F32R), v_lo=([8, D], F32R), gate=([2, TOK], F32),
             h=([2, TOK], F32), p=([TOK], F32), p_hi=([8, TOK], F32R), p_lo=([8, TOK], F32R))
        E["gel"] = E["h"][:, 0, :]
        stage_experts_early(nc, S, A, E)
        stage_experts(nc, S, A, E)


def const_table():
    t = np.zeros((P, C_END), np.float32)
    idx = np.arange(P)
    t[:, C_ID:C_ID + P] = np.eye(P)
    t[:, C_BLK:C_BLK + P] = idx[:, None] // HD == idx[None, :] // HD
    d = idx % HD
    for m in range(P):
        if d[m] < HD // 2:
            t[m + HD // 2, C_ROT + m] = -1.0
        else:
            t[m - HD // 2, C_ROT + m] = 1.0
    t[:, C_IOTA:C_IOTA + P] = idx[None, :]
    half = HD // 2
    inv = np.float32(10000.0) ** (-np.arange(half, dtype=np.float32) / np.float32(half))
    pos = np.concatenate([np.arange(SEQ), PAST + np.arange(DEC)]).astype(np.float32)
    ang = pos[None, :] * inv[idx % half][:, None]
    t[:, C_COS:C_COS + TOK] = np.cos(ang)
    t[:, C_SIN:C_SIN + TOK] = np.sin(ang)
    t[:, C_RST:C_RST + TOK] = (np.arange(TOK) % P != 0)[None, :]
    j, i = idx[:, None], idx[None, :]
    for n, m in enumerate(LEVELS):
        t[:, C_MSK + n * P:C_MSK + (n + 1) * P] = (
            (j // (2 * m) == i // (2 * m)) & (j % (2 * m) < m) & (i % (2 * m) >= m))
    n = len(LEVELS)
    t[:, C_MSK + n * P:C_MSK + (n + 1) * P] = np.eye(P)
    return t


def kernel(**inputs):
    import numpy as _np
    import concourse.bacc as _bacc
    from concourse import mybir as _mybir
    from concourse.bass_utils import run_bass_kernel_spmd as _run

    x = {k: _np.asarray(v) for k, v in inputs.items()}

    def tiles(w):
        n = w.shape[1] // P
        return w.reshape(KT, P, n, P).transpose(2, 1, 0, 3).reshape(n, P, D)

    def columns(v):
        return v.reshape(-1, P).T

    w_in = x["w_in"][0]
    starts = _np.cumsum([0, D, D, D, D // 2, D // 2, D, RANK, D, D, D])
    dq, dk, dv, gq, gk, gv, glr, gr, ga, gb = [w_in[:, a:b] for a, b in zip(starts[:-1], starts[1:])]
    gla = _np.stack([_np.concatenate([tiles(gq), tiles(gk)]), tiles(gr), tiles(gv)], axis=1).reshape(3 * KT, P, D)
    w_all = _np.concatenate([tiles(w) for w in (dq, dk, dv)] + [gla]
                            + [tiles(w) for w in (ga, gb, x["w_branch_a"][0], x["w_branch_b"][0], x["w_out"][0],
                                                  x["peer_w_q"][0])])
    frames = _np.concatenate([x["x_prompt"][0], x["x_sample"][0]])
    qk = x["qk_norm_g"][0]
    lam = _np.zeros((P, 4), _np.float32)
    lam[:HD] = x["da_lambda"][0].T
    gains = _np.concatenate([
        columns(x["norm1_g"][0]), columns(x["norm2_g"][0]),
        _np.tile(_np.concatenate([qk[0], qk[0]])[:, None], (1, 8)),
        _np.tile(_np.concatenate([qk[1], qk[1]])[:, None], (1, 8)),
        columns(x["da_subln_g"][0]), columns(x["gla_norm_g"][0]), columns(x["gla_b_gate"][0]), lam], axis=1)
    arrays = {
        "xT": frames.T.reshape(KT, P, TOK).transpose(1, 0, 2).reshape(P, KT * TOK),
        "w_all": w_all,
        "gains": gains,
        "const": const_table(),
        "w_glr": glr.reshape(KT, P, RANK).transpose(1, 0, 2).reshape(P, KT * RANK),
        "w_gate": x["gla_w_gate2"][0],
        "ckT": x["cache_k"][0, 0].reshape(PAST, NH, P).transpose(2, 1, 0),
        "cv": x["cache_v"][0, 0].reshape(2, P, NH, P).transpose(1, 2, 0, 3).reshape(P, NH, PAST),
        "state_in": x["state_gla"][0, 0].transpose(1, 0, 2),
        "skT": x["peer_sub_keys"][0].reshape(2 * PH, N_KEYS, P).transpose(2, 0, 1).reshape(P, 2 * PH * N_KEYS),
        "u": x["peer_u"][0].reshape(N_KEYS, N_KEYS, KT, P).transpose(0, 3, 2, 1).reshape(N_KEYS, P, D),
        "v": x["peer_v"][0].reshape(N_KEYS, N_KEYS, D),
    }
    arrays = {k: _np.ascontiguousarray(v) for k, v in arrays.items()}

    nc = _bacc.Bacc("TRN2", target_bir_lowering=False, num_devices=1)
    A = {}
    for name, a in arrays.items():
        A[name] = nc.dram_tensor("in_" + name, a.shape, _mybir.dt.from_np(a.dtype), kind="ExternalInput").ap()
    for name in ("w_all", "u", "v"):
        A[name] = A[name].rearrange("t p n -> p t n")
    outs = {"kT_out": (D, TOK), "vT_out": (D, TOK), "yT_out": (D, TOK), "s_out": (2 * GH, P, 256)}
    for name, shape in outs.items():
        ap = nc.dram_tensor("out_" + name, shape, _mybir.dt.float32, kind="ExternalOutput").ap()
        A[name] = (ap.rearrange("h p n -> p h n") if name == "s_out"
                            else ap.rearrange("(k p) n -> p k n", p=P))
    A["gate"] = nc.dram_tensor("gate_by_expert", (N_KEYS, TOK // CHUNK_TOK, N_KEYS, CHUNK_TOK), _mybir.dt.float32,
                               kind="Internal").ap()
    z = nc.dram_tensor("branch_gates", (2 * KT, P, TOK), _mybir.dt.float32, kind="Internal").ap()
    A["z"] = z.rearrange("t p n -> p t n")
    h = nc.dram_tensor("early_gelu", (EARLY, N_KEYS, TOK), _mybir.dt.float32, kind="Internal").ap()
    A["h"] = h.rearrange("i j t -> j i t")
    build(nc, A)
    r = _run(nc, [{"in_" + k: v for k, v in arrays.items()}], core_ids=[0]).results[0]

    def by_frame(name, *shape):
        rows = _np.asarray(r["out_" + name]).T
        return rows[:SEQ].reshape(*shape[0]), rows[SEQ:].reshape(*shape[1])

    y_p, y_s = by_frame("yT_out", (1, SEQ, D), (1, DEC, D))
    k_p, k_s = by_frame("kT_out", (1, 1, SEQ, NH, 2, HD), (1, 1, DEC, NH, 2, HD))
    v_p, v_s = by_frame("vT_out", (1, 1, SEQ, NH, P), (1, 1, DEC, NH, P))
    s = _np.asarray(r["out_s_out"]).reshape(2, 1, 1, GH, P, 256)
    return y_p, y_s, k_p, v_p, s[0], k_s, v_s, s[1]
```
